# Optimizing a Trainium2 kernel written in Bass

```python
import jax
import jax.numpy as jnp
from jax import lax
import numpy as np

D_MODEL = 1024
BATCH = 1
SEQ = 512
DEPTH = 2

N_MIXERS = 2
EPS = 1e-6
NEG = -1e30
BIG = 1e9
ROPE_THETA = 500000.0

NSA_HEADS = 16
NSA_KV_GROUPS = 2
NSA_HEADS_PER_GROUP = NSA_HEADS // NSA_KV_GROUPS
HEAD_DIM = D_MODEL // NSA_HEADS
ROT_DIM = HEAD_DIM // 4
CMP_BLOCK = 32
CMP_STRIDE = 16
CMP_HIDDEN = 256
SEL_BLOCK = 64
SEL_TOPN = 8
WINDOW = 512
NSA_Q_BLOCK = 64
NSA_BRANCHES = 3
NSA_Q_COLS = NSA_HEADS * HEAD_DIM
NSA_KV_COLS = NSA_KV_GROUPS * HEAD_DIM
NSA_GATE_COLS = NSA_BRANCHES * NSA_HEADS
NSA_IN_COLS = NSA_Q_COLS + 2 * NSA_BRANCHES * NSA_KV_COLS + NSA_GATE_COLS

MLSTM_HEADS = 4
MLSTM_V_DIM = D_MODEL // MLSTM_HEADS
MLSTM_QK_DIM = MLSTM_V_DIM // 2
MLSTM_CHUNK = 64
GATE_SOFTCAP = 15.0
MLSTM_IN_COLS = 2 * MLSTM_HEADS * MLSTM_QK_DIM + 2 * MLSTM_HEADS * MLSTM_V_DIM + 2 * MLSTM_HEADS

N_EXPERTS = 32
N_GROUPS = 4
EXPERTS_PER_GROUP = N_EXPERTS // N_GROUPS
TOP_K = 2
D_EXPERT = 512
MOE_BLOCK = 128

kernel_name = 'hybrid_nsa_mlstm_grouped_moe_adaln'

def rms_norm(x, gain):
    xf = x.astype(jnp.float32)
    y = xf * lax.rsqrt(jnp.mean(xf * xf, axis=-1, keepdims=True) + EPS)
    return (y * gain.astype(jnp.float32)).astype(x.dtype)

def softcap(a):
    return GATE_SOFTCAP * jnp.tanh(a / GATE_SOFTCAP)

def partial_rope(x, pos):
    half = ROT_DIM // 2
    inv_freq = ROPE_THETA ** (-jnp.arange(half, dtype=jnp.float32) / half)
    ang = pos.astype(jnp.float32)[:, None] * inv_freq[None, :]
    cos = jnp.cos(ang)[:, None, :]
    sin = jnp.sin(ang)[:, None, :]
    xr = x[..., :ROT_DIM].astype(jnp.float32)
    x1, x2 = xr[..., :half], xr[..., half:]
    rot = jnp.concatenate([x1 * cos - x2 * sin, x2 * cos + x1 * sin], axis=-1).astype(x.dtype)
    return jnp.concatenate([rot, x[..., ROT_DIM:]], axis=-1)

def split_cols(a, sizes):
    return jnp.split(a, np.cumsum(sizes)[:-1].tolist(), axis=-1)

def to_group_major(a):
    return jnp.transpose(a, (0, 2, 1, 3))

def nsa_compress(a, pe, w1, b1, w2, b2):
    B, S, G, dh = a.shape
    nc = (S - CMP_BLOCK) // CMP_STRIDE + 1
    idx = np.arange(nc)[:, None] * CMP_STRIDE + np.arange(CMP_BLOCK)[None, :]
    blocks = a[:, idx] + pe[None, None, :, None, :]
    blocks = blocks.transpose(0, 1, 3, 2, 4).reshape(B, nc, G, CMP_BLOCK * dh)
    return jax.nn.gelu(blocks @ w1 + b1) @ w2 + b2

def nsa_mixer(h, w_in, w_out, q_gain, k_gain, cmp_pe, cmp_w1, cmp_b1, cmp_w2, cmp_b2):
    B, S, _ = h.shape
    G, R, dh, QB = NSA_KV_GROUPS, NSA_HEADS_PER_GROUP, HEAD_DIM, NSA_Q_BLOCK
    f32 = jnp.float32
    pos = jnp.arange(S, dtype=jnp.int32)
    q, kc, vc, ks, vs, kw, vw, gates = split_cols(h @ w_in, [NSA_Q_COLS] + [NSA_KV_COLS] * 6 + [NSA_GATE_COLS])
    q = partial_rope(rms_norm(q.reshape(B, S, NSA_HEADS, dh), q_gain), pos)
    ks = partial_rope(rms_norm(ks.reshape(B, S, G, dh), k_gain[1]), pos)
    kw = partial_rope(rms_norm(kw.reshape(B, S, G, dh), k_gain[2]), pos)
    kc = nsa_compress(kc.reshape(B, S, G, dh), cmp_pe[0], cmp_w1[0], cmp_b1[0], cmp_w2[0], cmp_b2[0])
    vc = nsa_compress(vc.reshape(B, S, G, dh), cmp_pe[1], cmp_w1[1], cmp_b1[1], cmp_w2[1], cmp_b2[1])
    nc = kc.shape[1]
    cmp_pos = jnp.arange(nc, dtype=jnp.int32) * CMP_STRIDE + (CMP_BLOCK - 1)
    kc = to_group_major(partial_rope(rms_norm(kc, k_gain[0]), cmp_pos))
    vc = to_group_major(vc)
    ns = S // SEL_BLOCK
    ks_blk = to_group_major(ks).reshape(B, G, ns, SEL_BLOCK, dh)
    vs_blk = to_group_major(vs.reshape(B, S, G, dh)).reshape(B, G, ns, SEL_BLOCK, dh)
    pad = ((0, 0), (0, 0), (WINDOW, 0), (0, 0))
    kw_pad = jnp.pad(to_group_major(kw), pad)
    vw_pad = jnp.pad(to_group_major(vw.reshape(B, S, G, dh)), pad)
    r, u = SEL_BLOCK // CMP_STRIDE, CMP_BLOCK // CMP_STRIDE
    c_idx = (r * np.arange(ns)[:, None, None] + np.arange(r)[None, :, None] + np.arange(u)[None, None, :]).reshape(ns, -1)
    cmp_to_sel = jnp.asarray((c_idx[:, :, None] == np.arange(nc)[None, None, :]).sum(1).T.astype(np.float32))
    n_top = min(SEL_TOPN, ns)
    scale = HEAD_DIM ** -0.5
    blk = jnp.arange(ns, dtype=jnp.int32)
    bi = jnp.arange(B)[:, None, None, None]
    gi = jnp.arange(G)[None, :, None, None]

    def attend_block(args):
        qb, gb, s0 = args
        t = s0 + jnp.arange(QB, dtype=jnp.int32)
        sc = jnp.einsum('bgrqd,bgcd->bgrqc', qb, kc).astype(f32) * scale
        valid_c = cmp_pos[None, :] <= t[:, None]
        p_c = jnp.where(valid_c, jax.nn.softmax(jnp.where(valid_c, sc, NEG), axis=-1), 0.0)
        o_c = jnp.einsum('bgrqc,bgcd->bgrqd', p_c.astype(vc.dtype), vc)
        imp = jnp.einsum('bgrqc,cj->bgqj', p_c, cmp_to_sel)
        cur = t // SEL_BLOCK
        forced = (blk[None, :] == 0) | (blk[None, :] == cur[:, None]) | (blk[None, :] == cur[:, None] - 1)
        allowed = blk[None, :] <= cur[:, None]
        imp = jnp.where(allowed, jnp.where(forced, BIG, imp), -BIG)
        _, sel = lax.top_k(imp, n_top)
        k_g = ks_blk[bi, gi, sel].reshape(B, G, QB, n_top * SEL_BLOCK, dh)
        v_g = vs_blk[bi, gi, sel].reshape(B, G, QB, n_top * SEL_BLOCK, dh)
        kpos = (sel[..., None] * SEL_BLOCK + jnp.arange(SEL_BLOCK, dtype=jnp.int32)).reshape(B, G, QB, n_top * SEL_BLOCK)
        valid_s = kpos[:, :, None] <= t[:, None]
        ss = jnp.einsum('bgrqd,bgqkd->bgrqk', qb, k_g).astype(f32) * scale
        p_s = jax.nn.softmax(jnp.where(valid_s, ss, NEG), axis=-1)
        o_s = jnp.einsum('bgrqk,bgqkd->bgrqd', p_s.astype(v_g.dtype), v_g)
        kwb = lax.dynamic_slice_in_dim(kw_pad, s0, WINDOW + QB, axis=2)
        vwb = lax.dynamic_slice_in_dim(vw_pad, s0, WINDOW + QB, axis=2)
        wpos = s0 - WINDOW + jnp.arange(WINDOW + QB, dtype=jnp.int32)
        valid_w = (wpos[None, :] <= t[:, None]) & (wpos[None, :] > t[:, None] - WINDOW) & (wpos[None, :] >= 0)
        sw = jnp.einsum('bgrqd,bgkd->bgrqk', qb, kwb).astype(f32) * scale
        p_w = jax.nn.softmax(jnp.where(valid_w, sw, NEG), axis=-1)
        o_w = jnp.einsum('bgrqk,bgkd->bgrqd', p_w.astype(vwb.dtype), vwb)
        return gb[:, 0][..., None] * o_c + gb[:, 1][..., None] * o_s + gb[:, 2][..., None] * o_w

    nq = S // QB
    q_blocks = q.reshape(B, nq, QB, G, R, dh).transpose(1, 0, 3, 4, 2, 5)
    g_blocks = jax.nn.sigmoid(gates).reshape(B, nq, QB, NSA_BRANCHES, G, R).transpose(1, 0, 3, 4, 5, 2)
    starts = jnp.arange(nq, dtype=jnp.int32) * QB
    o = lax.map(attend_block, (q_blocks, g_blocks, starts))
    o = o.transpose(1, 0, 4, 2, 3, 5).reshape(B, S, NSA_Q_COLS)
    return o @ w_out

def mlstm_mixer(h, w_in, w_out, b_igate, b_fgate, norm_gain):
    B, S, _ = h.shape
    NH, dqk, dv, L = MLSTM_HEADS, MLSTM_QK_DIM, MLSTM_V_DIM, MLSTM_CHUNK
    f32 = jnp.float32
    q, k, v, o, ig, fg = split_cols(h @ w_in, [NH * dqk, NH * dqk, NH * dv, NH * dv, NH, NH])

    def to_heads(a, d):
        return a.reshape(B, S, NH, d).transpose(0, 2, 1, 3).astype(f32)

    q = to_heads(q, dqk)
    k = to_heads(k, dqk) * (dqk ** -0.5)
    v = to_heads(v, dv)
    li = softcap(ig.astype(f32) + b_igate.astype(f32)).transpose(0, 2, 1)
    lf = jax.nn.log_sigmoid(softcap(fg.astype(f32) + b_fgate.astype(f32))).transpose(0, 2, 1)
    nch = S // L

    def to_chunks(a):
        return jnp.moveaxis(a.reshape(B, NH, nch, L, *a.shape[3:]), 2, 0)

    causal = np.tril(np.ones((L, L), dtype=bool))

    def step(carry, xs):
        C, n, m = carry
        qc, kc, vc, lic, lfc = xs
        b = jnp.cumsum(lfc, axis=-1)
        D = jnp.where(causal, b[..., :, None] - b[..., None, :] + lic[..., None, :], NEG)
        m_inter = b + m[..., None]
        m_t = jnp.maximum(m_inter, D.max(-1))
        A = jnp.exp(D - m_t[..., None]) * jnp.einsum('bhqd,bhkd->bhqk', qc, kc)
        inter = jnp.exp(m_inter - m_t)
        num = jnp.einsum('bhqk,bhkv->bhqv', A, vc) + inter[..., None] * jnp.einsum('bhqd,bhdv->bhqv', qc, C)
        den = A.sum(-1) + inter * jnp.einsum('bhqd,bhd->bhq', qc, n)
        h_out = num / jnp.maximum(jnp.abs(den), jnp.exp(-m_t))[..., None]
        m_new = m_t[..., -1]
        w = jnp.exp(b[..., -1:] - b + lic - m_new[..., None])
        decay = jnp.exp(m_inter[..., -1] - m_new)
        C_new = decay[..., None, None] * C + jnp.einsum('bhs,bhsd,bhsv->bhdv', w, kc, vc)
        n_new = decay[..., None] * n + jnp.einsum('bhs,bhsd->bhd', w, kc)
        return (C_new, n_new, m_new), h_out

    init = (jnp.zeros((B, NH, dqk, dv), f32), jnp.zeros((B, NH, dqk), f32), jnp.zeros((B, NH), f32))
    _, hs = lax.scan(step, init, (to_chunks(q), to_chunks(k), to_chunks(v), to_chunks(li), to_chunks(lf)))
    hs = jnp.moveaxis(hs, 0, 2).reshape(B, NH, S, dv).transpose(0, 2, 1, 3)
    hs = rms_norm(hs, norm_gain).reshape(B, S, NH * dv).astype(h.dtype)
    return (jax.nn.sigmoid(o) * hs) @ w_out

def moe_ffn(h, router_w, router_b, w_gate, w_up, w_down):
    B, S, D = h.shape
    T = B * S
    f32 = jnp.float32
    xf = h.reshape(T, D)
    affinity = jax.nn.sigmoid(xf.astype(f32) @ router_w.astype(f32))
    choice = (affinity + router_b.astype(f32)).reshape(T, N_GROUPS, EXPERTS_PER_GROUP)
    group_score = lax.top_k(choice, TOP_K)[0].sum(-1)
    group = jnp.argmax(group_score, axis=-1).astype(jnp.int32)
    in_group = jnp.take_along_axis(choice, group[:, None, None], axis=1)[:, 0]
    _, local = lax.top_k(in_group, TOP_K)
    expert = group[:, None] * EXPERTS_PER_GROUP + local
    aff = jnp.take_along_axis(affinity, expert, axis=1)
    weight = (aff / aff.sum(-1, keepdims=True)).astype(h.dtype)
    A = T * TOP_K
    e_flat = expert.reshape(A)
    tok_flat = jnp.repeat(jnp.arange(T, dtype=jnp.int32), TOP_K)
    w_flat = weight.reshape(A)
    order = jnp.argsort(e_flat)
    e_s, tok_s, w_s = e_flat[order], tok_flat[order], w_flat[order]
    counts = jax.ops.segment_sum(jnp.ones((A,), jnp.int32), e_flat, num_segments=N_EXPERTS)
    starts = jnp.cumsum(counts) - counts
    padded = (counts + MOE_BLOCK - 1) // MOE_BLOCK * MOE_BLOCK
    p_ends = jnp.cumsum(padded)
    p_starts = p_ends - padded
    dest = p_starts[e_s] + (jnp.arange(A, dtype=jnp.int32) - starts[e_s])
    nb = -(-A // MOE_BLOCK) + N_EXPERTS
    P = nb * MOE_BLOCK
    buf_tok = jnp.full((P,), T, jnp.int32).at[dest].set(tok_s)
    buf_w = jnp.zeros((P,), h.dtype).at[dest].set(w_s)
    block_start = jnp.arange(nb, dtype=jnp.int32) * MOE_BLOCK
    block_expert = jnp.minimum(jnp.searchsorted(p_ends, block_start, side='right'), N_EXPERTS - 1).astype(jnp.int32)
    x_pad = jnp.concatenate([xf, jnp.zeros((1, D), h.dtype)], axis=0)

    def expert_block(args):
        e, toks, ws = args
        xb = x_pad[toks]
        hid = jax.nn.silu(xb @ w_gate[e]) * (xb @ w_up[e])
        return (hid @ w_down[e]) * ws[:, None]

    out = lax.map(expert_block, (block_expert, buf_tok.reshape(nb, MOE_BLOCK), buf_w.reshape(nb, MOE_BLOCK)))
    y = jnp.zeros((T + 1, D), h.dtype).at[buf_tok].add(out.reshape(P, D))
    return y[:T].reshape(B, S, D)

def setup_inputs(seed: int = 0) -> dict:
    key = jax.random.key(seed)
    ks = jax.random.split(key, 32)
    D = D_MODEL
    n_nsa = (DEPTH + 1) // 2
    n_ml = DEPTH // 2

    def nrm(k, shape, s):
        return jax.random.normal(k, shape, jnp.float32) * s

    return {
        'x': nrm(ks[0], (BATCH, SEQ, D), 1.0),
        'c': nrm(ks[1], (BATCH, D), 1.0),
        'ada_w': nrm(ks[2], (DEPTH, D, 6 * D), 0.5 * D ** -0.5),
        'ada_b': nrm(ks[3], (DEPTH, 6 * D), 0.02),
        'norm_mix_gain': 1.0 + nrm(ks[4], (DEPTH, D), 0.05),
        'norm_ffn_gain': 1.0 + nrm(ks[5], (DEPTH, D), 0.05),
        'nsa_w_in': nrm(ks[6], (n_nsa, D, NSA_IN_COLS), D ** -0.5),
        'nsa_w_out': nrm(ks[7], (n_nsa, NSA_Q_COLS, D), NSA_Q_COLS ** -0.5),
        'nsa_q_gain': 1.0 + nrm(ks[8], (n_nsa, HEAD_DIM), 0.05),
        'nsa_k_gain': 1.0 + nrm(ks[9], (n_nsa, NSA_BRANCHES, HEAD_DIM), 0.05),
        'nsa_cmp_pe': nrm(ks[10], (n_nsa, 2, CMP_BLOCK, HEAD_DIM), 0.1),
        'nsa_cmp_w1': nrm(ks[11], (n_nsa, 2, CMP_BLOCK * HEAD_DIM, CMP_HIDDEN), (CMP_BLOCK * HEAD_DIM) ** -0.5),
        'nsa_cmp_b1': nrm(ks[12], (n_nsa, 2, CMP_HIDDEN), 0.02),
        'nsa_cmp_w2': nrm(ks[13], (n_nsa, 2, CMP_HIDDEN, HEAD_DIM), CMP_HIDDEN ** -0.5),
        'nsa_cmp_b2': nrm(ks[14], (n_nsa, 2, HEAD_DIM), 0.02),
        'mlstm_w_in': nrm(ks[15], (n_ml, D, MLSTM_IN_COLS), D ** -0.5),
        'mlstm_b_igate': nrm(ks[16], (n_ml, MLSTM_HEADS), 0.1),
        'mlstm_b_fgate': 3.0 + nrm(ks[17], (n_ml, MLSTM_HEADS), 0.5),
        'mlstm_norm_gain': 1.0 + nrm(ks[18], (n_ml, MLSTM_HEADS, MLSTM_V_DIM), 0.05),
        'mlstm_w_out': nrm(ks[19], (n_ml, MLSTM_HEADS * MLSTM_V_DIM, D), (MLSTM_HEADS * MLSTM_V_DIM) ** -0.5),
        'router_w': nrm(ks[20], (D, N_EXPERTS), D ** -0.5),
        'router_b': nrm(ks[21], (N_EXPERTS,), 0.01),
        'moe_w_gate': nrm(ks[22], (DEPTH, N_EXPERTS, D, D_EXPERT), D ** -0.5),
        'moe_w_up': nrm(ks[23], (DEPTH, N_EXPERTS, D, D_EXPERT), D ** -0.5),
        'moe_w_down': nrm(ks[24], (DEPTH, N_EXPERTS, D_EXPERT, D), D_EXPERT ** -0.5),
    }

def reference(x, c, ada_w, ada_b, norm_mix_gain, norm_ffn_gain,
              nsa_w_in, nsa_w_out, nsa_q_gain, nsa_k_gain, nsa_cmp_pe, nsa_cmp_w1, nsa_cmp_b1, nsa_cmp_w2, nsa_cmp_b2,
              mlstm_w_in, mlstm_b_igate, mlstm_b_fgate, mlstm_norm_gain, mlstm_w_out,
              router_w, router_b, moe_w_gate, moe_w_up, moe_w_down):
    cond = jax.nn.silu(c)
    for i in range(DEPTH):
        mod = cond @ ada_w[i] + ada_b[i]
        sh_m, sc_m, g_m, sh_f, sc_f, g_f = jnp.split(mod[:, None, :], 6, axis=-1)
        hm = rms_norm(x, norm_mix_gain[i]) * (1.0 + sc_m) + sh_m
        j = i // N_MIXERS
        if i % N_MIXERS == 0:
            y = nsa_mixer(hm, nsa_w_in[j], nsa_w_out[j], nsa_q_gain[j], nsa_k_gain[j], nsa_cmp_pe[j],
                          nsa_cmp_w1[j], nsa_cmp_b1[j], nsa_cmp_w2[j], nsa_cmp_b2[j])
        else:
            y = mlstm_mixer(hm, mlstm_w_in[j], mlstm_w_out[j], mlstm_b_igate[j], mlstm_b_fgate[j], mlstm_norm_gain[j])
        x = x + g_m * y
        hf = rms_norm(x, norm_ffn_gain[i]) * (1.0 + sc_f) + sh_f
        x = x + g_f * moe_ffn(hf, router_w, router_b, moe_w_gate[i], moe_w_up[i], moe_w_down[i])
    return x


_drawn_inputs = setup_inputs


def setup_inputs(seed=0):
    import zlib

    import numpy as np

    out = dict(_drawn_inputs(seed))
    spreads = {}
    factors = {'nsa_q_gain': 3.897,
     'nsa_k_gain': 4.57,
     'nsa_cmp_b1': 8.0,
     'nsa_cmp_b2': 2.906,
     'mlstm_b_igate': 64.0,
     'mlstm_norm_gain': 2.914}
    for name, (base, spread) in spreads.items():
        noise = np.random.default_rng([zlib.crc32(name.encode()), seed]).standard_normal(out[name].shape)
        drawn = base * np.exp(spread * noise) if base else spread * noise
        out[name] = jnp.asarray(drawn.astype(out[name].dtype))
    for name, factor in factors.items():
        out[name] = (out[name] * factor).astype(out[name].dtype)
    return out
```

```python
from contextlib import ExitStack

import concourse.bass as bass
from concourse import mybir

F32 = mybir.dt.float32
I32 = mybir.dt.int32
ALU = mybir.AluOpType
ACT = mybir.ActivationFunctionType
AX = mybir.AxisListType.X

P = 128
SEQ, D = 512, 1024
NT, KD = SEQ // P, D // P
LAYERS = 2
EPS = 1e-6
NEG = -1e30

HEADS, GROUPS, DH = 16, 2, 64
PAIRS = HEADS // 2
ROT = DH // 4
HALF = ROT // 2
CMP_BLOCK, CMP_STRIDE, CMP_HIDDEN = 32, 16, 256
NCMP = (SEQ - CMP_BLOCK) // CMP_STRIDE + 1
NC = 32
CMP_CHUNKS = CMP_BLOCK * DH // P
SEL_BLOCK, SEL_TOPN, WINDOW = 64, 8, 512
assert SEQ // SEL_BLOCK <= SEL_TOPN and WINDOW >= SEQ and NCMP < NC
NSA_COLS = HEADS * DH + 6 * GROUPS * DH + 3 * HEADS
SCALE = DH ** -0.5

MH, DQK, DV = 4, 128, 256
SOFTCAP = 15.0
ML_COLS = 2 * MH * DQK + 2 * MH * DV + 2 * MH

EXPERTS, EGROUPS, EPG, DE = 32, 4, 8, 512
SLOTS = 128
OVERFLOW = 7
NB = EXPERTS + OVERFLOW + 1
NOBODY = SEQ

ADA_COLS = 6 * D
ADA_BLOCKS, ADA_W = 16, 384
assert ADA_BLOCKS * ADA_W == ADA_COLS
SH_M, SC_M, G_M, SH_F, SC_F, G_F = (D * i for i in range(6))

GRANT = 1

C_ID, C_TRI, C_CAUSAL, C_CAUSAL_T, C_CMASK = 0, 128, 256, 384, 512
C_ROPE = 640
C_CROPE = C_ROPE + NT * ROT
C_ROWOK = C_CROPE + ROT
C_IOTA_E = C_ROWOK + NT
C_IOTA_8 = C_IOTA_E + EXPERTS
C_IOTA_4 = C_IOTA_8 + EXPERTS
C_TOKEN = C_IOTA_4 + EGROUPS
C_IOTA_OV = C_TOKEN + NT
C_ZERO = C_IOTA_OV + 8
C_COLS = C_ZERO + EXPERTS

AREA = 24576
SLOT = AREA // 2
UP, DOWN = KD * DE, 2 * KD * DE
A_PROB, A_PROBT = 8192, 8192 + 2048
A_KTZ = KD * NSA_COLS
A_KC = A_KTZ + 8 * SEQ
KC_ROW = 530
A_V = A_KC + 4 * KC_ROW
A_VCBD = A_V + NT * 2 * P
A_KCTZ = A_VCBD + 2 * 256
A_HGAIN = A_KCTZ + P
A_PE = A_HGAIN + 4 * DH
A_B1 = A_PE + 2 * CMP_CHUNKS
A_B2 = A_B1 + 2 * CMP_HIDDEN
A_W2 = A_B2 + 2 * DH
A_SMALL = A_W2 + 4 * DH
A_CBLK = A_SMALL + 500
assert A_KC >= SLOT and A_CBLK <= AREA

HIDDEN, HIDDEN_T, CMP_OUT, KEY_T = 2, 3, 4, 5
CMP_VALUES, KEY_STD = 4, 5
KEY_VAR, KEY_ROW, KEY_COLUMNS = 3, 4, 5

M_QK, M_V, M_O = 0, 8192, 16384
VROW = DV + 1
M_VALS = 0
M_RAW = M_VALS + NT * MH * VROW
M_ROWS = M_V
M_GAIN = M_ROWS + 7 * SEQ
M_DIAG = M_GAIN + D
M_W = M_DIAG + SEQ
M_AT = M_W + 2 * SEQ
M_SQ = M_AT + 2 * SEQ
assert M_RAW + 2 * NT * VROW <= M_V and M_SQ + NT * DV <= M_O

LF, CUM_B, U_IN, U_MAX, EXP_M, ZERO = range(6)

R_W, R_B = 0, KD * EXPERTS
R_AFF, R_CH, R_EQ, R_MSK, R_E1, R_E2, R_SUM, R_BLK, R_SLOT, R_F, R_TMP = (288 + 128 * i for i in range(11))
R_S = 288 + 128 * 11


def build_trunk(nc, x, c, ada_w, ada_b, norm_mix_gain, norm_ffn_gain,
                nsa_w_in, nsa_w_out, nsa_q_gain, nsa_k_gain, nsa_cmp_pe, nsa_cmp_w1, nsa_cmp_b1, nsa_cmp_w2, nsa_cmp_b2,
                mlstm_w_in, mlstm_b_igate, mlstm_b_fgate, mlstm_norm_gain, mlstm_w_out,
                router_w, router_b, moe_w_gate, moe_w_up, moe_w_down, consts, empty_slots, out):
    x_d = x.rearrange("b (t p) d -> p (b t) d", p=P)
    out_d = out.rearrange("b (t p) d -> p (b t) d", p=P)
    gate_rows = moe_w_gate.rearrange("l e (k p) f -> p (l e) k f", p=P)
    up_rows = moe_w_up.rearrange("l e (k p) f -> p (l e) k f", p=P)
    down_rows = moe_w_down.rearrange("l e (k p) n -> p (l e) k n", p=P)
    ada_rows = ada_w.rearrange("l (p k) n -> l p k n", k=KD)
    mlstm_rows = mlstm_w_in[0].rearrange("(k p) n -> p k n", p=P)

    with ExitStack() as ctx:
        def sb(name, shape, dt=F32):
            return ctx.enter_context(nc.sbuf_tensor(name, shape, dt))

        hf_dram = [nc.dram_tensor(f"hf_{l}", (SEQ, D), F32).ap() for l in range(LAYERS)]
        z_dram = [nc.dram_tensor(f"z_{l}", (NB * SLOTS, D), F32).ap() for l in range(LAYERS)]
        slot_dram = [nc.dram_tensor(f"slot_{l}", (SLOTS * NB, 1), I32).ap() for l in range(LAYERS)]

        xs = sb("xs", [P, NT, D])
        hn = sb("hn", [P, NT * D])
        hT = sb("hT", [P, KD * SEQ])
        area = sb("area", [P, AREA])
        mods = sb("mods", [P, ADA_COLS])
        ada_buf = sb("ada_buf", [P, KD, ADA_W])
        ada_acc = sb("ada_acc", [P, 2, ADA_W])
        ada_bias = sb("ada_bias", [P, 2, ADA_W])
        arena = sb("arena", [P, 4096])
        cs = sb("cs", [P, C_COLS])
        ones = sb("ones", [P, P])
        cond = sb("cond", [P, 2 * KD])
        small = sb("small", [P, 104])
        gates = sb("gates", [P, NT * 3 * HEADS])
        slot_tok = sb("slot_tok", [P, NB], I32)
        slot_cur = sb("slot_cur", [P, 2], I32)
        route = sb("route", [P, 8 + 5 * NT], I32)

        ps = ctx.enter_context(nc.psum_tensor("ps", [P, 8, 512], F32))

        sems = {}

        def sem(name):
            if name not in sems:
                sems[name] = ctx.enter_context(nc.semaphore(name))
            return sems[name]

        ident = cs[:, C_ID:C_ID + P]
        hnt = hn[:, :].rearrange("p (t d) -> p t d", t=NT)
        hTk = hT[:, :].rearrange("p (k s) -> p k s", k=KD)
        gain_tile = hT[:, 0:D]
        ssq, rstd, var = small[:, 0:4], small[:, 4:8], small[:, 8:12]

        w_in0 = area[:, 0:A_KTZ].rearrange("p (k n) -> p k n", k=KD)
        w1 = area[:, 0:2 * CMP_CHUNKS * CMP_HIDDEN].rearrange("p (a m n) -> p a m n", a=2, m=CMP_CHUNKS)
        w_out = [area[:, lo:lo + KD * D].rearrange("p (k n) -> p k n", k=KD) for lo in (0, M_O)]
        prob = area[:, A_PROB:A_PROB + 2048].rearrange("p (u b s) -> p u b s", u=2, b=2)
        probT = area[:, A_PROBT:A_PROBT + 2048].rearrange("p (u b s) -> p u b s", u=2, b=2)
        ktz = area[:, A_KTZ:A_KC].rearrange("p (b g r s) -> p b g r s", b=2, g=2, r=2)
        kcvT = area[:, A_KC:A_V].rearrange("p (a g s) -> p a g s", a=2, g=2)
        vals = area[:, A_V:A_VCBD].rearrange("p (t b n) -> p t b n", t=NT, b=2)
        vcbd = area[:, A_VCBD:A_KCTZ].rearrange("p (g n) -> p g n", g=2)
        kctz = area[:, A_KCTZ:A_HGAIN].rearrange("p (r n) -> p r n", r=2)
        hgain = area[:, A_HGAIN:A_PE]
        pe_t = area[:, A_PE:A_B1].rearrange("p (a m) -> p a m", a=2)
        b1_row, b2_row = area[0:1, A_B1:A_B2], area[0:1, A_B2:A_W2]
        w2 = area[:, A_W2:A_SMALL].rearrange("p (a m n) -> p a m n", a=2, m=2)
        qT = arena[:, :].rearrange("p (r s) -> p r s", r=PAIRS)
        nrm = [hn[:, 2048 * u:2048 * u + 20 * DH] for u in range(2)]
        kcv = [hn[:, 2048 * u + 1280:2048 * u + 1536] for u in range(2)]
        rope_tmp = [area[:, A_SMALL + 160 * i:A_SMALL + 160 * i + 160] for i in range(3)]
        head_ss = small[:, 12:24]
        blk = hn[:, 0:2048].rearrange("p (a m c) -> p a m c", a=2, m=CMP_CHUNKS)
        hid_c = hn[0:64, 2048:2560].rearrange("p (a n) -> p a n", a=2)
        hidT_c = hn[:, 2560:2816].rearrange("p (q c) -> p q c", q=4)
        kcn, ksq = hn[0:64, 2816:2944], hn[0:64, 2944:3008]
        pc = hn[:, 0:2048].rearrange("p (t n) -> p t n", t=NT)
        pcT = hn[:, 2048:4096].rearrange("p (t q n) -> p t q n", t=NT, q=4)

        def head_rstd(u):
            return small[:, 24 + 20 * u:44 + 20 * u]

        def neg_max(u):
            return small[:, 64 + 2 * u:66 + 2 * u]

        def raw_max(u):
            return small[:, 68 + 2 * u:70 + 2 * u]

        def sum_l(u):
            return small[:, 72 + 2 * u:74 + 2 * u]

        def inv_l(u):
            return small[:, 76 + 2 * u:78 + 2 * u]

        cmp_r = small[:, 80:96]

        def moe_w(k):
            return small[:, 96 + 4 * k:100 + 4 * k]

        ml_vals = area[:, M_VALS:M_RAW].rearrange("p (t h d) -> p t h d", t=NT, h=MH)
        ml_sel = area[0:MH, M_ROWS + 6 * SEQ:M_ROWS + 7 * SEQ].rearrange("p (h s) -> p h s", h=MH)
        ml_diag = area[:, M_DIAG:M_DIAG + SEQ]
        ml_sq = area[:, M_SQ:M_SQ + NT * DV]
        ml_li = gates[:, 104:136].rearrange("p (t g) -> p t g", t=NT)
        ml_cols = gates[:, 136:168].rearrange("p (a n) -> p a n", a=2)

        def ml_row(i):
            return area[:, M_ROWS + i * SEQ:M_ROWS + (i + 1) * SEQ]

        def ml_raw(u):
            return area[:, M_RAW + u * NT * VROW:M_RAW + (u + 1) * NT * VROW].rearrange("p (t d) -> p t d", t=NT)

        def ml_w(u):
            return area[:, M_W + u * SEQ:M_W + (u + 1) * SEQ]

        def ml_at(u):
            return area[:, M_AT + u * SEQ:M_AT + (u + 1) * SEQ]

        xb = [hn[:, D * u:D * u + D] for u in range(2)]
        zb = [hn[:, 2 * D + D * u:2 * D + D * u + D] for u in range(2)]
        z_in = [[hn[:, D * (2 * u + k):D * (2 * u + k) + D] for k in range(2)] for u in range(2)]
        xbT = hT[:, 0:D].rearrange("p (k s) -> p k s", k=KD)
        hid, sig, hidT = hT[:, 1024:1536], hT[:, 1536:2048], hT[:, 2048:2560].rearrange("p (k s) -> p k s", k=4)
        ffn_gate = hT[:, 3072:4096]

        def w_gu(u, m):
            return area[:, u * SLOT + m * UP:u * SLOT + m * UP + UP].rearrange("p (k n) -> p k n", k=KD)

        def w_dn(u):
            return area[:, u * SLOT + DOWN:u * SLOT + DOWN + UP].rearrange("p (k n) -> p k n", k=DE // P)

        block = ctx.enter_context(nc.Block())

        @block.sync
        def _(sp):
            def ada_load(layer, buf, b_expr, which, used):
                cols = bass.ds(b_expr * ADA_W, ADA_W)
                sp.wait_ge(sem(f"ada_read_{which}"), used + GRANT)
                u = 1 if which == "b" else 0
                sp.dma_start(buf, ada_rows[layer, :, :, cols]).then_inc(sem(f"ada_loaded_{which}"), 16)
                sp.dma_start(ada_bias[0:1, u, :], ada_b[layer:layer + 1, cols]).then_inc(sem(f"ada_loaded_{which}"), 16)

            def ada_pairs(first, n):
                with sp.Fori(first // 2, (first + n) // 2) as i:
                    ada_load(0, ada_buf[:, :, :], i * 2, "a", i)
                    ada_load(0, arena[:, 0:KD * ADA_W].rearrange("p (k n) -> p k n", k=KD), i * 2 + 1, "b", i)

            def expert_load(l, e_expr, u, before):
                row = bass.ds(e_expr + l * EXPERTS, 1)
                parts = [area[:, u * SLOT + lo:u * SLOT + lo + UP].rearrange("p (e k n) -> p e k n", e=1, k=k)
                         for lo, k in ((0, KD), (UP, KD), (DOWN, DE // P))]
                sp.wait_ge(sem(f"gu_{l}"), before * 2)
                sp.dma_start(parts[0], gate_rows[:, row, :, :]).then_inc(sem(f"wgu_{l}_{u}"), 16)
                sp.dma_start(parts[1], up_rows[:, row, :, :]).then_inc(sem(f"wgu_{l}_{u}"), 16)
                sp.wait_ge(sem(f"y_{l}"), before)
                sp.dma_start(parts[2], down_rows[:, row, :, :]).then_inc(sem(f"wd_{l}_{u}"), 16)

            def moe_loads(l):
                sp.wait_ge(sem("w_out_used"), NT * (l + 1))
                sp.dma_start(arena[:, R_W:R_B].rearrange("p (k e) -> p k e", k=KD),
                             router_w.rearrange("(k p) e -> p k e", p=P)).then_inc(sem("router_w"), 16)
                sp.dma_start(arena[:, R_B:R_B + EXPERTS],
                             router_b.rearrange("(o e) -> o e", o=1).to_broadcast([P, EXPERTS])).then_inc(sem("router_w"), 16)
                for t in range(NT):
                    sp.wait_ge(sem("hn_ready"), NT * (2 * l + 1) + t + 1)
                    sp.dma_start(hf_dram[l][t * P:(t + 1) * P, :], hnt[:, t, :]).then_inc(sem("hf_stored"), 16)
                expert_load(l, 0, 0, 0)
                expert_load(l, 1, 1, 0)
                if l == 0:
                    sp.wait_ge(sem("ffn_gate"), 1)
                with sp.Fori(1, EXPERTS // 2) as i:
                    if l == 0:
                        ada_load(1, ada_buf[:, :, :], i - 1, "next", i - 1)
                    for u in range(2):
                        expert_load(l, i * 2 + u, u, i * 2 + (u - 1))
                if l == 0:
                    ada_load(1, ada_buf[:, :, :], ADA_BLOCKS - 1, "next", ADA_BLOCKS - 1)
                sp.wait_ge(sem("route_ready"), l + 1)
                n_ov = sp.value_load(route[0:1, 0:1], min_val=0, max_val=OVERFLOW)
                with sp.If(n_ov > 0), sp.Fori(0, n_ov) as j:
                    e = sp.value_load(route[0:1, bass.ds(j + 1, 1)], min_val=0, max_val=EXPERTS - 1)
                    expert_load(l, e, 0, j + EXPERTS)
                sp.wait_ge(sem(f"y_{l}"), n_ov + EXPERTS)

            sp.dma_start(cond[:, 0:KD], c.rearrange("b (p k) -> p (b k)", k=KD)).then_inc(sem("c_loaded"), 16)
            sp.dma_start(cs[:, :], consts).then_inc(sem("consts"), 16)
            sp.wait_ge(sem("bias_zeroed"), 1)
            ada_pairs(0, 8)
            sp.dma_start(xs[:, :, :], x_d).then_inc(sem("x_ready_0"), 16)
            sp.dma_start(gain_tile, norm_mix_gain[0:1, :].to_broadcast([P, D])).then_inc(sem("norm_gain"), 16)
            w_rows = nsa_w_in[0].rearrange("(k p) n -> p k n", p=P)
            for h in range(2):
                sp.dma_start(w_in0[:, 4 * h:4 * h + 4, :], w_rows[:, 4 * h:4 * h + 4, :]).then_inc(sem("w_in_0"), 16)
            for g, src in enumerate((nsa_q_gain[0:1, :], nsa_k_gain[0, 1:2, :], nsa_k_gain[0, 2:3, :], nsa_k_gain[0, 0:1, :])):
                sp.dma_start(hgain[:, g * DH:g * DH + DH], src.to_broadcast([P, DH])).then_inc(sem("nsa_small"), 16)
            with nc.allow_non_contiguous_dma(reason="4096 position embeddings, once"):
                for a in range(2):
                    sp.dma_start(pe_t[:, a, :], nsa_cmp_pe[0, a].rearrange("(m r) d -> (r d) m", r=2))\
                      .then_inc(sem("nsa_small"), 16)
            sp.dma_start(b1_row, nsa_cmp_b1.rearrange("o a n -> o (a n)")).then_inc(sem("nsa_small"), 16)
            sp.dma_start(b2_row, nsa_cmp_b2.rearrange("o a n -> o (a n)")).then_inc(sem("nsa_small"), 16)
            for a in range(2):
                sp.dma_start(w2[:, a, :, :], nsa_cmp_w2[0, a].rearrange("(m p) n -> p m n", p=P)).then_inc(sem("nsa_small"), 16)
            ada_pairs(8, 8)
            for l in range(LAYERS):
                sp.dma_start(slot_dram[l], empty_slots).then_inc(sem("slots_empty"), 16)
            for l in range(LAYERS):
                for half in range(2):
                    lo = (EXPERTS * SLOTS) + half * SEQ
                    sp.dma_start(z_dram[l][lo:lo + SEQ, :], x.rearrange("b s d -> (b s) d")).then_inc(sem("z_filled"), 16)
            sp.wait_ge(sem("proj0_ready"), 4 * NT)
            for a in range(2):
                sp.dma_start(w1[:, a, :, :], nsa_cmp_w1[0, a].rearrange("(m p) n -> p m n", p=P)).then_inc(sem("w1"), 16)
            sp.wait_ge(sem("cmp_pe"), HIDDEN)
            sp.dma_start(w_out[0], nsa_w_out[0].rearrange("(k p) n -> p k n", p=P)).then_inc(sem("w_out_loaded"), 16)
            sp.wait_ge(sem("w_out_used"), NT)
            sp.dma_start(gain_tile, norm_ffn_gain[0:1, :].to_broadcast([P, D])).then_inc(sem("norm_gain"), 16)
            moe_loads(0)

            qk, vo = 2 * MH * DQK, MH * DV
            sp.dma_start(area[:, M_QK:M_V].rearrange("p (k n) -> p k n", k=KD), mlstm_rows[:, :, 0:qk]).then_inc(sem("w_qk"), 16)
            sp.dma_start(area[:, M_V:M_O].rearrange("p (k n) -> p k n", k=KD), mlstm_rows[:, :, qk:qk + vo]).then_inc(sem("w_v"), 16)
            sp.dma_start(area[:, M_O:AREA].rearrange("p (k n) -> p k n", k=KD), mlstm_rows[:, :, qk + vo:qk + 2 * vo])\
              .then_inc(sem("w_o"), 16)
            sp.dma_start(gates[:, 0:64].rearrange("p (k n) -> p k n", k=KD), mlstm_rows[:, :, qk + 2 * vo:]).then_inc(sem("w_gates"), 16)
            sp.dma_start(gates[:, 96:100], mlstm_b_igate.to_broadcast([P, MH])).then_inc(sem("w_gates"), 16)
            sp.dma_start(gates[:, 100:104], mlstm_b_fgate.to_broadcast([P, MH])).then_inc(sem("w_gates"), 16)
            sp.wait_ge(sem("x_ready_2"), NT)
            sp.dma_start(gain_tile, norm_mix_gain[1:2, :].to_broadcast([P, D])).then_inc(sem("norm_gain"), 16)
            sp.wait_ge(sem("proj1_ready"), 16)
            sp.dma_start(area[:, M_GAIN:M_GAIN + D],
                         mlstm_norm_gain.rearrange("o h d -> o (h d)").to_broadcast([P, D])).then_inc(sem("ml_gain"), 16)
            sp.wait_ge(sem("proj1_ready"), 24)
            sp.dma_start(w_out[1], mlstm_w_out[0].rearrange("(k p) n -> p k n", p=P)).then_inc(sem("w_out_loaded"), 16)
            sp.wait_ge(sem("w_out_used"), 2 * NT)
            sp.dma_start(gain_tile, norm_ffn_gain[1:2, :].to_broadcast([P, D])).then_inc(sem("norm_gain"), 16)
            moe_loads(1)

            for t in range(NT):
                sp.wait_ge(sem("x_ready_4"), t + 1)
                sp.dma_start(out_d[:, t, :], xs[:, t, :]).then_inc(sem("out_stored"), 16)
            sp.wait_ge(sem("out_stored"), 16 * NT)

        @block.gpsimd
        def _(pool):
            last_row = pool.to_reg(SEQ - 1)
            last_slot = pool.to_reg(SLOTS * NB - 1)
            last_z = pool.to_reg(SLOTS * NB - 1)
            pool.memset(ada_bias[:, :, :], 0.0).then_inc(sem("bias_zeroed"), 1)
            pool.memset(ones[:, :], 1.0).then_inc(sem("ones"), 1)
            pool.memset(area[:, A_KTZ:A_HGAIN], 0.0).then_inc(sem("nsa_zeroed"), 1)

            def settled():
                pool.sem_inc(sem("pool_settled"), 1)

            def norm_shift(n):
                shift = SH_F if n % 2 else SH_M
                for t in range(NT):
                    pool.wait_ge(sem("hn_scaled"), NT * n + t + 1)
                    pool.tensor_tensor(hnt[:, t, :], hnt[:, t, :], mods[:, shift:shift + D], ALU.add)\
                        .then_inc(sem("hn_ready"), 1)

            def gather(l, b_expr, u, transposed):
                src = slot_tok[:, bass.ds(b_expr, 1)]
                pool.wait_ge(sem(f"xb_used_{l}"), transposed)
                pool.tensor_copy(slot_cur[:, u:u + 1], src).then_inc(sem(f"slot_cur_{l}_{u}"), 1)

            def gather_go(l, u, nth, s=None):
                pool.wait_ge(sem(f"slot_cur_{l}_{u}"), nth)
                settled()
                pool.indirect_dma_start(xb[u], None, hf_dram[l], bass.IndirectOffsetOnAxis(ap=slot_cur[:, u:u + 1], axis=0),
                                        bounds_check=last_row, oob_is_err=False).then_inc(sem(s or f"xb_{l}_{u}"), 16)

            def moe_pool(l):
                pool.wait_ge(sem("slots_empty"), 16 * LAYERS)
                pool.wait_ge(sem("route_ready"), l + 1)
                for k in range(2):
                    for t in range(NT):
                        at = 8 + k * NT + t
                        pool.indirect_dma_start(slot_dram[l], bass.IndirectOffsetOnAxis(ap=route[:, at:at + 1], axis=0),
                                                route[:, 24 + t:25 + t], None, bounds_check=last_slot,
                                                oob_is_err=False).then_inc(sem("scattered"), 16)
                pool.wait_ge(sem("scattered"), 16 * 2 * NT * (l + 1))
                pool.dma_start(slot_tok[:, :], slot_dram[l].rearrange("(s b) o -> s (b o)", b=NB)).then_inc(sem("slot_tok_loaded"), 16)
                pool.wait_ge(sem("slot_tok_loaded"), 16 * (l + 1))
                pool.wait_ge(sem("hf_stored"), 16 * NT * (l + 1))
                for u in range(2):
                    gather(l, u, u, 0)
                    gather_go(l, u, 1)
                with pool.Fori(1, EXPERTS // 2) as i:
                    for u in range(2):
                        gather(l, i * 2 + u, u, i * 2 + u - 1)
                        gather_go(l, u, i + 1)
                n_ov = pool.value_load(route[0:1, 0:1], min_val=0, max_val=OVERFLOW)
                with pool.If(n_ov > 0), pool.Fori(0, n_ov) as j:
                    gather(l, j + EXPERTS, 0, j + EXPERTS)
                    gather_go(l, 0, j + EXPERTS // 2 + 1)
                pool.wait_ge(sem("z_filled"), 16 * 2 * LAYERS)
                for u in range(2):
                    pool.wait_ge(sem(f"z_stored_{l}_{u}"), 16 * (EXPERTS // 2) + 16 * GRANT)
                pool.wait_ge(sem(f"z_stored_{l}_ov"), n_ov * 16 + 16 * GRANT)
                settled()
                for t in range(NT):
                    u = t % 2
                    if t >= 2:
                        pool.wait_ge(sem(f"x_ready_{2 * l + 2}"), t - 1)
                    for k in range(2):
                        at = 16 + k * NT + t
                        pool.indirect_dma_start(z_in[u][k], None, z_dram[l], bass.IndirectOffsetOnAxis(ap=route[:, at:at + 1], axis=0),
                                                bounds_check=last_z, oob_is_err=False).then_inc(sem(f"z_in_{u}"), 16)

            norm_shift(0)
            unit = 0
            for t in range(NT):
                for h in range(HEADS):
                    pool.wait_ge(sem("prob_scale"), unit + 1)
                    for b in range(2):
                        n = (t + 1) * P
                        ins = pool.tensor_scalar(prob[:, unit % 2, b, 0:n], prob[:, unit % 2, b, 0:n],
                                                 inv_l(unit % 2)[:, b:b + 1], None, ALU.mult)
                    ins.then_inc(sem("prob_ready"), 1)
                    unit += 1
            norm_shift(1)
            moe_pool(0)
            norm_shift(2)
            pool.wait_ge(sem("proj1_ready"), 8)
            pool.memset(ml_vals[:, :, :, DV:VROW], 1.0).then_inc(sem("ml_ones"), 1)
            norm_shift(3)
            moe_pool(1)

        @block.tensor
        def _(pe):
            def ada_sum(u, b):
                pe.wait_ge(sem("ada_acc"), b + 1)
                pe.wait_ge(sem("ada_mods"), b + GRANT)
                pe.matmul(ps[:, 7, 0:ADA_W], ones[:, :], ada_acc[:, u, :], start=True, stop=True).then_inc(sem("ada_summed"), 1)

            def norm_transposes(n):
                for t in range(NT):
                    pe.wait_ge(sem("hn_ready"), NT * n + t + 1)
                    for half in range(2):
                        if t >= 2:
                            pe.wait_ge(sem(f"hT_{'ad'[half]}"), NT * n + t - 1)
                        for k in range(4):
                            ins = pe.transpose(ps[:, (t % 2) * 2 + half, k * P:(k + 1) * P],
                                               hnt[:, t, (4 * half + k) * P:(4 * half + k + 1) * P], ident)
                        ins.then_inc(sem("hT_tr"), 1)
                pe.wait_ge(sem("hT_a"), NT * (n + 1))
                pe.wait_ge(sem("hT_d"), NT * (n + 1))

            def nsa_project(t):
                for g in range(4):
                    cols = slice(512 * g, min(512 * g + 512, NSA_COLS))
                    if t:
                        pe.wait_ge(sem("proj0_taken"), 4 * (t - 1) + g + 1)
                    for k in range(KD):
                        ins = pe.matmul(ps[:, g, 0:cols.stop - cols.start], hTk[:, k, t * P:(t + 1) * P], w_in0[:, k, cols],
                                        start=(k == 0), stop=(k == KD - 1))
                    ins.then_inc(sem("proj0_ready"), 1)

            def nsa_transposes(t):
                pe.wait_ge(sem("nrm_ready"), t + 1)
                pe.wait_ge(sem("ada_mods"), ADA_BLOCKS + GRANT)
                if t:
                    pe.wait_ge(sem("qT_a"), t)
                    pe.wait_ge(sem("qT_d"), t)
                for pr in range(PAIRS):
                    pe.transpose(ps[:, 4 + pr // 4, (pr % 4) * P:(pr % 4 + 1) * P], nrm[t % 2][:, pr * P:(pr + 1) * P], ident)
                for b in range(2):
                    pe.transpose(ps[:, 6, b * P:(b + 1) * P], nrm[t % 2][:, 1024 + b * P:1024 + (b + 1) * P], ident)
                for a in range(2):
                    ins = pe.transpose(ps[:, 7, a * P:(a + 1) * P], kcv[t % 2][:, a * P:(a + 1) * P], ident)
                ins.then_inc(sem("nsa_tr"), 1)

            def compress():
                pe.wait_ge(sem("w1"), 32)
                pe.wait_ge(sem("nsa_small"), 16 * 10)
                for a in range(2):
                    pe.wait_ge(sem("cmp_dve"), a + 1)
                    for m in range(CMP_CHUNKS):
                        pe.matmul(ps[0:64, a, 0:CMP_HIDDEN], blk[:, a, m, :], w1[:, a, m, :], start=(m == 0), stop=False)
                    pe.matmul(ps[0:64, a, 0:CMP_HIDDEN], ones[0:1, 0:64], b1_row[:, a * CMP_HIDDEN:(a + 1) * CMP_HIDDEN],
                              start=False, stop=True).then_inc(sem("cmp_pe"), 1)
                for a in range(2):
                    pe.wait_ge(sem("cmp_act"), a + 1)
                    for m in range(2):
                        ins = pe.transpose(ps[:, 2, (2 * a + m) * 64:(2 * a + m + 1) * 64], hid_c[:, a, m * P:(m + 1) * P],
                                           ident[0:64, 0:64])
                ins.then_inc(sem("cmp_pe"), 1)
                pe.wait_ge(sem("cmp_act"), HIDDEN_T)
                for a in range(2):
                    for m in range(2):
                        pe.matmul(ps[0:64, 3 + a, 0:DH], hidT_c[:, 2 * a + m, :], w2[:, a, m, :],
                                  start=(m == 0), stop=False)
                    ins = pe.matmul(ps[0:64, 3 + a, 0:DH], ones[0:1, 0:64], b2_row[:, a * DH:(a + 1) * DH],
                                    start=False, stop=True)
                ins.then_inc(sem("cmp_pe"), 1)
                pe.wait_ge(sem("cmp_dve"), KEY_ROW)
                pe.transpose(ps[:, 0, 0:64], kcn, ident[0:64, 0:64]).then_inc(sem("cmp_pe"), 1)
                pe.wait_ge(sem("cmp_dve"), KEY_COLUMNS)

            def cmp_scores(t):
                if t >= 2:
                    pe.wait_ge(sem("cmp_s_read"), t - 1)
                for pr in range(PAIRS):
                    g = pr // (PAIRS // 2)
                    ins = pe.matmul(ps[:, 1 + t % 2, pr * 64:(pr + 1) * 64].rearrange("p (r c) -> p r c", r=2),
                                    qT[:, pr, t * P:(t + 1) * P],
                                    kctz[:, :, g * NC:(g + 1) * NC], start=True, stop=True)
                ins.then_inc(sem("cmp_s"), 1)

            def cmp_transposes(t):
                pe.wait_ge(sem("pc_ready"), t + 1)
                if t >= 2:
                    pe.wait_ge(sem("pcT_ready"), t - 1)
                for q in range(4):
                    ins = pe.transpose(ps[:, 4 + t % 2, q * P:(q + 1) * P], pc[:, t, q * P:(q + 1) * P], ident)
                ins.then_inc(sem("pc_tr"), 1)

            units = [(t, h) for t in range(NT) for h in range(HEADS)]

            def scores(n):
                t, h = units[n]
                if n >= 2:
                    pe.wait_ge(sem("exp_done"), n - 1)
                for b in range(2):
                    ins = pe.matmul(ps[:, 2 * (n % 2) + b, 0:(t + 1) * P], qT[:, h // 2, t * P:(t + 1) * P],
                                    ktz[:, b, h // 8, h % 2, 0:(t + 1) * P], start=True, stop=True)
                ins.then_inc(sem("scores"), 1)

            def prob_transposes(n):
                t, h = units[n]
                pe.wait_ge(sem("prob_ready"), n + 1)
                for b in range(2):
                    if n:
                        pe.wait_ge(sem(f"probT_{'ad'[b]}"), n)
                    for j in range(t + 1):
                        ins = pe.transpose(ps[:, 4 + b, j * P:(j + 1) * P], prob[:, n % 2, b, j * P:(j + 1) * P], ident)
                ins.then_inc(sem("prob_tr"), 1)

            def weighted_values(n):
                t, h = units[n]
                pr, r = n // 2, h % 2
                bank = 6 + pr % 2
                for b in range(2):
                    pe.wait_ge(sem(f"probT_{'ad'[b]}"), n + 1)
                if r == 0:
                    if pr >= 2:
                        pe.wait_ge(sem("oT_ready"), pr - 1)
                    quad, half = h // 4, (h // 2) % 2
                    pe.matmul(ps[:, bank, 0:P], vcbd[:, h // 8, half * P:(half + 1) * P], pcT[:, t, quad, :],
                              start=True, stop=False, skip_group_check=True)
                for b in range(2):
                    for j in range(t + 1):
                        ins = pe.matmul(ps[r * 64:(r + 1) * 64, bank, 0:P], vals[:, j, b, (h // 8) * DH:(h // 8 + 1) * DH],
                                        probT[:, n % 2, b, j * P:(j + 1) * P], start=False,
                                        stop=(b == 1 and j == t), skip_group_check=True)
                ins.then_inc(sem("pv"), 1)

            def out_project(l):
                pe.wait_ge(sem("w_out_loaded"), 16 * (l + 1))
                for t in range(NT):
                    for half in range(2):
                        if t >= 2:
                            pe.wait_ge(sem("y_taken"), 2 * (NT * l + t - 2) + half + 1)
                        for k in range(KD):
                            ins = pe.matmul(ps[:, 2 * (t % 2) + half, :], hTk[:, k, t * P:(t + 1) * P],
                                            w_out[l][:, k, half * 512:(half + 1) * 512], start=(k == 0), stop=(k == KD - 1))
                        ins.then_inc(sem("y_ready"), 1)

            def router(l):
                pe.wait_ge(sem("router_w"), 32 * (l + 1))
                for t in range(NT):
                    for k in range(KD):
                        ins = pe.matmul(ps[:, 6, t * EXPERTS:(t + 1) * EXPERTS], hTk[:, k, t * P:(t + 1) * P],
                                        arena[:, R_W + k * EXPERTS:R_W + (k + 1) * EXPERTS], start=(k == 0), stop=(k == KD - 1))
                ins.then_inc(sem("logits"), 1)
                pe.wait_ge(sem("chosen"), l + 1)
                tri = cs[:, C_TRI:C_TRI + P]
                for t in range(NT):
                    for s in range(t + 1):
                        pe.matmul(ps[:, 6, P + t * EXPERTS:P + (t + 1) * EXPERTS], tri if s == t else ones[:, :],
                                  arena[:, R_SUM + s * EXPERTS:R_SUM + (s + 1) * EXPERTS], start=(s == 0), stop=(s == t))
                for s in range(NT):
                    ins = pe.matmul(ps[:, 6, 2 * P:2 * P + EXPERTS], ones[:, :],
                                    arena[:, R_SUM + s * EXPERTS:R_SUM + (s + 1) * EXPERTS], start=(s == 0), stop=(s == NT - 1))
                ins.then_inc(sem("ranks"), 1)

            def x_transposes(l, u, nth, b):
                pe.wait_ge(sem(f"xb_{l}_{u}"), nth * 16 + 16)
                pe.wait_ge(sem(f"xbT_a_{l}"), b)
                pe.wait_ge(sem(f"xbT_d_{l}"), b)
                for k in range(KD):
                    ins = pe.transpose(ps[:, 2 + k // 4, (k % 4) * P:(k % 4 + 1) * P], xb[u][:, k * P:(k + 1) * P], ident)
                ins.then_inc(sem(f"xb_used_{l}"), 1)

            def gate_up(l, u, nth, b):
                pe.wait_ge(sem(f"wgu_{l}_{u}"), nth * 32 + 32)
                pe.wait_ge(sem(f"xbT_a_{l}"), b + 1)
                pe.wait_ge(sem(f"xbT_d_{l}"), b + 1)
                pe.wait_ge(sem(f"hid_{l}"), b)
                for m in range(2):
                    for k in range(KD):
                        ins = pe.matmul(ps[:, m, :], xbT[:, k, :], w_gu(u, m)[:, k, :], start=(k == 0), stop=(k == KD - 1))
                    ins.then_inc(sem(f"gu_{l}"), 1)

            def hid_transposes(l, b):
                pe.wait_ge(sem(f"hid_{l}"), b + 1)
                pe.wait_ge(sem(f"hidT_{l}"), b)
                for k in range(4):
                    ins = pe.transpose(ps[:, 6, k * P:(k + 1) * P], hid[:, k * P:(k + 1) * P], ident)
                ins.then_inc(sem(f"hid_tr_{l}"), 1)

            def down(l, u, nth, b):
                pe.wait_ge(sem(f"wd_{l}_{u}"), nth * 16 + 16)
                pe.wait_ge(sem(f"hidT_{l}"), b + 1)
                pe.wait_ge(sem(f"zb_{l}"), b + GRANT)
                for half in range(2):
                    for k in range(4):
                        ins = pe.matmul(ps[:, 4 + half, :], hidT[:, k, :], w_dn(u)[:, k, half * 512:(half + 1) * 512],
                                        start=(k == 0), stop=(k == 3))
                ins.then_inc(sem(f"y_{l}"), 1)

            def moe(l):
                router(l)
                x_transposes(l, 0, 0, 0)
                gate_up(l, 0, 0, 0)
                x_transposes(l, 1, 0, 1)
                hid_transposes(l, 0)

                def step(u, nth, b, prev_nth, next_nth):
                    gate_up(l, u, nth, b)
                    if next_nth is not None:
                        x_transposes(l, 1 - u, next_nth, b + 1)
                    down(l, 1 - u, prev_nth, b - 1)
                    hid_transposes(l, b)
                with pe.Fori(0, EXPERTS // 2 - 1) as i:
                    step(1, i, i * 2 + 1, i, i + 1)
                    if l == 0:
                        ada_sum(0, i + ADA_BLOCKS)
                    step(0, i + 1, i * 2 + 2, i, i + 1)
                last = EXPERTS - 1
                step(1, last // 2, last, last // 2, None)
                if l == 0:
                    ada_sum(0, 2 * ADA_BLOCKS - 1)
                down(l, 1, last // 2, last)
                n_ov = pe.value_load(route[0:1, 0:1], min_val=0, max_val=OVERFLOW)
                with pe.If(n_ov > 0), pe.Fori(0, n_ov) as j:
                    x_transposes(l, 0, j + EXPERTS // 2, j + EXPERTS)
                    gate_up(l, 0, j + EXPERTS // 2, j + EXPERTS)
                    hid_transposes(l, j + EXPERTS)
                    down(l, 0, j + EXPERTS // 2, j + EXPERTS)

            def mlstm_project():
                def begin(job):
                    if job >= 4:
                        pe.wait_ge(sem("proj1_taken"), job - 3)
                    return ps[:, job % 4, :]
                pe.wait_ge(sem("w_qk"), 16)
                w = area[:, M_QK:M_V].rearrange("p (k n) -> p k n", k=KD)
                for r in range(2 * MH):
                    o = begin(r)
                    for k in range(KD):
                        ins = pe.matmul(o, w[:, k, r * P:(r + 1) * P], hTk[:, k, :], start=(k == 0), stop=(k == KD - 1))
                    ins.then_inc(sem("proj1_ready"), 1)
                pe.wait_ge(sem("w_gates"), 48)
                wg = gates[:, 0:64].rearrange("p (k n) -> p k n", k=KD)
                for t in range(NT):
                    for k in range(KD):
                        ins = pe.matmul(ps[:, 4, t * 8:(t + 1) * 8], hTk[:, k, t * P:(t + 1) * P], wg[:, k, :],
                                        start=(k == 0), stop=(k == KD - 1))
                ins.then_inc(sem("ml_gate_pe"), 1)
                for part, (name, lo) in enumerate((("w_v", M_V), ("w_o", M_O))):
                    pe.wait_ge(sem(name), 16)
                    w = area[:, lo:lo + KD * D].rearrange("p (k n) -> p k n", k=KD)
                    for t in range(NT):
                        for half in range(2):
                            o = begin(8 + 8 * part + 2 * t + half)
                            for k in range(KD):
                                ins = pe.matmul(o, hTk[:, k, t * P:(t + 1) * P], w[:, k, half * 512:(half + 1) * 512],
                                                start=(k == 0), stop=(k == KD - 1))
                            ins.then_inc(sem("proj1_ready"), 1)
                    if part == 0:
                        pe.wait_ge(sem("ml_gate_dve"), 2)
                        for t in range(NT):
                            pe.transpose(ps[0:MH, 5, t * P:(t + 1) * P], ml_li[:, t, MH:2 * MH], ident)
                            ins = pe.transpose(ps[0:MH, 6, t * P:(t + 1) * P], ml_li[:, t, 0:MH], ident)
                        ins.then_inc(sem("ml_gate_pe"), 1)

            def mlstm():
                pe.wait_ge(sem("ml_gate_act"), 2)
                for t in range(NT):
                    pe.transpose(ps[:, 7, t * MH:(t + 1) * MH], ml_row(U_IN)[0:MH, t * P:(t + 1) * P], ident[0:MH, 0:MH])
                    ins = pe.transpose(ps[:, 7, 64 + t * MH:64 + (t + 1) * MH], ml_row(EXP_M)[0:MH, t * P:(t + 1) * P],
                                       ident[0:MH, 0:MH])
                ins.then_inc(sem("ml_gate_pe"), 1)
                pe.wait_ge(sem("ml_ones"), 1)
                for h in range(MH):
                    if h < 2:
                        pe.wait_ge(sem("ml_gate_act"), 3)
                    if h >= 2:
                        pe.wait_ge(sem("ml_w"), NT * (h - 1))
                        pe.wait_ge(sem("ml_diag"), h - 1)
                    pe.matmul(ps[:, 6 + h % 2, :], ml_sel[:, h, :], ml_row(U_MAX)[0:MH, :], start=True, stop=True)\
                      .then_inc(sem("ml_u"), 1)
                    if h == 0:
                        pe.wait_ge(sem("proj1_taken"), 24)

                    def ml_scores(j):
                        n = NT * h + j
                        if n >= 2:
                            pe.wait_ge(sem("ml_at"), n - 1)
                        pe.matmul(ps[:, 4 + n % 2, 0:(NT - j) * P], qT[:, MH + h, j * P:(j + 1) * P], qT[:, h, j * P:SEQ],
                                  start=True, stop=True).then_inc(sem("ml_s"), 1)

                    def ml_values(j):
                        n = NT * h + j
                        pe.wait_ge(sem("ml_at"), n + 1)
                        for t in reversed(range(j, NT)):
                            if j == 0 and h:
                                pe.wait_ge(sem("ml_raw"), NT * (h - 1) + t + 1)
                            ins = pe.matmul(ps[:, t, 0:VROW], ml_at(n % 2)[:, (t - j) * P:(t - j + 1) * P], ml_vals[:, j, h, :],
                                            start=(j == 0), stop=(j == t))
                        ins.then_inc(sem("ml_num"), 1)
                    ml_scores(0)
                    for j in range(NT):
                        if j + 1 < NT:
                            ml_scores(j + 1)
                        ml_values(j)
                for t in range(NT):
                    pe.wait_ge(sem("ml_out"), MH)
                    if t == 0:
                        pe.wait_ge(sem("ml_at"), NT * MH)
                        pe.wait_ge(sem("ml_diag"), MH)
                    for half in range(2):
                        if t >= 2:
                            pe.wait_ge(sem(f"mo_{'ad'[half]}"), t - 1)
                        for k in range(4):
                            ins = pe.transpose(ps[:, 4 + 2 * (t % 2) + half, k * P:(k + 1) * P],
                                               hnt[:, t, (4 * half + k) * P:(4 * half + k + 1) * P], ident)
                        ins.then_inc(sem("mo_tr"), 1)
                pe.wait_ge(sem("mo_a"), NT)
                pe.wait_ge(sem("mo_d"), NT)

            pe.sem_inc(sem("ada_summed"), GRANT)
            pe.wait_ge(sem("ones"), 1)
            pe.wait_ge(sem("consts"), 16)
            with pe.Fori(0, 4) as i:
                for u in range(2):
                    ada_sum(u, i * 2 + u)
            norm_transposes(0)
            pe.wait_ge(sem("w_in_0"), 32)
            nsa_project(0)
            with pe.Fori(4, 8) as i:
                for u in range(2):
                    ada_sum(u, i * 2 + u)
            for t in range(1, NT):
                nsa_project(t)
                nsa_transposes(t - 1)
            nsa_transposes(NT - 1)
            compress()
            pe.wait_ge(sem("qT_a"), NT)
            pe.wait_ge(sem("qT_d"), NT)
            for t in range(NT):
                cmp_scores(t)
                if t:
                    cmp_transposes(t - 1)
            cmp_transposes(NT - 1)
            pe.wait_ge(sem("pcT_ready"), NT)
            pe.wait_ge(sem("cmp_act"), CMP_VALUES)
            pe.wait_ge(sem("ada_mods"), ADA_BLOCKS + GRANT)
            for n in range(len(units) + 2):
                if n < len(units):
                    scores(n)
                if 1 <= n <= len(units):
                    prob_transposes(n - 1)
                if n >= 2:
                    weighted_values(n - 2)
            pe.wait_ge(sem("oT_ready"), NT * PAIRS)
            out_project(0)
            norm_transposes(1)
            moe(0)

            norm_transposes(2)
            mlstm_project()
            mlstm()
            out_project(1)
            norm_transposes(3)
            moe(1)

        @block.scalar
        def _(act):
            count = [0]

            def link(ins):
                count[0] += 1
                ins.then_inc(sem("act_chain"), 1)
                act.wait_ge(sem("act_chain"), count[0])

            def ada_take(b):
                act.wait_ge(sem("ada_summed"), b + 1 + GRANT)
                act.activation(mods[:, bass.ds(b * ADA_W, ADA_W)], ps[:, 7, 0:ADA_W], ACT.Copy).then_inc(sem("ada_mods"), 1)

            def norm(n):
                for t in range(NT):
                    act.wait_ge(sem(f"x_ready_{n}"), 16 if n == 0 else t + 1)
                    link(act.activation(ps[:, 4:6, :], xs[:, t, :].rearrange("p (a n) -> p a n", a=2), ACT.Square,
                                        accum_out=ssq[:, t:t + 1]))
                act.activation(var, ssq, ACT.Copy, scale=1.0 / D).then_inc(sem("norm_ssq"), 1)
                act.wait_ge(sem("norm_var"), n + 1)
                act.activation(rstd, var, ACT.Sqrt).then_inc(sem("norm_std"), 1)

            def norm_take(n):
                for t in range(NT):
                    act.wait_ge(sem("hT_tr"), 2 * (NT * n + t) + 1)
                    act.activation(hTk[:, 0:4, t * P:(t + 1) * P], ps[:, (t % 2) * 2, :].rearrange("p (k s) -> p k s", k=4),
                                   ACT.Copy).then_inc(sem("hT_a"), 1)

            def nsa_take(t):
                u = t % 2
                if t >= 2:
                    act.wait_ge(sem("nsa_tr"), t - 1)
                act.wait_ge(sem("nsa_zeroed"), 1)
                act.wait_ge(sem("proj0_ready"), 4 * t + 1)
                act.activation(nrm[u][:, 0:512], ps[:, 0, :], ACT.Copy).then_inc(sem("proj0_taken"), 1)
                act.wait_ge(sem("proj0_ready"), 4 * t + 2)
                act.activation(nrm[u][:, 512:1024], ps[:, 1, :], ACT.Copy).then_inc(sem("proj0_taken"), 1)
                act.wait_ge(sem("proj0_ready"), 4 * t + 3)
                act.activation(kcv[u], ps[:, 2, 0:256], ACT.Copy)
                act.activation(nrm[u][:, 1024:1152], ps[:, 2, 256:384], ACT.Copy)
                act.activation(vals[:, t, 0, :], ps[:, 2, 384:512], ACT.Copy).then_inc(sem("proj0_taken"), 1)
                act.wait_ge(sem("proj0_ready"), 4 * t + 4)
                act.activation(nrm[u][:, 1152:1280], ps[:, 3, 0:128], ACT.Copy)
                act.activation(vals[:, t, 1, :], ps[:, 3, 128:256], ACT.Copy)
                act.activation(gates[:, t * 48:(t + 1) * 48], ps[:, 3, 256:304], ACT.Sigmoid).then_inc(sem("proj0_taken"), 1)

            def nsa_std(t):
                act.wait_ge(sem("head_var"), t + 1)
                act.activation(head_rstd(t % 2), head_rstd(t % 2), ACT.Sqrt).then_inc(sem("head_std"), 1)

            def nsa_take_T(t):
                cols = slice(t * P, (t + 1) * P)
                act.wait_ge(sem("nsa_tr"), t + 1)
                act.activation(qT[:, 0:4, cols], ps[:, 4, :].rearrange("p (r s) -> p r s", r=4), ACT.Copy)
                src = ps[:, 7, 0:256].rearrange("p (a s) -> p a s", a=2)
                for g in range(2):
                    rows = slice(64 * g, 64 * g + 64)
                    act.activation(kcvT[0:64, :, g, t * P + 1:t * P + 1 + P], src[rows, :, :], ACT.Copy)
                    ins = act.activation(kcvT[64:128, :, g, t * P:t * P + P], src[rows, :, :], ACT.Copy)
                ins.then_inc(sem("qT_a"), 1)

            def compress():
                for a in range(2):
                    act.wait_ge(sem("cmp_pe"), a + 1)
                    act.activation(hid_c[:, a, :], ps[0:64, a, 0:CMP_HIDDEN], ACT.Gelu_apprx_tanh).then_inc(sem("cmp_act"), 1)
                act.wait_ge(sem("cmp_pe"), HIDDEN_T)
                act.activation(hidT_c, ps[:, 2, 0:256].rearrange("p (q c) -> p q c", q=4), ACT.Copy).then_inc(sem("cmp_act"), 1)
                act.wait_ge(sem("cmp_pe"), CMP_OUT)
                for g in range(2):
                    for j in range(4):
                        ins = act.activation(vcbd[32 * j:32 * j + 32, g, 64 * j:64 * j + 64], ps[32 * g:32 * g + 32, 4, 0:DH],
                                             ACT.Copy)
                ins.then_inc(sem("cmp_act"), 1)
                act.wait_ge(sem("cmp_dve"), KEY_VAR)
                act.activation(head_ss[0:64, 1:2], head_ss[0:64, 1:2], ACT.Sqrt).then_inc(sem("cmp_act"), 1)

            def cmp_exp(t):
                act.wait_ge(sem("pc_shifted"), t + 1)
                act.activation(pc[:, t, :], pc[:, t, :], ACT.Exp).then_inc(sem("pc_exp"), 1)

            def cmp_take(t):
                act.wait_ge(sem("pc_tr"), t + 1)
                act.activation(pcT[:, t, :, :], ps[:, 4 + t % 2, :].rearrange("p (q n) -> p q n", q=4), ACT.Copy)\
                   .then_inc(sem("pcT_ready"), 1)

            units = [(t, h) for t in range(NT) for h in range(HEADS)]

            def attend():
                for n in range(len(units) + 2):
                    if n < len(units):
                        t, h = units[n]
                        act.wait_ge(sem("neg_max"), n + 1)
                        if n >= 2:
                            act.wait_ge(sem("prob_tr"), n - 1)
                        for b in range(2):
                            ins = act.activation(prob[:, n % 2, b, 0:(t + 1) * P], ps[:, 2 * (n % 2) + b, 0:(t + 1) * P],
                                                 ACT.Exp, bias=neg_max(n % 2)[:, b:b + 1], scale=SCALE,
                                                 accum_out=sum_l(n % 2)[:, b:b + 1])
                        ins.then_inc(sem("exp_done"), 1)
                    if 1 <= n <= len(units):
                        m = n - 1
                        t, h = units[m]
                        act.wait_ge(sem("prob_tr"), m + 1)
                        if m >= 2:
                            act.wait_ge(sem("pv"), m - 1)
                        act.activation(probT[:, m % 2, 0, 0:(t + 1) * P], ps[:, 4, 0:(t + 1) * P], ACT.Copy)\
                           .then_inc(sem("probT_a"), 1)
                    if n >= 2 and (n - 2) % 2:
                        m = n - 2
                        t, h = units[m]
                        act.wait_ge(sem("pv"), m + 1)
                        act.activation(hTk[:, h // 2, t * P:(t + 1) * P], ps[:, 6 + (m // 2) % 2, 0:P], ACT.Copy)\
                           .then_inc(sem("oT_ready"), 1)

            def moe(l):
                act.wait_ge(sem("logits"), l + 1)
                act.activation(arena[:, R_AFF:R_AFF + P], ps[:, 6, 0:P], ACT.Sigmoid).then_inc(sem("affinity"), 1)
                act.activation(ffn_gate, mods[:, G_F:G_F + D], ACT.Copy).then_inc(sem("ffn_gate"), 1)

                def take_x(b):
                    act.wait_ge(sem(f"xb_used_{l}"), b + 1)
                    act.activation(xbT[:, 0:4, :], ps[:, 2, :].rearrange("p (k s) -> p k s", k=4), ACT.Copy)\
                       .then_inc(sem(f"xbT_a_{l}"), 1)

                def sigmoid(b):
                    act.wait_ge(sem(f"gu_{l}"), b * 2 + 1)
                    act.activation(sig, ps[:, 0, :], ACT.Sigmoid).then_inc(sem(f"sig_{l}"), 1)
                    act.wait_ge(sem(f"gu_{l}"), b * 2 + 2)

                def take_y(b, u, nth, stored=None):
                    rows = z_dram[l].rearrange("(b s) d -> s b d", s=SLOTS)[:, bass.ds(b, 1), :]
                    act.wait_ge(sem(f"y_{l}"), b + 1)
                    stored = stored or f"z_stored_{l}_{u}"
                    act.wait_ge(sem(stored), nth * 16 + 16 * GRANT)
                    act.activation(zb[u].rearrange("p (a n) -> p a n", a=2), ps[:, 4:6, :], ACT.Copy).then_inc(sem(f"zb_{l}"), 1)
                    act.wait_ge(sem(f"zb_{l}"), b + 1 + GRANT)
                    act.dma_start(rows, zb[u].rearrange("p (b n) -> p b n", b=1)).then_inc(sem(stored), 16)

                def take_hid(b):
                    act.wait_ge(sem(f"hid_tr_{l}"), b + 1)
                    act.activation(hidT, ps[:, 6, :].rearrange("p (k s) -> p k s", k=4), ACT.Copy).then_inc(sem(f"hidT_{l}"), 1)

                act.sem_inc(sem(f"zb_{l}"), GRANT)
                for which in ("0", "1", "ov"):
                    act.sem_inc(sem(f"z_stored_{l}_{which}"), 16 * GRANT)
                take_x(0)
                sigmoid(0)
                take_x(1)
                take_hid(0)

                def step(u, b, prev_nth, last=False):
                    sigmoid(b)
                    if not last:
                        take_x(b + 1)
                    take_y(b - 1, 1 - u, prev_nth)
                    take_hid(b)
                with act.Fori(0, EXPERTS // 2 - 1) as i:
                    step(1, i * 2 + 1, i)
                    if l == 0:
                        act.wait_ge(sem("ada_summed"), i + ADA_BLOCKS + 1 + GRANT)
                        act.activation(mods[:, bass.ds(i * ADA_W, ADA_W)], ps[:, 7, 0:ADA_W], ACT.Copy).then_inc(sem("ada_mods"), 1)
                    step(0, i * 2 + 2, i)
                last = EXPERTS - 1
                step(1, last, last // 2, last=True)
                if l == 0:
                    act.wait_ge(sem("ada_summed"), 2 * ADA_BLOCKS + GRANT)
                    act.activation(mods[:, (ADA_BLOCKS - 1) * ADA_W:ADA_COLS], ps[:, 7, 0:ADA_W], ACT.Copy)\
                       .then_inc(sem("ada_mods"), 1)
                take_y(last, 1, last // 2)
                act.wait_ge(sem(f"z_stored_{l}_0"), 16 * (EXPERTS // 2) + 16 * GRANT)
                n_ov = act.value_load(route[0:1, 0:1], min_val=0, max_val=OVERFLOW)
                with act.If(n_ov > 0), act.Fori(0, n_ov) as j:
                    take_x(j + EXPERTS)
                    sigmoid(j + EXPERTS)
                    take_hid(j + EXPERTS)
                    act.wait_ge(sem("z_filled"), 16 * 2 * LAYERS)
                    take_y(j + EXPERTS, 0, j, stored=f"z_stored_{l}_ov")

            def mlstm_take(job):
                act.wait_ge(sem("proj1_ready"), job + 1)
                src = ps[:, job % 4, :]
                if job < 8:
                    ins = act.activation(qT[:, job, :], src, ACT.Copy)
                elif job < 16:
                    t, half = divmod(job - 8, 2)
                    ins = act.activation(ml_vals[:, t, 2 * half:2 * half + 2, 0:DV], src.rearrange("p (h d) -> p h d", h=2), ACT.Copy)
                else:
                    t, half = divmod(job - 16, 2)
                    ins = act.activation(hnt[:, t, half * 512:(half + 1) * 512], src, ACT.Sigmoid)
                ins.then_inc(sem("proj1_taken"), 1)

            def mlstm_gates():
                act.wait_ge(sem("ml_gate_dve"), 1)
                link(act.activation(ml_li, ml_li, ACT.Tanh, scale=1.0 / SOFTCAP))
                link(act.activation(ml_li[:, :, MH:2 * MH], ml_li[:, :, MH:2 * MH], ACT.Exp, scale=-SOFTCAP))
                act.activation(ml_li[:, :, MH:2 * MH], ml_li[:, :, MH:2 * MH], ACT.Ln, bias=1.0).then_inc(sem("ml_gate_act"), 1)

            def mlstm():
                act.wait_ge(sem("ml_gate_dve"), 3)
                act.activation(ml_row(EXP_M)[0:MH, :], ml_row(EXP_M)[0:MH, :], ACT.Exp, scale=-1.0).then_inc(sem("ml_gate_act"), 1)
                act.wait_ge(sem("ml_gate_pe"), 3)
                act.activation(ml_cols, ps[:, 7, 0:128].rearrange("p (a n) -> p a n", a=2)[:, :, 0:16], ACT.Copy)\
                   .then_inc(sem("ml_gate_act"), 1)
                act.wait_ge(sem("ml_gate_act"), 3)
                for h in range(MH):
                    act.wait_ge(sem("ml_u"), h + 1)
                    act.wait_ge(sem("ml_diag"), h + 1)
                    for j in range(NT):
                        n = NT * h + j
                        if n >= 2:
                            act.wait_ge(sem("ml_at"), n - 1)
                        u_col = ml_cols[:, 0, j * MH + h:j * MH + h + 1]
                        ins = act.activation(ml_w(n % 2)[:, 0:P], ml_diag[:, j * P:(j + 1) * P], ACT.Exp, bias=u_col, scale=-1.0)
                        if j < NT - 1:
                            ins = act.activation(ml_w(n % 2)[:, P:(NT - j) * P], ps[:, 6 + h % 2, (j + 1) * P:SEQ], ACT.Exp,
                                                 bias=u_col, scale=-1.0)
                        ins.then_inc(sem("ml_w"), 1)
                    for t in range(NT):
                        if h >= 2:
                            act.wait_ge(sem("ml_raw_read"), h - 1)
                        act.wait_ge(sem("ml_num"), NT * h + t + 1)
                        act.activation(ml_raw(h % 2)[:, t, :], ps[:, t, 0:VROW], ACT.Copy).then_inc(sem("ml_raw"), 1)
                    for f in ([h - 1] if h else []) + ([h] if h == MH - 1 else []):
                        act.wait_ge(sem("ml_hvar"), f + 1)
                        act.activation(head_ss[:, 4:8], head_ss[:, 4:8], ACT.Sqrt).then_inc(sem("ml_hstd"), 1)
                for t in range(NT):
                    act.wait_ge(sem("mo_tr"), 2 * t + 1)
                    act.activation(hTk[:, 0:4, t * P:(t + 1) * P], ps[:, 4 + 2 * (t % 2), :].rearrange("p (k s) -> p k s", k=4),
                                   ACT.Copy).then_inc(sem("mo_a"), 1)

            act.sem_inc(sem("ada_mods"), GRANT)
            act.wait_ge(sem("c_loaded"), 16)
            act.activation(cond[:, KD:2 * KD], cond[:, 0:KD], ACT.Sigmoid).then_inc(sem("cond_sig"), 1)
            with act.Fori(0, 8) as b:
                ada_take(b)
            norm(0)
            norm_take(0)
            nsa_take(0)
            with act.Fori(8, ADA_BLOCKS) as b:
                ada_take(b)
            nsa_std(0)
            for t in range(1, NT):
                nsa_take(t)
                nsa_take_T(t - 1)
                nsa_std(t)
            nsa_take_T(NT - 1)
            compress()
            for t in range(NT):
                cmp_exp(t)
                if t:
                    cmp_take(t - 1)
            cmp_take(NT - 1)
            attend()
            norm(1)
            norm_take(1)
            moe(0)

            norm(2)
            norm_take(2)
            for job in range(8):
                mlstm_take(job)
            mlstm_gates()
            for job in range(8, 24):
                mlstm_take(job)
            mlstm()
            norm(3)
            norm_take(3)
            moe(1)

        @block.vector
        def _(dve):
            count = [0]

            def link(ins):
                count[0] += 1
                ins.then_inc(sem("dve_chain"), 1)
                dve.wait_ge(sem("dve_chain"), count[0])

            def ada_products(buf, u, done, steps):
                dve.wait_ge(sem("ada_summed"), done + GRANT)
                src = ada_bias[:, u, :]
                for k in range(KD):
                    ins = dve.scalar_tensor_tensor(out=ada_acc[:, u, :], in0=buf[:, k, :], scalar=cond[:, KD + k:KD + k + 1],
                                                   in1=src, op0=ALU.mult, op1=ALU.add)
                    src = ada_acc[:, u, :]
                    if k < KD - 1:
                        ins.then_inc(sem("ada_chain"), 1)
                        dve.wait_ge(sem("ada_chain"), steps * (KD - 1) + (k + 1))
                return ins

            def ada_block(which, buf, u, nth, b, summed):
                dve.wait_ge(sem(f"ada_loaded_{which}"), nth * 32 + 32)
                ada_products(buf, u, summed, b).then_inc(sem("ada_acc"), 1)
                dve.wait_ge(sem("ada_acc"), b + 1)
                dve.sem_inc(sem(f"ada_read_{which}"), 1)

            def norm(n):
                scale = SC_F if n % 2 else SC_M
                dve.wait_ge(sem("norm_gain"), 16 * (n + 1))
                if n in (0, 2):
                    dve.wait_ge(sem("ada_mods"), (8 if n == 0 else 2 * ADA_BLOCKS) + GRANT)
                if n == 1:
                    dve.wait_ge(sem("ada_mods"), ADA_BLOCKS + GRANT)
                link(dve.scalar_tensor_tensor(out=mods[:, scale:scale + D], in0=mods[:, scale:scale + D], scalar=1.0,
                                              in1=gain_tile, op0=ALU.add, op1=ALU.mult))
                dve.wait_ge(sem("norm_ssq"), n + 1)
                dve.tensor_scalar(var, var, EPS, None, ALU.add).then_inc(sem("norm_var"), 1)
                dve.wait_ge(sem("norm_std"), n + 1)
                link(dve.reciprocal(rstd, rstd))
                for t in range(NT):
                    dve.scalar_tensor_tensor(out=hnt[:, t, :], in0=xs[:, t, :], scalar=rstd[:, t:t + 1],
                                             in1=mods[:, scale:scale + D], op0=ALU.mult, op1=ALU.mult)\
                       .then_inc(sem("hn_scaled"), 1)

            def norm_take(n):
                for t in range(NT):
                    dve.wait_ge(sem("hT_tr"), 2 * (NT * n + t) + 2)
                    dve.tensor_copy(hTk[:, 4:8, t * P:(t + 1) * P], ps[:, (t % 2) * 2 + 1, :].rearrange("p (k s) -> p k s", k=4))\
                       .then_inc(sem("hT_d"), 1)

            def rope(heads, cos, sin, tmp):
                x1, x2 = heads[:, :, 0:HALF], heads[:, :, HALF:ROT]
                rows, n = heads.shape[0], heads.shape[1]
                shape = [rows, n, HALF]
                cos = cos.rearrange("p (o e) -> p o e", o=1).to_broadcast(shape)
                sin = sin.rearrange("p (o e) -> p o e", o=1).to_broadcast(shape)
                a, b, d = tmp
                dve.tensor_tensor(a, x1, cos, ALU.mult)
                dve.tensor_tensor(b, x2, sin, ALU.mult)
                link(dve.tensor_tensor(d, x1, sin, ALU.mult))
                link(dve.tensor_tensor(x1, a, b, ALU.subtract))
                link(dve.tensor_tensor(a, x2, cos, ALU.mult))
                return dve.tensor_tensor(x2, a, d, ALU.add)

            def nsa_norm(t):
                u = t % 2
                heads = nrm[u].rearrange("p (h e) -> p h e", e=DH)
                dve.wait_ge(sem("proj0_taken"), 4 * t + 4)
                for lo in range(0, 20, 8):
                    n = min(8, 20 - lo)
                    sq = area[:, A_SMALL:A_SMALL + n * DH]
                    link(dve.tensor_tensor(sq, nrm[u][:, lo * DH:(lo + n) * DH], nrm[u][:, lo * DH:(lo + n) * DH], ALU.mult))
                    link(dve.tensor_reduce(head_rstd(u)[:, lo:lo + n], sq.rearrange("p (h e) -> p h e", e=DH), AX, ALU.add))
                dve.tensor_scalar(head_rstd(u), head_rstd(u), 1.0 / DH, EPS, ALU.mult, ALU.add).then_inc(sem("head_var"), 1)
                dve.wait_ge(sem("head_std"), t + 1)
                link(dve.reciprocal(head_rstd(u), head_rstd(u)))
                link(dve.tensor_tensor(heads, heads, head_rstd(u).rearrange("p (h o) -> p h o", o=1).to_broadcast([P, 20, DH]),
                                       ALU.mult))
                for g, (lo, hi) in enumerate(((0, 16), (16, 18), (18, 20))):
                    gain = hgain[:, g * DH:(g + 1) * DH].rearrange("p (o e) -> p o e", o=1).to_broadcast([P, hi - lo, DH])
                    ins = dve.tensor_tensor(heads[:, lo:hi, :], heads[:, lo:hi, :], gain, ALU.mult)
                link(ins)
                at = C_ROPE + t * ROT
                rope(heads, cs[:, at:at + HALF], cs[:, at + HALF:at + ROT],
                     [r.rearrange("p (h e) -> p h e", e=HALF) for r in rope_tmp]).then_inc(sem("nrm_ready"), 1)

            def nsa_take_T(t):
                cols = slice(t * P, (t + 1) * P)
                dve.wait_ge(sem("nsa_tr"), t + 1)
                dve.tensor_copy(qT[:, 4:8, cols], ps[:, 5, :].rearrange("p (r s) -> p r s", r=4))
                src = ps[:, 6, 0:256].rearrange("p (b s) -> p b s", b=2)
                for g in range(2):
                    for r in range(2):
                        ins = dve.tensor_copy(ktz[64 * r:64 * r + 64, :, g, r, cols], src[64 * g:64 * g + 64, :, :])
                ins.then_inc(sem("qT_d"), 1)

            def compress():
                dve.wait_ge(sem("qT_a"), NT)
                for a in range(2):
                    for g in range(2):
                        for hi in range(2):
                            lo = 1 + 16 * hi
                            src = kcvT[:, a, g, lo:lo + SEQ].rearrange("p (c m two) -> p m c two", m=8, two=2)[:, :, :, 0]
                            ins = dve.tensor_tensor(blk[:, a, 8 * hi:8 * hi + 8, g * NC:(g + 1) * NC], src,
                                                    pe_t[:, a, 8 * hi:8 * hi + 8].rearrange("p (m o) -> p m o", o=1)
                                                    .to_broadcast([P, 8, NC]), ALU.add)
                    ins.then_inc(sem("cmp_dve"), 1)
                k0 = kcn[:, 0:DH]
                dve.wait_ge(sem("cmp_pe"), CMP_OUT)
                link(dve.tensor_copy(k0, ps[0:64, 3, 0:DH]))
                link(dve.tensor_tensor(ksq, k0, k0, ALU.mult))
                link(dve.tensor_reduce(head_ss[0:64, 0:1], ksq, AX, ALU.add))
                dve.tensor_scalar(head_ss[0:64, 1:2], head_ss[0:64, 0:1], 1.0 / DH, EPS, ALU.mult, ALU.add).then_inc(sem("cmp_dve"), 1)
                dve.wait_ge(sem("cmp_act"), KEY_STD)
                link(dve.reciprocal(head_ss[0:64, 2:3], head_ss[0:64, 1:2]))
                link(dve.scalar_tensor_tensor(out=k0, in0=k0, scalar=head_ss[0:64, 2:3], in1=hgain[0:64, 3 * DH:4 * DH],
                                              op0=ALU.mult, op1=ALU.mult))
                link(rope(k0.rearrange("p (h e) -> p h e", h=1), cs[0:64, C_CROPE:C_CROPE + HALF],
                          cs[0:64, C_CROPE + HALF:C_CROPE + ROT],
                          [r[0:64, 0:HALF].rearrange("p (h e) -> p h e", e=HALF) for r in rope_tmp]))
                dve.tensor_copy(kcn[:, DH:2 * DH], k0).then_inc(sem("cmp_dve"), 1)
                dve.wait_ge(sem("cmp_pe"), KEY_T)
                dve.tensor_copy(kctz[0:64, 0, :], ps[0:64, 0, 0:64])
                dve.tensor_copy(kctz[64:128, 1, :], ps[64:128, 0, 0:64]).then_inc(sem("cmp_dve"), 1)

            def cmp_softmax(t):
                s = pc[:, t, :]
                heads = s.rearrange("p (h c) -> p h c", c=NC)

                def over_slots(v):
                    return v.rearrange("p (h o) -> p h o", o=1).to_broadcast([P, HEADS, NC])
                mask = cs[:, C_CMASK + t * NC:C_CMASK + (t + 1) * NC].rearrange("p (o c) -> p o c", o=1)\
                    .to_broadcast([P, HEADS, NC])
                r = cmp_r
                dve.wait_ge(sem("cmp_s"), t + 1)
                dve.scalar_tensor_tensor(out=heads, in0=ps[:, 1 + t % 2, :].rearrange("p (h c) -> p h c", c=NC), scalar=SCALE,
                                         in1=mask, op0=ALU.mult, op1=ALU.add).then_inc(sem("cmp_s_read"), 1)
                dve.wait_ge(sem("cmp_s_read"), t + 1)
                link(dve.tensor_reduce(r, heads, AX, ALU.max))
                dve.tensor_tensor(heads, heads, over_slots(r), ALU.subtract).then_inc(sem("pc_shifted"), 1)
                dve.wait_ge(sem("pc_exp"), t + 1)
                link(dve.tensor_reduce(r, heads, AX, ALU.add))
                link(dve.reciprocal(r, r))
                link(dve.scalar_tensor_tensor(out=r, in0=r, scalar=cs[:, C_ROWOK + t:C_ROWOK + t + 1],
                                              in1=gates[:, t * 48:t * 48 + HEADS], op0=ALU.mult, op1=ALU.mult))
                dve.tensor_tensor(heads, heads, over_slots(r), ALU.mult).then_inc(sem("pc_ready"), 1)

            units = [(t, h) for t in range(NT) for h in range(HEADS)]

            def attend():
                causal = cs[:, C_CAUSAL:C_CAUSAL + P].rearrange("p (o s) -> p o s", o=1).to_broadcast([P, 2, P])
                for n in range(len(units) + 2):
                    if n < len(units):
                        t, h = units[n]
                        u = n % 2
                        s = ps[:, 2 * u:2 * u + 2, :]
                        dve.wait_ge(sem("scores"), n + 1)
                        link(dve.tensor_tensor(s[:, :, t * P:(t + 1) * P], s[:, :, t * P:(t + 1) * P], causal, ALU.add))
                        link(dve.tensor_reduce(raw_max(u), s[:, :, 0:(t + 1) * P], AX, ALU.max))
                        dve.tensor_scalar(neg_max(u), raw_max(u), -SCALE, None, ALU.mult).then_inc(sem("neg_max"), 1)
                    if 1 <= n <= len(units):
                        m = n - 1
                        t, h = units[m]
                        dve.wait_ge(sem("prob_tr"), m + 1)
                        if m >= 2:
                            dve.wait_ge(sem("pv"), m - 1)
                        dve.tensor_copy(probT[:, m % 2, 1, 0:(t + 1) * P], ps[:, 5, 0:(t + 1) * P]).then_inc(sem("probT_d"), 1)
                    if n < len(units):
                        t, h = units[n]
                        u = n % 2
                        gate = gates[:, t * 48 + 16:t * 48 + 48].rearrange("p (b h) -> p b h", b=2)[:, :, h]
                        dve.wait_ge(sem("exp_done"), n + 1)
                        if n >= 2:
                            dve.wait_ge(sem("prob_ready"), n - 1)
                        link(dve.reciprocal(inv_l(u), sum_l(u)))
                        dve.tensor_tensor(inv_l(u), inv_l(u), gate, ALU.mult).then_inc(sem("prob_scale"), 1)

            def residual(l):
                for t in range(NT):
                    for half in range(2):
                        y = ps[:, 2 * (t % 2) + half, :]
                        cols = slice(half * 512, (half + 1) * 512)
                        dve.wait_ge(sem("y_ready"), 2 * (NT * l + t) + half + 1)
                        link(dve.tensor_tensor(y, y, mods[:, G_M + half * 512:G_M + (half + 1) * 512], ALU.mult))
                        dve.tensor_tensor(xs[:, t, cols], xs[:, t, cols], y, ALU.add).then_inc(sem("y_taken"), 1)
                        dve.wait_ge(sem("y_taken"), 2 * (NT * l + t) + half + 1)
                    dve.sem_inc(sem(f"x_ready_{2 * l + 1}"), 1)
                    dve.sem_inc(sem("w_out_used"), 1)

            def routing(l):
                def a(lo, n=P):
                    return arena[:, lo:lo + n]

                def t_e(v):
                    return v.rearrange("p (t e) -> p t e", t=NT)

                def tg_e(v):
                    return v.rearrange("p (q e) -> p q e", e=EPG)
                AFF, CH, EQ, MSK, E1, E2, SUM, BLK, SLT, F, TMP = (a(r) for r in (R_AFF, R_CH, R_EQ, R_MSK, R_E1, R_E2, R_SUM,
                                                                                 R_BLK, R_SLOT, R_F, R_TMP))
                M1, M2, FI, GS, GO = (a(R_S + 16 * i, 16) for i in range(5))
                OV, CUM, EXC = (a(R_S + 96 + 32 * i, 32) for i in range(3))
                QUAD = [a(R_S + 192 + 4 * i, 4) for i in range(16)]
                OVX = a(R_S + 256, 8)
                CNT = a(R_S + 264, 32)
                OVC = a(R_S + 296, 8 * EXPERTS)

                def bc(v, shape):
                    return v.rearrange("p (q o) -> p q o", o=1).to_broadcast(shape)

                def row(lo, n, times):
                    return cs[:, lo:lo + n].rearrange("p (o e) -> p o e", o=1).to_broadcast([P, times, n])

                def first_of(values, best, hot, groups, per, iota):
                    v, h3 = (w.rearrange("p (q e) -> p q e", e=per) for w in (values, hot))
                    fi = FI[:, 0:groups]
                    link(dve.tensor_tensor(h3, v, bc(best, [P, groups, per]), ALU.is_equal))
                    link(dve.tensor_tensor(h3, h3, row(iota, per, groups), ALU.mult))
                    link(dve.tensor_reduce(fi, h3, AX, ALU.min))
                    link(dve.tensor_tensor(h3, row(iota, per, groups), bc(fi, [P, groups, per]), ALU.is_equal))

                dve.wait_ge(sem("affinity"), l + 1)
                dve.wait_ge(sem("router_w"), 32 * (l + 1))
                link(dve.tensor_tensor(t_e(CH), t_e(AFF), a(R_B, EXPERTS).rearrange("p (o e) -> p o e", o=1)
                                       .to_broadcast([P, NT, EXPERTS]), ALU.add))
                link(dve.tensor_reduce(M1, tg_e(CH), AX, ALU.max))
                first_of(CH, M1, E1, NT * EGROUPS, EPG, C_IOTA_8)
                link(dve.scalar_tensor_tensor(out=MSK, in0=E1, scalar=NEG, in1=CH, op0=ALU.mult, op1=ALU.add))
                link(dve.tensor_reduce(M2, tg_e(MSK), AX, ALU.max))
                first_of(MSK, M2, E2, NT * EGROUPS, EPG, C_IOTA_8)
                link(dve.tensor_tensor(GS, M1, M2, ALU.add))
                link(dve.tensor_reduce(QUAD[0], GS.rearrange("p (t g) -> p t g", t=NT), AX, ALU.max))
                first_of(GS, QUAD[0], GO, NT, EGROUPS, C_IOTA_4)
                for e in (E1, E2):
                    link(dve.tensor_tensor(tg_e(e), tg_e(e), bc(GO, [P, NT * EGROUPS, EPG]), ALU.mult))
                dve.tensor_tensor(SUM, E1, E2, ALU.add).then_inc(sem("chosen"), 1)
                for k, e in enumerate((E1, E2)):
                    link(dve.tensor_tensor(TMP, AFF, e, ALU.mult))
                    link(dve.tensor_reduce(QUAD[1 + k], t_e(TMP), AX, ALU.add))
                link(dve.tensor_tensor(QUAD[3], QUAD[1], QUAD[2], ALU.add))
                link(dve.reciprocal(QUAD[3], QUAD[3]))
                dve.tensor_tensor(moe_w(0), QUAD[1], QUAD[3], ALU.mult)
                link(dve.tensor_tensor(moe_w(1), QUAD[2], QUAD[3], ALU.mult))
                dve.wait_ge(sem("ranks"), l + 1)
                dve.tensor_copy(CNT, ps[:, 6, 2 * P:2 * P + EXPERTS])
                link(dve.tensor_copy(TMP, ps[:, 6, P:2 * P]))
                for dst, src in ((F, TMP), (OV, CNT)):
                    bound = SLOTS if dst is F else SLOTS + 1
                    link(dve.tensor_scalar(dst, src, float(bound), None, ALU.is_ge))
                    for m in range(1, SEQ // SLOTS - 1):
                        link(dve.scalar_tensor_tensor(out=dst, in0=src, scalar=float(bound + m * SLOTS), in1=dst,
                                                      op0=ALU.is_ge, op1=ALU.add))
                link(dve.scalar_tensor_tensor(out=SLT, in0=F, scalar=-float(SLOTS), in1=TMP, op0=ALU.mult, op1=ALU.add))
                link(dve.tensor_tensor_scan(CUM, OV, cs[:, C_ZERO:C_ZERO + EXPERTS], 0.0, ALU.add, ALU.add))
                link(dve.tensor_tensor(EXC, CUM, OV, ALU.subtract))
                iota_e = cs[:, C_IOTA_E:C_IOTA_E + EXPERTS]
                link(dve.tensor_tensor(EXC, EXC, iota_e, ALU.subtract))
                link(dve.scalar_tensor_tensor(out=t_e(TMP), in0=t_e(F), scalar=float(EXPERTS - 1),
                                              in1=EXC.rearrange("p (o e) -> p o e", o=1).to_broadcast([P, NT, EXPERTS]),
                                              op0=ALU.add, op1=ALU.add))
                link(dve.scalar_tensor_tensor(out=BLK, in0=F, scalar=0.0, in1=TMP, op0=ALU.is_gt, op1=ALU.mult))
                link(dve.tensor_tensor(t_e(BLK), t_e(BLK), row(C_IOTA_E, EXPERTS, NT), ALU.add))
                for k, e in enumerate((E1, E2)):
                    b_k, s_k, at_s, at_z = QUAD[4 + 4 * k:8 + 4 * k]
                    link(dve.tensor_tensor(TMP, BLK, e, ALU.mult))
                    link(dve.tensor_reduce(b_k, t_e(TMP), AX, ALU.add))
                    link(dve.tensor_tensor(TMP, SLT, e, ALU.mult))
                    link(dve.tensor_reduce(s_k, t_e(TMP), AX, ALU.add))
                    dve.scalar_tensor_tensor(out=at_s, in0=s_k, scalar=float(NB), in1=b_k, op0=ALU.mult, op1=ALU.add)
                    link(dve.scalar_tensor_tensor(out=at_z, in0=b_k, scalar=float(SLOTS), in1=s_k, op0=ALU.mult, op1=ALU.add))
                    dve.tensor_copy(route[:, 8 + k * NT:8 + (k + 1) * NT], at_s)
                    link(dve.tensor_copy(route[:, 16 + k * NT:16 + (k + 1) * NT], at_z))
                ovc = OVC.rearrange("p (j e) -> p j e", e=EXPERTS)
                link(dve.tensor_tensor(ovc, CUM.rearrange("p (o e) -> p o e", o=1).to_broadcast([P, 8, EXPERTS]),
                                       bc(cs[:, C_IOTA_OV:C_IOTA_OV + 8], [P, 8, EXPERTS]), ALU.is_le))
                link(dve.tensor_reduce(OVX, ovc, AX, ALU.add))
                link(dve.tensor_scalar(OVX, OVX, float(EXPERTS - 1), None, ALU.min))
                dve.tensor_copy(route[:, 1:8], OVX[:, 0:7])
                dve.tensor_copy(route[:, 24:24 + NT], cs[:, C_TOKEN:C_TOKEN + NT])
                dve.tensor_copy(route[:, 0:1], CUM[:, EXPERTS - 1:EXPERTS]).then_inc(sem("route_ready"), 1)

            def moe(l):
                def take_x(b):
                    dve.wait_ge(sem(f"xb_used_{l}"), b + 1)
                    dve.wait_ge(sem(f"gu_{l}"), b * 2)
                    dve.tensor_copy(xbT[:, 4:8, :], ps[:, 3, :].rearrange("p (k s) -> p k s", k=4)).then_inc(sem(f"xbT_d_{l}"), 1)

                def hidden(b):
                    dve.wait_ge(sem(f"sig_{l}"), b + 1)
                    dve.wait_ge(sem(f"hid_tr_{l}"), b)
                    dve.tensor_tensor(hid, sig, ps[:, 0, :], ALU.mult).then_inc(sem(f"silu_{l}"), 1)
                    dve.wait_ge(sem(f"silu_{l}"), b + 1)
                    dve.wait_ge(sem(f"gu_{l}"), b * 2 + 2)
                    dve.tensor_tensor(hid, hid, ps[:, 1, :], ALU.mult).then_inc(sem(f"hid_{l}"), 1)

                take_x(0)
                hidden(0)
                take_x(1)
                with dve.Fori(0, EXPERTS // 2 - 1) as i:
                    for u in range(2):
                        hidden(i * 2 + 1 + u)
                        take_x(i * 2 + 2 + u)
                        if l == 0 and u == 0:
                            ada_block("next", ada_buf, 0, i, i + ADA_BLOCKS, i + ADA_BLOCKS)
                hidden(EXPERTS - 1)
                if l == 0:
                    ada_block("next", ada_buf, 0, ADA_BLOCKS - 1, 2 * ADA_BLOCKS - 1, 2 * ADA_BLOCKS - 1)
                dve.wait_ge(sem("route_ready"), l + 1)
                n_ov = dve.value_load(route[0:1, 0:1], min_val=0, max_val=OVERFLOW)
                with dve.If(n_ov > 0), dve.Fori(0, n_ov) as j:
                    take_x(j + EXPERTS)
                    hidden(j + EXPERTS)
                dve.wait_ge(sem("ffn_gate"), l + 1)
                for t in range(NT):
                    z0, z1 = z_in[t % 2]
                    dve.wait_ge(sem(f"z_in_{t % 2}"), 32 * (l * (NT // 2) + t // 2 + 1))
                    link(dve.tensor_scalar(z0, z0, moe_w(0)[:, t:t + 1], None, ALU.mult))
                    link(dve.scalar_tensor_tensor(out=z0, in0=z1, scalar=moe_w(1)[:, t:t + 1], in1=z0, op0=ALU.mult, op1=ALU.add))
                    link(dve.tensor_tensor(z0, z0, ffn_gate, ALU.mult))
                    dve.tensor_tensor(xs[:, t, :], xs[:, t, :], z0, ALU.add).then_inc(sem(f"x_ready_{2 * l + 2}"), 1)

            def mlstm_gates():
                dve.wait_ge(sem("ml_gate_pe"), 1)
                dve.tensor_tensor(ml_li, ps[:, 4, 0:8 * NT].rearrange("p (t g) -> p t g", t=NT),
                                  gates[:, 96:104].rearrange("p (o g) -> p o g", o=1).to_broadcast([P, NT, 8]), ALU.add)\
                   .then_inc(sem("ml_gate_dve"), 1)
                dve.wait_ge(sem("ml_gate_act"), 1)
                dve.tensor_scalar(ml_li[:, :, 0:MH], ml_li[:, :, 0:MH], SOFTCAP, None, ALU.mult)
                dve.tensor_scalar(ml_li[:, :, MH:2 * MH], ml_li[:, :, MH:2 * MH], -1.0, None, ALU.mult).then_inc(sem("ml_gate_dve"), 1)

            def mlstm_rows():
                dve.wait_ge(sem("proj1_ready"), 16)
                dve.wait_ge(sem("ml_gate_pe"), 2)

                def r(i):
                    return ml_row(i)[0:MH, :]
                link(dve.memset(r(ZERO), 0.0))
                link(dve.tensor_copy(r(LF), ps[0:MH, 5, :]))
                link(dve.tensor_tensor_scan(r(CUM_B), r(LF), r(ZERO), 0.0, ALU.add, ALU.add))
                link(dve.tensor_tensor(r(U_IN), ps[0:MH, 6, :], r(CUM_B), ALU.subtract))
                link(dve.tensor_tensor_scan(r(U_MAX), r(U_IN), r(U_IN), 0.0, ALU.max, ALU.max))
                dve.tensor_copy(ml_sel, ident[0:MH, 0:MH].rearrange("p (h o) -> p h o", o=1).to_broadcast([MH, MH, P]))
                dve.tensor_tensor(r(EXP_M), r(CUM_B), r(U_MAX), ALU.add).then_inc(sem("ml_gate_dve"), 1)

            def mlstm():
                later = cs[:, C_CAUSAL_T:C_CAUSAL_T + P].rearrange("p (o s) -> p o s", o=1).to_broadcast([P, NT, P])

                def attend(h):
                    dve.wait_ge(sem("ml_u"), h + 1)
                    if h:
                        dve.wait_ge(sem("ml_w"), NT * h)
                    dve.tensor_tensor(ml_diag.rearrange("p (t s) -> p t s", t=NT),
                                      ps[:, 6 + h % 2, :].rearrange("p (t s) -> p t s", t=NT), later, ALU.add)\
                       .then_inc(sem("ml_diag"), 1)
                    for j in range(NT):
                        n = NT * h + j
                        dve.wait_ge(sem("ml_s"), n + 1)
                        dve.wait_ge(sem("ml_w"), n + 1)
                        if n >= 2:
                            dve.wait_ge(sem("ml_num"), n - 1)
                        cols = slice(0, (NT - j) * P)
                        dve.scalar_tensor_tensor(out=ml_at(n % 2)[:, cols], in0=ps[:, 4 + n % 2, cols], scalar=DQK ** -0.5,
                                                 in1=ml_w(n % 2)[:, cols], op0=ALU.mult, op1=ALU.mult).then_inc(sem("ml_at"), 1)

                def finish(h):
                    raw = ml_raw(h % 2)
                    num, den = raw[:, :, 0:DV], raw[:, :, DV]
                    r4 = head_ss[:, 0:4]
                    dve.wait_ge(sem("ml_raw"), NT * (h + 1))
                    link(dve.scalar_tensor_tensor(out=r4, in0=den, scalar=-1.0, in1=den, op0=ALU.mult, op1=ALU.max))
                    e_m = ml_cols[:, 1, :].rearrange("p (t h) -> p t h", t=NT)[:, :, h]
                    link(dve.tensor_tensor(r4, r4, e_m, ALU.max))
                    link(dve.reciprocal(r4, r4))

                    def over(v):
                        return v.rearrange("p (t o) -> p t o", o=1).to_broadcast([P, NT, DV])
                    link(dve.tensor_tensor(num, num, over(r4), ALU.mult))
                    sq = ml_sq.rearrange("p (t d) -> p t d", t=NT)
                    link(dve.tensor_tensor(sq, num, num, ALU.mult))
                    link(dve.tensor_reduce(r4, sq, AX, ALU.add))
                    dve.tensor_scalar(head_ss[:, 4:8], r4, 1.0 / DV, EPS, ALU.mult, ALU.add).then_inc(sem("ml_hvar"), 1)
                    dve.wait_ge(sem("ml_hstd"), h + 1)
                    link(dve.reciprocal(r4, head_ss[:, 4:8]))
                    link(dve.tensor_tensor(num, num, over(r4), ALU.mult))
                    gain = area[:, M_GAIN + h * DV:M_GAIN + (h + 1) * DV].rearrange("p (o d) -> p o d", o=1).to_broadcast([P, NT, DV])
                    dve.tensor_tensor(num, num, gain, ALU.mult).then_inc(sem("ml_raw_gained"), 1)
                    dve.wait_ge(sem("ml_raw_gained"), h + 1)
                    o = hnt[:, :, h * DV:(h + 1) * DV]
                    dve.tensor_tensor(o, o, num, ALU.mult).then_inc(sem("ml_out"), 1)
                    dve.wait_ge(sem("ml_out"), h + 1)
                    dve.sem_inc(sem("ml_raw_read"), 1)

                dve.wait_ge(sem("ml_gain"), 16)
                dve.wait_ge(sem("proj1_taken"), 24)
                for h in range(MH):
                    attend(h)
                    if h:
                        finish(h - 1)
                finish(MH - 1)
                for t in range(NT):
                    dve.wait_ge(sem("mo_tr"), 2 * t + 2)
                    dve.tensor_copy(hTk[:, 4:8, t * P:(t + 1) * P], ps[:, 5 + 2 * (t % 2), :].rearrange("p (k s) -> p k s", k=4))\
                       .then_inc(sem("mo_d"), 1)

            arena_buf = arena[:, 0:KD * ADA_W].rearrange("p (k n) -> p k n", k=KD)

            def ada_pairs(first, n):
                with dve.Fori(first // 2, (first + n) // 2) as i:
                    ada_block("a", ada_buf, 0, i, i * 2, i * 2)
                    ada_block("b", arena_buf, 1, i, i * 2 + 1, i * 2)
            for which in ("a", "b", "next"):
                dve.sem_inc(sem(f"ada_read_{which}"), GRANT)
            dve.wait_ge(sem("cond_sig"), 1)
            link(dve.tensor_tensor(cond[:, KD:2 * KD], cond[:, KD:2 * KD], cond[:, 0:KD], ALU.mult))
            dve.wait_ge(sem("bias_zeroed"), 1)
            ada_pairs(0, 8)
            dve.wait_ge(sem("consts"), 16)
            norm(0)
            norm_take(0)
            ada_pairs(8, 8)
            dve.wait_ge(sem("nsa_small"), 16 * 10)
            dve.wait_ge(sem("nsa_zeroed"), 1)
            nsa_norm(0)
            for t in range(1, NT):
                nsa_take_T(t - 1)
                nsa_norm(t)
            nsa_take_T(NT - 1)
            compress()
            for t in range(NT):
                cmp_softmax(t)
            attend()
            residual(0)
            norm(1)
            norm_take(1)
            routing(0)
            moe(0)

            norm(2)
            norm_take(2)
            mlstm_gates()
            mlstm_rows()
            mlstm()
            residual(1)
            norm(3)
            norm_take(3)
            routing(1)
            moe(1)


def constants():
    import numpy as np
    cs = np.zeros((P, C_COLS), np.float32)
    p = np.arange(P)
    cs[:, C_ID:C_ID + P] = np.eye(P)
    cs[:, C_TRI:C_TRI + P] = p[:, None] < p[None, :]
    cs[:, C_CAUSAL:C_CAUSAL + P] = np.where(p[None, :] <= p[:, None], 0.0, NEG)
    cs[:, C_CAUSAL_T:C_CAUSAL_T + P] = np.where(p[None, :] < p[:, None], -NEG, 0.0)
    slot = np.arange(NC)
    slot_end = slot * CMP_STRIDE + CMP_BLOCK - 1
    inv_freq = np.float32(500000.0) ** (-np.arange(HALF, dtype=np.float32) / np.float32(HALF))

    def angles(pos):
        a = (pos.astype(np.float32)[:, None] * inv_freq[None, :]).astype(np.float32)
        return np.concatenate([np.cos(a), np.sin(a)], 1)
    for t in range(NT):
        token = t * P + p
        cs[:, C_CMASK + t * NC:C_CMASK + (t + 1) * NC] = np.where((slot_end[None, :] <= token[:, None]) & (slot < NCMP), 0.0, NEG)
        cs[:, C_ROPE + t * ROT:C_ROPE + (t + 1) * ROT] = angles(token)
        cs[:, C_ROWOK + t] = token >= CMP_BLOCK - 1
        cs[:, C_TOKEN + t] = token
    cs[0:2 * NC, C_CROPE:C_CROPE + ROT] = angles(np.tile(slot_end, 2))
    cs[:, C_IOTA_E:C_IOTA_E + EXPERTS] = np.arange(EXPERTS)
    cs[:, C_IOTA_8:C_IOTA_8 + EXPERTS] = np.arange(EXPERTS) % EPG - EPG
    cs[:, C_IOTA_4:C_IOTA_4 + EGROUPS] = np.arange(EGROUPS) - EGROUPS
    cs[:, C_IOTA_OV:C_IOTA_OV + 8] = np.arange(8)
    return cs, np.full((SLOTS * NB, 1), NOBODY, np.int32)


_INS = ["x", "c", "ada_w", "ada_b", "norm_mix_gain", "norm_ffn_gain",
        "nsa_w_in", "nsa_w_out", "nsa_q_gain", "nsa_k_gain", "nsa_cmp_pe", "nsa_cmp_w1", "nsa_cmp_b1", "nsa_cmp_w2",
        "nsa_cmp_b2", "mlstm_w_in", "mlstm_b_igate", "mlstm_b_fgate", "mlstm_norm_gain", "mlstm_w_out",
        "router_w", "router_b", "moe_w_gate", "moe_w_up", "moe_w_down"]


def kernel(**inputs):
    import numpy as np
    import concourse.bacc as bacc
    from concourse.bass_utils import run_bass_kernel_spmd

    nc = bacc.Bacc("TRN2", target_bir_lowering=False, num_devices=1)
    host = {f"in_{name}": np.ascontiguousarray(inputs[name]) for name in _INS}
    host["in_consts"], host["in_empty_slots"] = constants()
    args = [nc.dram_tensor(name, a.shape, mybir.dt.from_np(a.dtype), kind="ExternalInput").ap() for name, a in host.items()]
    result = nc.dram_tensor("out_0", (1, SEQ, D), F32, kind="ExternalOutput").ap()
    build_trunk(nc, *args, result)
    run = run_bass_kernel_spmd(nc, [host], core_ids=[0])
    return run.results[0]["out_0"]
```

```python
from contextlib import ExitStack

import concourse.bass as bass
from concourse import mybir

F32 = mybir.dt.float32
I32 = mybir.dt.int32
ALU = mybir.AluOpType
ACT = mybir.ActivationFunctionType
AX = mybir.AxisListType.X

P = 128
SEQ, D = 512, 1024
NT, KD = SEQ // P, D // P
LAYERS = 2
EPS = 1e-6
NEG = -1e30

HEADS, GROUPS, DH = 16, 2, 64
PAIRS = HEADS // 2
ROT = DH // 4
HALF = ROT // 2
CMP_BLOCK, CMP_STRIDE, CMP_HIDDEN = 32, 16, 256
NCMP = (SEQ - CMP_BLOCK) // CMP_STRIDE + 1
NC = 32
CMP_CHUNKS = CMP_BLOCK * DH // P
SEL_BLOCK, SEL_TOPN, WINDOW = 64, 8, 512
assert SEQ // SEL_BLOCK <= SEL_TOPN and WINDOW >= SEQ and NCMP < NC
NSA_COLS = HEADS * DH + 6 * GROUPS * DH + 3 * HEADS
SCALE = DH ** -0.5

MH, DQK, DV = 4, 128, 256
SOFTCAP = 15.0
ML_COLS = 2 * MH * DQK + 2 * MH * DV + 2 * MH

EXPERTS, EGROUPS, EPG, DE = 32, 4, 8, 512
SLOTS = 128
OVERFLOW = 7
NB = EXPERTS + OVERFLOW + 1
NOBODY = SEQ

ADA_COLS = 6 * D
ADA_BLOCKS, ADA_W = 16, 384
assert ADA_BLOCKS * ADA_W == ADA_COLS
SH_M, SC_M, G_M, SH_F, SC_F, G_F = (D * i for i in range(6))

GRANT = 1
TAKE_LAG = 3

C_ID, C_TRI, C_CAUSAL, C_CAUSAL_T, C_CMASK = 0, 128, 256, 384, 512
C_ROPE = 640
C_CROPE = C_ROPE + NT * ROT
C_ROWOK = C_CROPE + ROT
C_IOTA_E = C_ROWOK + NT
C_IOTA_8 = C_IOTA_E + EXPERTS
C_IOTA_4 = C_IOTA_8 + EXPERTS
C_TOKEN = C_IOTA_4 + EGROUPS
C_IOTA_OV = C_TOKEN + NT
C_ZERO = C_IOTA_OV + 8
C_COLS = C_ZERO + EXPERTS

AREA = 24576
SLOT = AREA // 2
UP, DOWN = KD * DE, 2 * KD * DE
A_PROB, A_PROBT = 8192, 8192 + 2048
A_KTZ = KD * NSA_COLS
A_KC = A_KTZ + 8 * SEQ
KC_ROW = 530
A_V = A_KC + 4 * KC_ROW
A_VCBD = A_V + NT * 2 * P
A_KCTZ = A_VCBD + 2 * 256
A_HGAIN = A_KCTZ + P
A_PE = A_HGAIN + 4 * DH
A_B1 = A_PE + 2 * CMP_CHUNKS
A_B2 = A_B1 + 2 * CMP_HIDDEN
A_W2 = A_B2 + 2 * DH
A_SMALL = A_W2 + 4 * DH
A_CBLK = A_SMALL + 500
assert A_KC >= SLOT and A_CBLK <= AREA

HIDDEN, HIDDEN_T, CMP_OUT, KEY_T = 2, 3, 4, 5
CMP_VALUES, KEY_STD = 4, 5
KEY_VAR, KEY_ROW, KEY_COLUMNS = 3, 4, 5

M_QK, M_V, M_O = 0, 8192, 16384
VROW = DV + 1
M_VALS = 0
M_ROWS = M_V
M_GAIN = M_ROWS + 7 * SEQ
M_DIAG = M_GAIN + D
M_W = M_DIAG + SEQ
M_AT = M_W + 2 * SEQ
M_SQ = M_AT + 2 * SEQ
assert M_VALS + NT * MH * VROW <= M_V and M_SQ + DV <= M_O

LF, CUM_B, U_IN, U_MAX, EXP_M, ZERO = range(6)

R_W, R_B = 0, KD * EXPERTS
R_AFF, R_CH, R_EQ, R_MSK, R_E1, R_E2, R_SUM, R_BLK, R_SLOT, R_F, R_TMP = (288 + 128 * i for i in range(11))
R_S = 288 + 128 * 11
R_GATE = 2304
R_SLOTS = R_GATE + D


def build_trunk(nc, x, c, ada_w, ada_b, norm_mix_gain, norm_ffn_gain,
                nsa_w_in, nsa_w_out, nsa_q_gain, nsa_k_gain, nsa_cmp_pe, nsa_cmp_w1, nsa_cmp_b1, nsa_cmp_w2, nsa_cmp_b2,
                mlstm_w_in, mlstm_b_igate, mlstm_b_fgate, mlstm_norm_gain, mlstm_w_out,
                router_w, router_b, moe_w_gate, moe_w_up, moe_w_down, consts, slot_index, out):
    x_d = x.rearrange("b (t p) d -> p (b t) d", p=P)
    out_d = out.rearrange("b (t p) d -> p (b t) d", p=P)
    gate_rows = moe_w_gate.rearrange("l e (k p) f -> p (l e) k f", p=P)
    up_rows = moe_w_up.rearrange("l e (k p) f -> p (l e) k f", p=P)
    down_rows = moe_w_down.rearrange("l e (k p) n -> p (l e) k n", p=P)
    ada_rows = ada_w.rearrange("l (p k) n -> l p k n", k=KD)
    mlstm_rows = mlstm_w_in[0].rearrange("(k p) n -> p k n", p=P)

    with ExitStack() as ctx:
        def sb(name, shape, dt=F32):
            return ctx.enter_context(nc.sbuf_tensor(name, shape, dt))

        hf_dram = [nc.dram_tensor(f"hf_{l}", (SEQ, D), F32).ap() for l in range(LAYERS)]
        z_dram = [nc.dram_tensor(f"z_{l}", (2 * SEQ, D), F32).ap() for l in range(LAYERS)]

        xs = sb("xs", [P, NT, D])
        hn = sb("hn", [P, NT * D])
        hT = sb("hT", [P, KD * SEQ])
        area = sb("area", [P, AREA])
        mods = sb("mods", [P, ADA_COLS])
        ada_buf = sb("ada_buf", [P, KD, ADA_W])
        ada_acc = sb("ada_acc", [P, 2, ADA_W])
        ada_bias = sb("ada_bias", [P, 2, ADA_W])
        arena = sb("arena", [P, 4096])
        cs = sb("cs", [P, C_COLS])
        ones = sb("ones", [P, P])
        cond = sb("cond", [P, 2 * KD])
        small = sb("small", [P, 105])
        gates = sb("gates", [P, NT * 3 * HEADS])
        slot_tok = sb("slot_tok", [P, NB], I32)
        slot_row = sb("slot_row", [P, NB], I32)
        slot_cur = sb("slot_cur", [P, 2], I32)
        row_cur = sb("row_cur", [P, 2], I32)
        route = sb("route", [P, 8], I32)

        ps = ctx.enter_context(nc.psum_tensor("ps", [P, 8, 512], F32))

        sems = {}

        def sem(name):
            if name not in sems:
                sems[name] = ctx.enter_context(nc.semaphore(name))
            return sems[name]

        ident = cs[:, C_ID:C_ID + P]
        hnt = hn[:, :].rearrange("p (t d) -> p t d", t=NT)
        hTk = hT[:, :].rearrange("p (k s) -> p k s", k=KD)
        gain_tile = [hT[:, 0:D]] + 3 * [ada_buf[:, :, :].rearrange("p k n -> p (k n)")[:, 0:D]]
        ssq, rstd, eps = small[:, 0:4], small[:, 4:8], small[:, 104:105]

        w_in0 = area[:, 0:A_KTZ].rearrange("p (k n) -> p k n", k=KD)
        w1 = area[:, 0:2 * CMP_CHUNKS * CMP_HIDDEN].rearrange("p (a m n) -> p a m n", a=2, m=CMP_CHUNKS)
        w_out = [area[:, lo:lo + KD * D].rearrange("p (k n) -> p k n", k=KD) for lo in (0, M_O)]
        prob = [area[:, lo:lo + 1024] for lo in (A_PROB, A_PROB + 1024)] + [hn[:, 0:1024]]
        prob = [v.rearrange("p (b s) -> p b s", b=2) for v in prob]
        probT = area[:, A_PROBT:A_PROBT + 2048].rearrange("p (u b s) -> p u b s", u=2, b=2)
        ktz = area[:, A_KTZ:A_KC].rearrange("p (b g r s) -> p b g r s", b=2, g=2, r=2)
        kcvT = area[:, A_KC:A_V].rearrange("p (a g s) -> p a g s", a=2, g=2)
        vals = area[:, A_V:A_VCBD].rearrange("p (t b n) -> p t b n", t=NT, b=2)
        vcbd = area[:, A_VCBD:A_KCTZ].rearrange("p (g n) -> p g n", g=2)
        kctz = area[:, A_KCTZ:A_HGAIN].rearrange("p (r n) -> p r n", r=2)
        hgain = area[:, A_HGAIN:A_PE]
        pe_t = area[:, A_PE:A_B1].rearrange("p (a m) -> p a m", a=2)
        b1_row, b2_row = area[0:1, A_B1:A_B2], area[0:1, A_B2:A_W2]
        w2 = area[:, A_W2:A_SMALL].rearrange("p (a m n) -> p a m n", a=2, m=2)
        qT = arena[:, :].rearrange("p (r s) -> p r s", r=PAIRS)
        nrm = [hn[:, 2048 * u:2048 * u + 20 * DH] for u in range(2)]
        kcv = [hn[:, 2048 * u + 1280:2048 * u + 1536] for u in range(2)]
        rope_tmp = [area[:, A_SMALL + 160 * i:A_SMALL + 160 * i + 160] for i in range(3)]
        head_ss = small[:, 12:24]
        blk = hn[:, 0:2048].rearrange("p (a m c) -> p a m c", a=2, m=CMP_CHUNKS)
        hid_c = hn[0:64, 2048:2560].rearrange("p (a n) -> p a n", a=2)
        hidT_c = hn[:, 2560:2816].rearrange("p (q c) -> p q c", q=4)
        kcn, ksq = hn[0:64, 2816:2944], hn[0:64, 2944:3008]
        pc = hn[:, 0:2048].rearrange("p (t n) -> p t n", t=NT)
        pcT = hn[:, 2048:4096].rearrange("p (t q n) -> p t q n", t=NT, q=4)

        def head_rstd(u):
            return small[:, 24 + 20 * u:44 + 20 * u]

        def neg_max(u):
            return small[:, 64 + 2 * u:66 + 2 * u]

        def raw_max(u):
            return small[:, 68 + 2 * u:70 + 2 * u]

        def sum_l(u):
            return small[:, 72 + 2 * u:74 + 2 * u]

        def inv_l(u):
            return small[:, 76 + 2 * u:78 + 2 * u]

        cmp_r = small[:, 80:96]

        def moe_w(k):
            return small[:, 96 + 4 * k:100 + 4 * k]

        ml_vals = area[:, M_VALS:M_VALS + NT * MH * VROW].rearrange("p (t h d) -> p t h d", t=NT, h=MH)
        ml_sel = area[0:MH, M_ROWS + 6 * SEQ:M_ROWS + 7 * SEQ].rearrange("p (h s) -> p h s", h=MH)
        ml_diag = area[:, M_DIAG:M_DIAG + SEQ]
        ml_sq = area[:, M_SQ:M_SQ + DV]
        ml_li = gates[:, 104:136].rearrange("p (t g) -> p t g", t=NT)
        ml_cols = gates[:, 136:168].rearrange("p (a n) -> p a n", a=2)

        ml_den, ml_scale, ml_ssq = small[:, 24:40], small[:, 44:60], small[:, 80:96]

        def ml_row(i):
            return area[:, M_ROWS + i * SEQ:M_ROWS + (i + 1) * SEQ]

        def ml_w(u):
            return area[:, M_W + u * SEQ:M_W + (u + 1) * SEQ]

        def ml_at(u):
            return area[:, M_AT + u * SEQ:M_AT + (u + 1) * SEQ]

        xb = [hn[:, D * u:D * u + D] for u in range(2)]
        zb = [hn[:, 2 * D + D * u:2 * D + D * u + D] for u in range(2)]
        z_in = [[v[:, D * (2 * u + k):D * (2 * u + k) + D] for k in range(2)] for v in (hn, area[:, DOWN:SLOT]) for u in range(2)]
        xbT = hT[:, 0:D].rearrange("p (k s) -> p k s", k=KD)
        hid, sig, hidT = hT[:, 1024:1536], hT[:, 1536:2048], hT[:, 2048:2560].rearrange("p (k s) -> p k s", k=4)
        ffn_gate = arena[:, R_GATE:R_GATE + D]
        n_hot = 2 * NT
        slot_hot, block_hot, block_val = (hT[:, n_hot * lo:n_hot * hi] for lo, hi in (
            (0, SLOTS), (SLOTS, SLOTS + NB), (SLOTS + NB, SLOTS + 3 * NB)))

        def w_gu(u, m):
            return area[:, u * SLOT + m * UP:u * SLOT + m * UP + UP].rearrange("p (k n) -> p k n", k=KD)

        def w_dn(u):
            return area[:, u * SLOT + DOWN:u * SLOT + DOWN + UP].rearrange("p (k n) -> p k n", k=DE // P)

        block = ctx.enter_context(nc.Block())

        @block.sync
        def _(sp):
            def ada_load(layer, buf, b_expr, which, used):
                cols = bass.ds(b_expr * ADA_W, ADA_W)
                sp.wait_ge(sem(f"ada_read_{which}"), used + GRANT)
                u = 1 if which == "b" else 0
                sp.dma_start(buf, ada_rows[layer, :, :, cols]).then_inc(sem(f"ada_loaded_{which}"), 16)
                sp.dma_start(ada_bias[0:1, u, :], ada_b[layer:layer + 1, cols]).then_inc(sem(f"ada_loaded_{which}"), 16)

            def ada_pairs(first, n):
                with sp.Fori(first // 2, (first + n) // 2) as i:
                    ada_load(0, ada_buf[:, :, :], i * 2, "a", i)
                    ada_load(0, arena[:, 0:KD * ADA_W].rearrange("p (k n) -> p k n", k=KD), i * 2 + 1, "b", i)

            def expert_load(l, e_expr, u, before):
                row = bass.ds(e_expr + l * EXPERTS, 1)
                parts = [area[:, u * SLOT + lo:u * SLOT + lo + UP].rearrange("p (e k n) -> p e k n", e=1, k=k)
                         for lo, k in ((0, KD), (UP, KD), (DOWN, DE // P))]
                sp.wait_ge(sem(f"gu_{l}"), before * 2)
                sp.dma_start(parts[0], gate_rows[:, row, :, :]).then_inc(sem(f"wgu_{l}_{u}"), 16)
                sp.dma_start(parts[1], up_rows[:, row, :, :]).then_inc(sem(f"wgu_{l}_{u}"), 16)
                sp.wait_ge(sem(f"y_{l}"), before)
                sp.dma_start(parts[2], down_rows[:, row, :, :]).then_inc(sem(f"wd_{l}_{u}"), 16)

            def moe_loads(l):
                sp.wait_ge(sem("w_out_used"), NT * (l + 1))
                sp.dma_start(arena[:, R_W:R_B].rearrange("p (k e) -> p k e", k=KD),
                             router_w.rearrange("(k p) e -> p k e", p=P)).then_inc(sem("router_w"), 16)
                sp.dma_start(arena[:, R_B:R_B + EXPERTS],
                             router_b.rearrange("(o e) -> o e", o=1).to_broadcast([P, EXPERTS])).then_inc(sem("router_w"), 16)
                sp.dma_start(arena[:, R_SLOTS:R_SLOTS + SLOTS], slot_index.to_broadcast([P, SLOTS])).then_inc(sem("router_w"), 16)
                for t in range(NT):
                    sp.wait_ge(sem("hn_ready"), NT * (2 * l + 1) + t + 1)
                    sp.dma_start(hf_dram[l][t * P:(t + 1) * P, :], hnt[:, t, :]).then_inc(sem("hf_stored"), 16)
                expert_load(l, 0, 0, 0)
                expert_load(l, 1, 1, 0)
                if l == 0:
                    sp.wait_ge(sem("ffn_gate"), 1)
                with sp.Fori(1, EXPERTS // 2) as i:
                    if l == 0:
                        ada_load(1, ada_buf[:, :, :], i - 1, "next", i - 1)
                    for u in range(2):
                        expert_load(l, i * 2 + u, u, i * 2 + (u - 1))
                if l == 0:
                    ada_load(1, ada_buf[:, :, :], ADA_BLOCKS - 1, "next", ADA_BLOCKS - 1)
                    sp.wait_ge(sem("y_0"), EXPERTS - 1)
                    sp.dma_start(area[:, M_QK:M_V].rearrange("p (k n) -> p k n", k=KD), mlstm_rows[:, :, 0:qk]).then_inc(sem("w_qk"), 16)
                    sp.wait_ge(sem("ada_read_next"), ADA_BLOCKS + GRANT)
                    sp.dma_start(gain_tile[2], norm_mix_gain[1:2, :].to_broadcast([P, D])).then_inc(sem("norm_gain"), 16)
                sp.wait_ge(sem("route_ready"), l + 1)
                n_ov = sp.value_load(route[0:1, 0:1], min_val=0, max_val=OVERFLOW)
                with sp.If(n_ov > 0), sp.Fori(0, n_ov) as j:
                    e = sp.value_load(route[0:1, bass.ds(j + 1, 1)], min_val=0, max_val=EXPERTS - 1)
                    expert_load(l, e, 1, j + EXPERTS)
                sp.wait_ge(sem(f"y_{l}"), n_ov + EXPERTS)
                sp.wait_ge(sem("z_whole"), l + 1)
                rows = z_dram[l].rearrange("(k t p) d -> p k t d", k=2, p=P)
                for t in range(NT):
                    for k in range(2):
                        sp.dma_start(z_in[t][k], rows[:, k, t, :]).then_inc(sem(f"z_in_{t}"), 16)

            qk, vo = 2 * MH * DQK, MH * DV

            sp.dma_start(cond[:, 0:KD], c.rearrange("b (p k) -> p (b k)", k=KD)).then_inc(sem("c_loaded"), 16)
            sp.dma_start(cs[:, :], consts).then_inc(sem("consts"), 16)
            sp.wait_ge(sem("bias_zeroed"), 1)
            ada_pairs(0, 8)
            sp.dma_start(xs[:, :, :], x_d).then_inc(sem("x_ready_0"), 16)
            sp.dma_start(gain_tile[0], norm_mix_gain[0:1, :].to_broadcast([P, D])).then_inc(sem("norm_gain"), 16)
            w_rows = nsa_w_in[0].rearrange("(k p) n -> p k n", p=P)
            for h in range(2):
                sp.dma_start(w_in0[:, 4 * h:4 * h + 4, :], w_rows[:, 4 * h:4 * h + 4, :]).then_inc(sem("w_in_0"), 16)
            for g, src in enumerate((nsa_q_gain[0:1, :], nsa_k_gain[0, 1:2, :], nsa_k_gain[0, 2:3, :], nsa_k_gain[0, 0:1, :])):
                sp.dma_start(hgain[:, g * DH:g * DH + DH], src.to_broadcast([P, DH])).then_inc(sem("nsa_small"), 16)
            with nc.allow_non_contiguous_dma(reason="4096 position embeddings, once"):
                for a in range(2):
                    sp.dma_start(pe_t[:, a, :], nsa_cmp_pe[0, a].rearrange("(m r) d -> (r d) m", r=2))\
                      .then_inc(sem("nsa_small"), 16)
            sp.dma_start(b1_row, nsa_cmp_b1.rearrange("o a n -> o (a n)")).then_inc(sem("nsa_small"), 16)
            sp.dma_start(b2_row, nsa_cmp_b2.rearrange("o a n -> o (a n)")).then_inc(sem("nsa_small"), 16)
            for a in range(2):
                sp.dma_start(w2[:, a, :, :], nsa_cmp_w2[0, a].rearrange("(m p) n -> p m n", p=P)).then_inc(sem("nsa_small"), 16)
            ada_pairs(8, 8)
            sp.wait_ge(sem("ada_read_a"), ADA_BLOCKS // 2 + GRANT)
            sp.dma_start(gain_tile[1], norm_ffn_gain[0:1, :].to_broadcast([P, D])).then_inc(sem("norm_gain"), 16)
            sp.wait_ge(sem("proj0_ready"), 4 * NT)
            for a in range(2):
                sp.dma_start(w1[:, a, :, :], nsa_cmp_w1[0, a].rearrange("(m p) n -> p m n", p=P)).then_inc(sem("w1"), 16)
            sp.wait_ge(sem("cmp_pe"), HIDDEN)
            sp.dma_start(w_out[0], nsa_w_out[0].rearrange("(k p) n -> p k n", p=P)).then_inc(sem("w_out_loaded"), 16)
            moe_loads(0)

            sp.dma_start(gates[:, 0:64].rearrange("p (k n) -> p k n", k=KD), mlstm_rows[:, :, qk + 2 * vo:]).then_inc(sem("w_gates"), 16)
            sp.dma_start(gates[:, 96:100], mlstm_b_igate.to_broadcast([P, MH])).then_inc(sem("w_gates"), 16)
            sp.dma_start(gates[:, 100:104], mlstm_b_fgate.to_broadcast([P, MH])).then_inc(sem("w_gates"), 16)
            for t in range(NT):
                sp.wait_ge(sem(f"z_in_{t}"), 32)
            sp.dma_start(area[:, M_O:AREA].rearrange("p (k n) -> p k n", k=KD), mlstm_rows[:, :, qk + vo:qk + 2 * vo])\
              .then_inc(sem("w_o"), 16)
            sp.wait_ge(sem("x_ready_2"), NT)
            sp.dma_start(area[:, M_V:M_O].rearrange("p (k n) -> p k n", k=KD), mlstm_rows[:, :, qk:qk + vo]).then_inc(sem("w_v"), 16)
            sp.wait_ge(sem("hn_ready"), 3 * NT)
            sp.dma_start(gain_tile[3], norm_ffn_gain[1:2, :].to_broadcast([P, D])).then_inc(sem("norm_gain"), 16)
            sp.wait_ge(sem("proj1_ready"), 16)
            sp.dma_start(area[:, M_GAIN:M_GAIN + D],
                         mlstm_norm_gain.rearrange("o h d -> o (h d)").to_broadcast([P, D])).then_inc(sem("ml_gain"), 16)
            sp.wait_ge(sem("proj1_ready"), 24)
            sp.dma_start(w_out[1], mlstm_w_out[0].rearrange("(k p) n -> p k n", p=P)).then_inc(sem("w_out_loaded"), 16)
            moe_loads(1)

            for t in range(NT):
                sp.wait_ge(sem("x_ready_4"), t + 1)
                sp.dma_start(out_d[:, t, :], xs[:, t, :]).then_inc(sem("out_stored"), 16)
            sp.wait_ge(sem("out_stored"), 16 * NT)

        @block.gpsimd
        def _(pool):
            last_row = pool.to_reg(SEQ - 1)
            last_z = pool.to_reg(2 * SEQ - 1)
            pool.memset(ada_bias[:, :, :], 0.0).then_inc(sem("bias_zeroed"), 1)
            pool.memset(eps, EPS)
            pool.memset(ones[:, :], 1.0).then_inc(sem("ones"), 1)
            pool.memset(area[:, A_KTZ:A_HGAIN], 0.0).then_inc(sem("nsa_zeroed"), 1)

            def settled():
                pool.sem_inc(sem("pool_settled"), 1)

            def norm_shift(n):
                shift = SH_F if n % 2 else SH_M
                for t in range(NT):
                    pool.wait_ge(sem("hn_scaled"), NT * n + t + 1)
                    pool.tensor_tensor(hnt[:, t, :], hnt[:, t, :], mods[:, shift:shift + D], ALU.add)\
                        .then_inc(sem("hn_ready"), 1)

            def gather(l, b_expr, u, transposed):
                src = slot_tok[:, bass.ds(b_expr, 1)]
                pool.wait_ge(sem(f"xb_used_{l}"), transposed)
                pool.tensor_copy(slot_cur[:, u:u + 1], src).then_inc(sem(f"slot_cur_{l}_{u}"), 1)

            def gather_go(l, u, nth, s=None):
                pool.wait_ge(sem(f"slot_cur_{l}_{u}"), nth)
                settled()
                pool.indirect_dma_start(xb[u], None, hf_dram[l], bass.IndirectOffsetOnAxis(ap=slot_cur[:, u:u + 1], axis=0),
                                        bounds_check=last_row, oob_is_err=False).then_inc(sem(s or f"xb_{l}_{u}"), 16)

            def store(l, b_expr, u, stored=None):
                pool.wait_ge(sem(f"zb_{l}"), b_expr + 1 + GRANT)
                pool.tensor_copy(row_cur[:, u:u + 1], slot_row[:, bass.ds(b_expr, 1)]).then_inc(sem(f"row_cur_{l}"), 1)
                pool.wait_ge(sem(f"row_cur_{l}"), b_expr + 1)
                settled()
                pool.indirect_dma_start(z_dram[l], bass.IndirectOffsetOnAxis(ap=row_cur[:, u:u + 1], axis=0), zb[u], None,
                                        bounds_check=last_z, oob_is_err=False).then_inc(sem(stored or f"z_stored_{l}_{u}"), 16)

            def moe_pool(l):
                pool.wait_ge(sem("slots_ready"), l + 1)
                pool.wait_ge(sem("hf_stored"), 16 * NT * (l + 1))
                for b in range(4):
                    gather(l, b, b % 2, max(b - 1, 0))
                    gather_go(l, b % 2, b // 2 + 1)
                with pool.Fori(2, EXPERTS // 2) as i:
                    for u in range(2):
                        gather(l, i * 2 + u, u, i * 2 + u - 1)
                        gather_go(l, u, i + 1)
                        store(l, i * 2 + u - 4, u)
                for b in range(EXPERTS - 4, EXPERTS):
                    store(l, b, b % 2)
                pool.wait_ge(sem("route_ready"), l + 1)
                n_ov = pool.value_load(route[0:1, 0:1], min_val=0, max_val=OVERFLOW)
                with pool.If(n_ov > 0), pool.Fori(0, n_ov) as j:
                    gather(l, j + EXPERTS, 0, j + EXPERTS)
                    gather_go(l, 0, j + EXPERTS // 2 + 1)
                    store(l, j + EXPERTS, 0, stored=f"z_stored_{l}_ov")
                    pool.wait_ge(sem(f"z_stored_{l}_ov"), j * 16 + 16)
                    settled()
                for u in range(2):
                    pool.wait_ge(sem(f"z_stored_{l}_{u}"), 16 * (EXPERTS // 2))
                pool.sem_inc(sem("z_whole"), 1)

            norm_shift(0)
            unit = 0
            for t in range(NT):
                for h in range(HEADS):
                    pool.wait_ge(sem("prob_scale"), unit + 1)
                    p0 = prob[unit % 3][:, 0, 0:(t + 1) * P]
                    pool.tensor_scalar(p0, p0, inv_l(unit % 2)[:, 0:1], None, ALU.mult).then_inc(sem("prob_ready_p"), 1)
                    unit += 1
            norm_shift(1)
            moe_pool(0)
            norm_shift(2)
            pool.wait_ge(sem("proj1_ready"), 8)
            pool.memset(ml_vals[:, :, :, DV:VROW], 1.0).then_inc(sem("ml_ones"), 1)
            pool.wait_ge(sem("ml_gain"), 16)
            for t in range(NT):
                pool.wait_ge(sem("proj1_taken"), 16 + 2 * t + 2)
                pool.tensor_tensor(hnt[:, t, :], hnt[:, t, :], area[:, M_GAIN:M_GAIN + D], ALU.mult).then_inc(sem("ml_o_gained"), 1)
            norm_shift(3)
            moe_pool(1)

        @block.tensor
        def _(pe):
            def ada_sum(u, b):
                pe.wait_ge(sem("ada_acc"), b + 1)
                pe.wait_ge(sem("ada_mods"), b + GRANT)
                pe.matmul(ps[:, 7, 0:ADA_W], ones[:, :], ada_acc[:, u, :], start=True, stop=True).then_inc(sem("ada_summed"), 1)

            def norm_transposes(n):
                l = n // 2
                if n % 2:
                    pe.wait_ge(sem("router_w"), 48 * (l + 1))
                for t in range(NT + 1):
                    if t < NT:
                        pe.wait_ge(sem("hn_ready"), NT * n + t + 1)
                        if n % 2 and t < 2:
                            pe.wait_ge(sem("y_taken"), 2 * (NT * l + t + 3))
                        for half in range(2):
                            if t >= 2:
                                pe.wait_ge(sem(f"hT_{'ad'[half]}"), NT * n + t - 1)
                            for k in range(4):
                                ins = pe.transpose(ps[:, (t % 2) * 2 + half, k * P:(k + 1) * P],
                                                   hnt[:, t, (4 * half + k) * P:(4 * half + k + 1) * P], ident)
                            ins.then_inc(sem("hT_tr"), 1)
                    if t:
                        pe.wait_ge(sem("hT_a"), NT * n + t)
                        pe.wait_ge(sem("hT_d"), NT * n + t)
                        if n % 2:
                            router(t - 1)

            def router(t):
                for k in range(KD):
                    ins = pe.matmul(ps[:, 6, t * EXPERTS:(t + 1) * EXPERTS], hTk[:, k, t * P:(t + 1) * P],
                                    arena[:, R_W + k * EXPERTS:R_W + (k + 1) * EXPERTS], start=(k == 0), stop=(k == KD - 1))
                if t == NT - 1:
                    ins.then_inc(sem("logits"), 1)

            def nsa_project(t, g):
                cols = slice(512 * g, min(512 * g + 512, NSA_COLS))
                if t:
                    pe.wait_ge(sem("proj0_taken"), 4 * (t - 1) + g + 1)
                for k in range(KD):
                    ins = pe.matmul(ps[:, g, 0:cols.stop - cols.start], hTk[:, k, t * P:(t + 1) * P], w_in0[:, k, cols],
                                    start=(k == 0), stop=(k == KD - 1))
                ins.then_inc(sem("proj0_ready"), 1)

            def nsa_transposes(t):
                pe.wait_ge(sem("nrm_ready"), t + 1)
                pe.wait_ge(sem("ada_mods"), ADA_BLOCKS + GRANT)
                if t:
                    pe.wait_ge(sem("qT_a"), t)
                    pe.wait_ge(sem("qT_d"), t)
                for pr in range(PAIRS):
                    pe.transpose(ps[:, 4 + pr // 4, (pr % 4) * P:(pr % 4 + 1) * P], nrm[t % 2][:, pr * P:(pr + 1) * P], ident)
                for b in range(2):
                    pe.transpose(ps[:, 6, b * P:(b + 1) * P], nrm[t % 2][:, 1024 + b * P:1024 + (b + 1) * P], ident)
                for a in range(2):
                    ins = pe.transpose(ps[:, 7, a * P:(a + 1) * P], kcv[t % 2][:, a * P:(a + 1) * P], ident)
                ins.then_inc(sem("nsa_tr"), 1)

            def compress():
                pe.wait_ge(sem("w1"), 32)
                pe.wait_ge(sem("nsa_small"), 16 * 10)
                for a in range(2):
                    pe.wait_ge(sem("cmp_dve"), a + 1)
                    for m in range(CMP_CHUNKS):
                        pe.matmul(ps[0:64, a, 0:CMP_HIDDEN], blk[:, a, m, :], w1[:, a, m, :], start=(m == 0), stop=False)
                    pe.matmul(ps[0:64, a, 0:CMP_HIDDEN], ones[0:1, 0:64], b1_row[:, a * CMP_HIDDEN:(a + 1) * CMP_HIDDEN],
                              start=False, stop=True).then_inc(sem("cmp_pe"), 1)
                for a in range(2):
                    pe.wait_ge(sem("cmp_act"), a + 1)
                    for m in range(2):
                        ins = pe.transpose(ps[:, 2, (2 * a + m) * 64:(2 * a + m + 1) * 64], hid_c[:, a, m * P:(m + 1) * P],
                                           ident[0:64, 0:64])
                ins.then_inc(sem("cmp_pe"), 1)
                pe.wait_ge(sem("cmp_act"), HIDDEN_T)
                for a in range(2):
                    for m in range(2):
                        pe.matmul(ps[0:64, 3 + a, 0:DH], hidT_c[:, 2 * a + m, :], w2[:, a, m, :],
                                  start=(m == 0), stop=False)
                    ins = pe.matmul(ps[0:64, 3 + a, 0:DH], ones[0:1, 0:64], b2_row[:, a * DH:(a + 1) * DH],
                                    start=False, stop=True)
                ins.then_inc(sem("cmp_pe"), 1)
                pe.wait_ge(sem("cmp_dve"), KEY_ROW)
                pe.transpose(ps[:, 0, 0:64], kcn, ident[0:64, 0:64]).then_inc(sem("cmp_pe"), 1)
                pe.wait_ge(sem("cmp_dve"), KEY_COLUMNS)

            def cmp_scores(t):
                if t >= 2:
                    pe.wait_ge(sem("cmp_s_read"), t - 1)
                for pr in range(PAIRS):
                    g = pr // (PAIRS // 2)
                    ins = pe.matmul(ps[:, 1 + t % 2, pr * 64:(pr + 1) * 64].rearrange("p (r c) -> p r c", r=2),
                                    qT[:, pr, t * P:(t + 1) * P],
                                    kctz[:, :, g * NC:(g + 1) * NC], start=True, stop=True)
                ins.then_inc(sem("cmp_s"), 1)

            def cmp_transposes(t):
                pe.wait_ge(sem("pc_ready"), t + 1)
                if t >= 2:
                    pe.wait_ge(sem("pcT_ready"), t - 1)
                for q in range(4):
                    ins = pe.transpose(ps[:, 4 + t % 2, q * P:(q + 1) * P], pc[:, t, q * P:(q + 1) * P], ident)
                ins.then_inc(sem("pc_tr"), 1)

            units = [(t, h) for t in range(NT) for h in range(HEADS)]

            def scores(n):
                t, h = units[n]
                if n >= 2:
                    pe.wait_ge(sem("exp_done"), n - 1)
                for b in range(2):
                    ins = pe.matmul(ps[:, 2 * (n % 2) + b, 0:(t + 1) * P], qT[:, h // 2, t * P:(t + 1) * P],
                                    ktz[:, b, h // 8, h % 2, 0:(t + 1) * P], start=True, stop=True)
                ins.then_inc(sem("scores"), 1)

            def prob_transposes(n):
                t, h = units[n]
                for b in range(2):
                    pe.wait_ge(sem(f"prob_ready_{'pd'[b]}"), n + 1)
                    if n:
                        pe.wait_ge(sem(f"probT_{'ad'[b]}"), n)
                    for j in range(t + 1):
                        ins = pe.transpose(ps[:, 4 + b, j * P:(j + 1) * P], prob[n % 3][:, b, j * P:(j + 1) * P], ident)
                ins.then_inc(sem("prob_tr"), 1)

            def weighted_values(n):
                t, h = units[n]
                pr, r = n // 2, h % 2
                bank = 6 + pr % 2
                for b in range(2):
                    pe.wait_ge(sem(f"probT_{'ad'[b]}"), n + 1)
                if r == 0:
                    if pr >= 2:
                        pe.wait_ge(sem("oT_ready"), pr - 1)
                    quad, half = h // 4, (h // 2) % 2
                    pe.matmul(ps[:, bank, 0:P], vcbd[:, h // 8, half * P:(half + 1) * P], pcT[:, t, quad, :],
                              start=True, stop=False, skip_group_check=True)
                for b in range(2):
                    for j in range(t + 1):
                        ins = pe.matmul(ps[r * 64:(r + 1) * 64, bank, 0:P], vals[:, j, b, (h // 8) * DH:(h // 8 + 1) * DH],
                                        probT[:, n % 2, b, j * P:(j + 1) * P], start=False,
                                        stop=(b == 1 and j == t), skip_group_check=True)
                ins.then_inc(sem("pv"), 1)

            def out_project(l):
                pe.wait_ge(sem("w_out_loaded"), 16 * (l + 1))
                for t in range(NT):
                    for half in range(2):
                        if t >= 2:
                            pe.wait_ge(sem("y_taken"), 2 * (NT * l + t - 2) + half + 1)
                        for k in range(KD):
                            ins = pe.matmul(ps[:, 2 * (t % 2) + half, :], hTk[:, k, t * P:(t + 1) * P],
                                            w_out[l][:, k, half * 512:(half + 1) * 512], start=(k == 0), stop=(k == KD - 1))
                        ins.then_inc(sem("y_ready"), 1)

            def place(l):
                pe.wait_ge(sem("chosen"), l + 1)
                total = arena[:, R_SUM:R_SUM + P + EXPERTS]
                pe.matmul(ps[:, 6, P:2 * P + EXPERTS], cs[:, C_TRI:C_TRI + P], total, start=True, stop=False, skip_group_check=True)
                for back in range(NT, 0, -1):
                    n = (NT + 1 - back) * EXPERTS
                    ins = pe.matmul(ps[:, 6, P + back * EXPERTS:P + (NT + 1) * EXPERTS], ones[:, :], total[:, 0:n],
                                    start=False, stop=(back == 1), skip_group_check=True)
                ins.then_inc(sem("ranks"), 1)
                pe.wait_ge(sem("hots_ready"), l + 1)
                for i in range(2 * NT):
                    ins = pe.matmul(ps[:, 6, 384:384 + 2 * NB], slot_hot[:, i * SLOTS:(i + 1) * SLOTS],
                                    block_val[:, i * 2 * NB:(i + 1) * 2 * NB],
                                    start=(i == 0), stop=(i == 2 * NT - 1), skip_group_check=True)
                ins.then_inc(sem("slots_summed"), 1)

            def x_transposes(l, u, nth, b):
                pe.wait_ge(sem(f"xb_{l}_{u}"), nth * 16 + 16)
                pe.wait_ge(sem(f"xbT_a_{l}"), b)
                pe.wait_ge(sem(f"xbT_d_{l}"), b)
                for k in range(KD):
                    ins = pe.transpose(ps[:, 2 + k // 4, (k % 4) * P:(k % 4 + 1) * P], xb[u][:, k * P:(k + 1) * P], ident)
                ins.then_inc(sem(f"xb_used_{l}"), 1)

            def gate_up(l, u, nth, b):
                pe.wait_ge(sem(f"wgu_{l}_{u}"), nth * 32 + 32)
                pe.wait_ge(sem(f"xbT_a_{l}"), b + 1)
                pe.wait_ge(sem(f"xbT_d_{l}"), b + 1)
                pe.wait_ge(sem(f"hid_{l}"), b)
                for m in range(2):
                    for k in range(KD):
                        ins = pe.matmul(ps[:, m, :], xbT[:, k, :], w_gu(u, m)[:, k, :], start=(k == 0), stop=(k == KD - 1))
                    ins.then_inc(sem(f"gu_{l}"), 1)

            def hid_transposes(l, b):
                pe.wait_ge(sem(f"hid_{l}"), b + 1)
                pe.wait_ge(sem(f"hidT_{l}"), b)
                for k in range(4):
                    ins = pe.transpose(ps[:, 6, k * P:(k + 1) * P], hid[:, k * P:(k + 1) * P], ident)
                ins.then_inc(sem(f"hid_tr_{l}"), 1)

            def down(l, u, nth, b):
                pe.wait_ge(sem(f"wd_{l}_{u}"), nth * 16 + 16)
                pe.wait_ge(sem(f"hidT_{l}"), b + 1)
                pe.wait_ge(sem(f"zb_{l}"), b + GRANT)
                for half in range(2):
                    for k in range(4):
                        ins = pe.matmul(ps[:, 4 + half, :], hidT[:, k, :], w_dn(u)[:, k, half * 512:(half + 1) * 512],
                                        start=(k == 0), stop=(k == 3))
                ins.then_inc(sem(f"y_{l}"), 1)

            def moe(l):
                place(l)
                x_transposes(l, 0, 0, 0)
                gate_up(l, 0, 0, 0)
                x_transposes(l, 1, 0, 1)
                hid_transposes(l, 0)

                def step(u, nth, b, prev_nth, next_nth):
                    gate_up(l, u, nth, b)
                    if next_nth is not None:
                        x_transposes(l, 1 - u, next_nth, b + 1)
                    down(l, 1 - u, prev_nth, b - 1)
                    hid_transposes(l, b)
                with pe.Fori(0, EXPERTS // 2 - 1) as i:
                    step(1, i, i * 2 + 1, i, i + 1)
                    if l == 0:
                        ada_sum(0, i + ADA_BLOCKS)
                    step(0, i + 1, i * 2 + 2, i, i + 1)
                last = EXPERTS - 1
                step(1, last // 2, last, last // 2, None)
                if l == 0:
                    ada_sum(0, 2 * ADA_BLOCKS - 1)
                down(l, 1, last // 2, last)
                pe.wait_ge(sem("route_ready"), l + 1)
                n_ov = pe.value_load(route[0:1, 0:1], min_val=0, max_val=OVERFLOW)
                with pe.If(n_ov > 0), pe.Fori(0, n_ov) as j:
                    x_transposes(l, 0, j + EXPERTS // 2, j + EXPERTS)
                    gate_up(l, 1, j + EXPERTS // 2, j + EXPERTS)
                    hid_transposes(l, j + EXPERTS)
                    down(l, 1, j + EXPERTS // 2, j + EXPERTS)

            def mlstm_project():
                def begin(job):
                    if job >= 4:
                        pe.wait_ge(sem("proj1_taken"), job - 3)
                    return ps[:, job % 4, :]
                pe.wait_ge(sem("w_qk"), 16)
                w = area[:, M_QK:M_V].rearrange("p (k n) -> p k n", k=KD)
                for r in range(2 * MH):
                    o = begin(r)
                    for k in range(KD):
                        ins = pe.matmul(o, w[:, k, r * P:(r + 1) * P], hTk[:, k, :], start=(k == 0), stop=(k == KD - 1))
                    ins.then_inc(sem("proj1_ready"), 1)
                pe.wait_ge(sem("w_gates"), 48)
                wg = gates[:, 0:64].rearrange("p (k n) -> p k n", k=KD)
                for t in range(NT):
                    for k in range(KD):
                        ins = pe.matmul(ps[:, 4, t * 8:(t + 1) * 8], hTk[:, k, t * P:(t + 1) * P], wg[:, k, :],
                                        start=(k == 0), stop=(k == KD - 1))
                ins.then_inc(sem("ml_gate_pe"), 1)
                for part, (name, lo) in enumerate((("w_v", M_V), ("w_o", M_O))):
                    pe.wait_ge(sem(name), 16)
                    w = area[:, lo:lo + KD * D].rearrange("p (k n) -> p k n", k=KD)
                    for t in range(NT):
                        for half in range(2):
                            o = begin(8 + 8 * part + 2 * t + half)
                            for k in range(KD):
                                ins = pe.matmul(o, hTk[:, k, t * P:(t + 1) * P], w[:, k, half * 512:(half + 1) * 512],
                                                start=(k == 0), stop=(k == KD - 1))
                            ins.then_inc(sem("proj1_ready"), 1)
                    if part == 0:
                        pe.wait_ge(sem("ml_gate_dve"), 2)
                        for t in range(NT):
                            pe.transpose(ps[0:MH, 5, t * P:(t + 1) * P], ml_li[:, t, MH:2 * MH], ident)
                            ins = pe.transpose(ps[0:MH, 6, t * P:(t + 1) * P], ml_li[:, t, 0:MH], ident)
                        ins.then_inc(sem("ml_gate_pe"), 1)

            def mlstm():
                pe.wait_ge(sem("ml_gate_act"), 2)
                for t in range(NT):
                    pe.transpose(ps[:, 7, t * MH:(t + 1) * MH], ml_row(U_IN)[0:MH, t * P:(t + 1) * P], ident[0:MH, 0:MH])
                    ins = pe.transpose(ps[:, 7, 64 + t * MH:64 + (t + 1) * MH], ml_row(EXP_M)[0:MH, t * P:(t + 1) * P],
                                       ident[0:MH, 0:MH])
                ins.then_inc(sem("ml_gate_pe"), 1)
                pe.wait_ge(sem("ml_ones"), 1)
                def ml_u(h):
                    if h < 2:
                        pe.wait_ge(sem("ml_gate_act"), 3)
                    else:
                        pe.wait_ge(sem("ml_w"), NT * (h - 1))
                        pe.wait_ge(sem("ml_diag"), h - 1)
                    pe.matmul(ps[:, 6 + h % 2, :], ml_sel[:, h, :], ml_row(U_MAX)[0:MH, :], start=True, stop=True)\
                      .then_inc(sem("ml_u"), 1)

                ml_u(0)
                pe.wait_ge(sem("proj1_taken"), 24)
                for h in range(MH):
                    def ml_scores(j):
                        n = NT * h + j
                        if n >= 2:
                            pe.wait_ge(sem("ml_at"), n - 1)
                        pe.matmul(ps[:, 4 + n % 2, 0:(NT - j) * P], qT[:, MH + h, j * P:(j + 1) * P], qT[:, h, j * P:SEQ],
                                  start=True, stop=True).then_inc(sem("ml_s"), 1)

                    def ml_values(j):
                        n = NT * h + j
                        pe.wait_ge(sem("ml_at"), n + 1)
                        for t in reversed(range(j, NT)):
                            if j == 0 and h:
                                pe.wait_ge(sem("ml_out"), NT * (h - 1) + t + 1)
                            ins = pe.matmul(ps[:, t, 0:VROW], ml_at(n % 2)[:, (t - j) * P:(t - j + 1) * P], ml_vals[:, j, h, :],
                                            start=(j == 0), stop=(j == t))
                        ins.then_inc(sem("ml_num"), 1)
                    ml_scores(0)
                    for j in range(NT):
                        if j + 1 < NT:
                            ml_scores(j + 1)
                        ml_values(j)
                        if j == 1 and h + 1 < MH:
                            ml_u(h + 1)
                for t in range(NT):
                    pe.wait_ge(sem("ml_tile"), t + 1)
                    if t == 0:
                        pe.wait_ge(sem("ml_at"), NT * MH)
                        pe.wait_ge(sem("ml_diag"), MH)
                    for half in range(2):
                        if t >= 2:
                            pe.wait_ge(sem(f"mo_{'ad'[half]}"), t - 1)
                        for k in range(4):
                            ins = pe.transpose(ps[:, 4 + 2 * (t % 2) + half, k * P:(k + 1) * P],
                                               hnt[:, t, (4 * half + k) * P:(4 * half + k + 1) * P], ident)
                        ins.then_inc(sem("mo_tr"), 1)
                pe.wait_ge(sem("mo_a"), NT)
                pe.wait_ge(sem("mo_d"), NT)

            pe.sem_inc(sem("ada_summed"), GRANT)
            pe.wait_ge(sem("ones"), 1)
            pe.wait_ge(sem("consts"), 16)
            with pe.Fori(0, 4) as i:
                for u in range(2):
                    ada_sum(u, i * 2 + u)
            norm_transposes(0)
            pe.wait_ge(sem("w_in_0"), 32)
            for i in range(8):
                nsa_project(i // 4, i % 4)
                ada_sum(i % 2, 8 + i)
            for g in range(4):
                nsa_project(2, g)
            nsa_transposes(0)
            for g in range(4):
                nsa_project(3, g)
            for t in range(1, NT):
                nsa_transposes(t)
            compress()
            pe.wait_ge(sem("qT_a"), NT)
            pe.wait_ge(sem("qT_d"), NT)
            for t in range(NT):
                cmp_scores(t)
                if t:
                    cmp_transposes(t - 1)
            cmp_transposes(NT - 1)
            pe.wait_ge(sem("pcT_ready"), NT)
            pe.wait_ge(sem("cmp_act"), CMP_VALUES)
            pe.wait_ge(sem("ada_mods"), ADA_BLOCKS + GRANT)
            for n in range(len(units) + 3):
                if n < len(units):
                    scores(n)
                if 2 <= n < len(units) + 2:
                    prob_transposes(n - 2)
                if n >= 3:
                    weighted_values(n - 3)
            pe.wait_ge(sem("oT_ready"), NT * PAIRS)
            out_project(0)
            norm_transposes(1)
            moe(0)

            norm_transposes(2)
            mlstm_project()
            mlstm()
            out_project(1)
            norm_transposes(3)
            moe(1)

        @block.scalar
        def _(act):
            count = [0]

            def link(ins):
                count[0] += 1
                ins.then_inc(sem("act_chain"), 1)
                act.wait_ge(sem("act_chain"), count[0])

            def ada_take(b):
                act.wait_ge(sem("ada_summed"), b + 1 + GRANT)
                act.activation(mods[:, bass.ds(b * ADA_W, ADA_W)], ps[:, 7, 0:ADA_W], ACT.Copy).then_inc(sem("ada_mods"), 1)

            def norm(n):
                act.wait_ge(sem("ones"), 1)
                for t in range(NT + TAKE_LAG):
                    if n == 2 and t <= NT:
                        for v in ((0, 1) if t == 0 else (t + 1,)):
                            scale_z(0, v)
                    if t < NT:
                        act.wait_ge(sem(f"x_ready_{n}"), 16 if n == 0 else t + 1)
                        link(act.activation(ps[:, 4:6, :], xs[:, t, :].rearrange("p (a n) -> p a n", a=2), ACT.Square,
                                            accum_out=ssq[:, t:t + 1]))
                        act.activation(rstd[:, t:t + 1], ssq[:, t:t + 1], ACT.Sqrt, bias=eps, scale=1.0 / D)\
                           .then_inc(sem("norm_std"), 1)
                    if t >= TAKE_LAG:
                        norm_take(n, t - TAKE_LAG)

            def norm_take(n, t):
                act.wait_ge(sem("hT_tr"), 2 * (NT * n + t) + 1)
                act.activation(hTk[:, 0:4, t * P:(t + 1) * P], ps[:, (t % 2) * 2, :].rearrange("p (k s) -> p k s", k=4),
                               ACT.Copy).then_inc(sem("hT_a"), 1)

            def scale_z(l, t):
                if t < NT:
                    act.wait_ge(sem("route_ready"), l + 1)
                    act.wait_ge(sem(f"z_in_{t}"), 32 * (l + 1))
                    act.activation(z_in[t][0], z_in[t][0], ACT.Copy, scale=moe_w(0)[:, t:t + 1]).then_inc(sem("z_scaled"), 1)

            def nsa_take(t, g):
                u = t % 2
                if t >= 2:
                    act.wait_ge(sem("nsa_tr"), t - 1)
                act.wait_ge(sem("nsa_zeroed"), 1)
                act.wait_ge(sem("proj0_ready"), 4 * t + g + 1)
                if g < 2:
                    ins = act.activation(nrm[u][:, 512 * g:512 * g + 512], ps[:, g, :], ACT.Copy)
                elif g == 2:
                    act.activation(kcv[u], ps[:, 2, 0:256], ACT.Copy)
                    act.activation(nrm[u][:, 1024:1152], ps[:, 2, 256:384], ACT.Copy)
                    ins = act.activation(vals[:, t, 0, :], ps[:, 2, 384:512], ACT.Copy)
                else:
                    act.activation(nrm[u][:, 1152:1280], ps[:, 3, 0:128], ACT.Copy)
                    act.activation(vals[:, t, 1, :], ps[:, 3, 128:256], ACT.Copy)
                    ins = act.activation(gates[:, t * 48:(t + 1) * 48], ps[:, 3, 256:304], ACT.Sigmoid)
                ins.then_inc(sem("proj0_taken"), 1)

            def nsa_std(t):
                act.wait_ge(sem("head_var"), t + 1)
                act.activation(head_rstd(t % 2), head_rstd(t % 2), ACT.Sqrt).then_inc(sem("head_std"), 1)

            def nsa_take_T(t):
                cols = slice(t * P, (t + 1) * P)
                act.wait_ge(sem("nsa_tr"), t + 1)
                act.activation(qT[:, 0:4, cols], ps[:, 4, :].rearrange("p (r s) -> p r s", r=4), ACT.Copy)
                src = ps[:, 7, 0:256].rearrange("p (a s) -> p a s", a=2)
                for g in range(2):
                    rows = slice(64 * g, 64 * g + 64)
                    act.activation(kcvT[0:64, :, g, t * P + 1:t * P + 1 + P], src[rows, :, :], ACT.Copy)
                    ins = act.activation(kcvT[64:128, :, g, t * P:t * P + P], src[rows, :, :], ACT.Copy)
                ins.then_inc(sem("qT_a"), 1)

            def compress():
                for a in range(2):
                    act.wait_ge(sem("cmp_pe"), a + 1)
                    act.activation(hid_c[:, a, :], ps[0:64, a, 0:CMP_HIDDEN], ACT.Gelu_apprx_tanh).then_inc(sem("cmp_act"), 1)
                act.wait_ge(sem("cmp_pe"), HIDDEN_T)
                act.activation(hidT_c, ps[:, 2, 0:256].rearrange("p (q c) -> p q c", q=4), ACT.Copy).then_inc(sem("cmp_act"), 1)
                act.wait_ge(sem("cmp_pe"), CMP_OUT)
                for g in range(2):
                    for j in range(4):
                        ins = act.activation(vcbd[32 * j:32 * j + 32, g, 64 * j:64 * j + 64], ps[32 * g:32 * g + 32, 4, 0:DH],
                                             ACT.Copy)
                ins.then_inc(sem("cmp_act"), 1)
                act.wait_ge(sem("cmp_dve"), KEY_VAR)
                act.activation(head_ss[0:64, 1:2], head_ss[0:64, 1:2], ACT.Sqrt).then_inc(sem("cmp_act"), 1)

            def cmp_exp(t):
                act.wait_ge(sem("pc_shifted"), t + 1)
                act.activation(pc[:, t, :], pc[:, t, :], ACT.Exp).then_inc(sem("pc_exp"), 1)

            def cmp_take(t):
                act.wait_ge(sem("pc_tr"), t + 1)
                act.activation(pcT[:, t, :, :], ps[:, 4 + t % 2, :].rearrange("p (q n) -> p q n", q=4), ACT.Copy)\
                   .then_inc(sem("pcT_ready"), 1)

            units = [(t, h) for t in range(NT) for h in range(HEADS)]

            def attend():
                for n in range(len(units) + 3):
                    if n < len(units):
                        t, h = units[n]
                        act.wait_ge(sem("neg_max"), n + 1)
                        if n >= 3:
                            act.wait_ge(sem("prob_tr"), n - 2)
                        for b in range(2):
                            ins = act.activation(prob[n % 3][:, b, 0:(t + 1) * P], ps[:, 2 * (n % 2) + b, 0:(t + 1) * P],
                                                 ACT.Exp, bias=neg_max(n % 2)[:, b:b + 1], scale=SCALE,
                                                 accum_out=sum_l(n % 2)[:, b:b + 1])
                        ins.then_inc(sem("exp_done"), 1)
                    if 2 <= n < len(units) + 2:
                        m = n - 2
                        t, h = units[m]
                        act.wait_ge(sem("prob_tr"), m + 1)
                        if m >= 2:
                            act.wait_ge(sem("pv"), m - 1)
                        act.activation(probT[:, m % 2, 0, 0:(t + 1) * P], ps[:, 4, 0:(t + 1) * P], ACT.Copy)\
                           .then_inc(sem("probT_a"), 1)
                    if n >= 3 and (n - 3) % 2:
                        m = n - 3
                        t, h = units[m]
                        act.wait_ge(sem("pv"), m + 1)
                        act.activation(hTk[:, h // 2, t * P:(t + 1) * P], ps[:, 6 + (m // 2) % 2, 0:P], ACT.Copy)\
                           .then_inc(sem("oT_ready"), 1)

            def moe(l):
                act.wait_ge(sem("logits"), l + 1)
                act.activation(arena[:, R_AFF:R_AFF + P], ps[:, 6, 0:P], ACT.Sigmoid).then_inc(sem("affinity"), 1)
                act.activation(ffn_gate, mods[:, G_F:G_F + D], ACT.Copy).then_inc(sem("ffn_gate"), 1)

                def take_x(b):
                    act.wait_ge(sem(f"xb_used_{l}"), b + 1)
                    act.activation(xbT[:, 0:4, :], ps[:, 2, :].rearrange("p (k s) -> p k s", k=4), ACT.Copy)\
                       .then_inc(sem(f"xbT_a_{l}"), 1)

                def sigmoid(b):
                    act.wait_ge(sem(f"gu_{l}"), b * 2 + 1)
                    act.activation(sig, ps[:, 0, :], ACT.Sigmoid).then_inc(sem(f"sig_{l}"), 1)
                    act.wait_ge(sem(f"gu_{l}"), b * 2 + 2)

                def take_y(b, u, nth):
                    act.wait_ge(sem(f"y_{l}"), b + 1)
                    if nth is not None:
                        act.wait_ge(sem(f"z_stored_{l}_{u}"), nth * 16)
                    act.activation(zb[u].rearrange("p (a n) -> p a n", a=2), ps[:, 4:6, :], ACT.Copy).then_inc(sem(f"zb_{l}"), 1)

                def take_hid(b):
                    act.wait_ge(sem(f"hid_tr_{l}"), b + 1)
                    act.activation(hidT, ps[:, 6, :].rearrange("p (k s) -> p k s", k=4), ACT.Copy).then_inc(sem(f"hidT_{l}"), 1)

                act.sem_inc(sem(f"zb_{l}"), GRANT)
                take_x(0)
                sigmoid(0)
                take_x(1)
                take_hid(0)

                def step(u, b, prev_nth, last=False):
                    sigmoid(b)
                    if not last:
                        take_x(b + 1)
                    take_y(b - 1, 1 - u, prev_nth)
                    take_hid(b)
                def pair(i, prev_nth):
                    step(1, i * 2 + 1, prev_nth)
                    if l == 0:
                        act.wait_ge(sem("ada_summed"), i + ADA_BLOCKS + 1 + GRANT)
                        act.activation(mods[:, bass.ds(i * ADA_W, ADA_W)], ps[:, 7, 0:ADA_W], ACT.Copy).then_inc(sem("ada_mods"), 1)
                    step(0, i * 2 + 2, prev_nth)
                pair(0, None)
                with act.Fori(1, EXPERTS // 2 - 1) as i:
                    pair(i, i)
                last = EXPERTS - 1
                step(1, last, last // 2, last=True)
                if l == 0:
                    act.wait_ge(sem("ada_summed"), 2 * ADA_BLOCKS + GRANT)
                    act.activation(mods[:, (ADA_BLOCKS - 1) * ADA_W:ADA_COLS], ps[:, 7, 0:ADA_W], ACT.Copy)\
                       .then_inc(sem("ada_mods"), 1)
                take_y(last, 1, last // 2)
                act.wait_ge(sem(f"z_stored_{l}_0"), 16 * (EXPERTS // 2))
                act.wait_ge(sem("route_ready"), l + 1)
                n_ov = act.value_load(route[0:1, 0:1], min_val=0, max_val=OVERFLOW)
                with act.If(n_ov > 0), act.Fori(0, n_ov) as j:
                    take_x(j + EXPERTS)
                    sigmoid(j + EXPERTS)
                    take_hid(j + EXPERTS)
                    take_y(j + EXPERTS, 0, None)

            def mlstm_take(job):
                act.wait_ge(sem("proj1_ready"), job + 1)
                src = ps[:, job % 4, :]
                if job < 8:
                    ins = act.activation(qT[:, job, :], src, ACT.Copy)
                elif job < 16:
                    t, half = divmod(job - 8, 2)
                    ins = act.activation(ml_vals[:, t, 2 * half:2 * half + 2, 0:DV], src.rearrange("p (h d) -> p h d", h=2), ACT.Copy)
                else:
                    t, half = divmod(job - 16, 2)
                    ins = act.activation(hnt[:, t, half * 512:(half + 1) * 512], src, ACT.Sigmoid)
                ins.then_inc(sem("proj1_taken"), 1)

            def mlstm_gates():
                act.wait_ge(sem("ml_gate_dve"), 1)
                link(act.activation(ml_li, ml_li, ACT.Tanh, scale=1.0 / SOFTCAP))
                link(act.activation(ml_li[:, :, MH:2 * MH], ml_li[:, :, MH:2 * MH], ACT.Exp, scale=-SOFTCAP))
                act.activation(ml_li[:, :, MH:2 * MH], ml_li[:, :, MH:2 * MH], ACT.Ln, bias=1.0).then_inc(sem("ml_gate_act"), 1)

            def mlstm():
                act.wait_ge(sem("ml_gate_dve"), 3)
                act.activation(ml_row(EXP_M)[0:MH, :], ml_row(EXP_M)[0:MH, :], ACT.Exp, scale=-1.0).then_inc(sem("ml_gate_act"), 1)
                act.wait_ge(sem("ml_gate_pe"), 3)
                act.activation(ml_cols, ps[:, 7, 0:128].rearrange("p (a n) -> p a n", a=2)[:, :, 0:16], ACT.Copy)\
                   .then_inc(sem("ml_gate_act"), 1)
                act.wait_ge(sem("ml_gate_act"), 3)
                for h in range(MH):
                    act.wait_ge(sem("ml_u"), h + 1)
                    act.wait_ge(sem("ml_diag"), h + 1)
                    for j in range(NT):
                        n = NT * h + j
                        if n >= 2:
                            act.wait_ge(sem("ml_at"), n - 1)
                        u_col = ml_cols[:, 0, j * MH + h:j * MH + h + 1]
                        ins = act.activation(ml_w(n % 2)[:, 0:P], ml_diag[:, j * P:(j + 1) * P], ACT.Exp, bias=u_col, scale=-1.0)
                        if j < NT - 1:
                            ins = act.activation(ml_w(n % 2)[:, P:(NT - j) * P], ps[:, 6 + h % 2, (j + 1) * P:SEQ], ACT.Exp,
                                                 bias=u_col, scale=-1.0)
                        ins.then_inc(sem("ml_w"), 1)
                    for t in range(NT):
                        at = t * MH + h
                        act.wait_ge(sem("ml_num"), NT * h + t + 1)
                        act.activation(ml_den[:, at:at + 1], ps[:, t, DV:VROW], ACT.Copy)
                        if h + t:
                            act.wait_ge(sem("ml_sums"), NT * h + t)
                        act.activation(ml_sq, ps[:, t, 0:DV], ACT.Square, accum_out=ml_ssq[:, at:at + 1]).then_inc(sem("ml_sums"), 1)
                act.wait_ge(sem("ml_hvar"), 1)
                act.activation(ml_scale, ml_scale, ACT.Sqrt).then_inc(sem("ml_hstd"), 1)
                for t in range(NT):
                    act.wait_ge(sem("mo_tr"), 2 * t + 1)
                    act.activation(hTk[:, 0:4, t * P:(t + 1) * P], ps[:, 4 + 2 * (t % 2), :].rearrange("p (k s) -> p k s", k=4),
                                   ACT.Copy).then_inc(sem("mo_a"), 1)

            act.sem_inc(sem("ada_mods"), GRANT)
            act.wait_ge(sem("c_loaded"), 16)
            act.activation(cond[:, KD:2 * KD], cond[:, 0:KD], ACT.Sigmoid).then_inc(sem("cond_sig"), 1)
            with act.Fori(0, 8) as b:
                ada_take(b)
            norm(0)
            for i in range(8):
                nsa_take(i // 4, i % 4)
                ada_take(8 + i)
            nsa_std(0)
            nsa_std(1)
            for t in range(2, NT):
                nsa_take_T(t - 2)
                for g in range(4):
                    nsa_take(t, g)
                nsa_std(t)
            for t in range(2, NT):
                nsa_take_T(t)
            compress()
            for t in range(NT):
                cmp_exp(t)
                if t:
                    cmp_take(t - 1)
            cmp_take(NT - 1)
            attend()
            norm(1)
            moe(0)

            norm(2)
            for job in range(8):
                mlstm_take(job)
            mlstm_gates()
            for job in range(8, 24):
                mlstm_take(job)
            mlstm()
            norm(3)
            moe(1)
            for t in range(NT):
                scale_z(1, t)

        @block.vector
        def _(dve):
            count = [0]

            def link(ins):
                count[0] += 1
                ins.then_inc(sem("dve_chain"), 1)
                dve.wait_ge(sem("dve_chain"), count[0])

            def ada_products(buf, u, done, steps):
                dve.wait_ge(sem("ada_summed"), done + GRANT)
                src = ada_bias[:, u, :]
                for k in range(KD):
                    ins = dve.scalar_tensor_tensor(out=ada_acc[:, u, :], in0=buf[:, k, :], scalar=cond[:, KD + k:KD + k + 1],
                                                   in1=src, op0=ALU.mult, op1=ALU.add)
                    src = ada_acc[:, u, :]
                    if k < KD - 1:
                        ins.then_inc(sem("ada_chain"), 1)
                        dve.wait_ge(sem("ada_chain"), steps * (KD - 1) + (k + 1))
                return ins

            def ada_block(which, buf, u, nth, b, summed):
                dve.wait_ge(sem(f"ada_loaded_{which}"), nth * 32 + 32)
                ada_products(buf, u, summed, b).then_inc(sem("ada_acc"), 1)
                dve.wait_ge(sem("ada_acc"), b + 1)
                dve.sem_inc(sem(f"ada_read_{which}"), 1)

            def norm(n, produce=None):
                scale = SC_F if n % 2 else SC_M
                dve.wait_ge(sem("norm_gain"), 16 * (n + 1))
                if n != 3:
                    dve.wait_ge(sem("ada_mods"), (8, ADA_BLOCKS, 2 * ADA_BLOCKS)[n] + GRANT)
                link(dve.scalar_tensor_tensor(out=mods[:, scale:scale + D], in0=mods[:, scale:scale + D], scalar=1.0,
                                              in1=gain_tile[n], op0=ALU.add, op1=ALU.mult))
                for t in range(NT + TAKE_LAG):
                    if produce and t < NT:
                        produce(t)
                    if 1 <= t <= NT:
                        v = t - 1
                        dve.wait_ge(sem("norm_std"), NT * n + v + 1)
                        link(dve.reciprocal(rstd[:, v:v + 1], rstd[:, v:v + 1]))
                        dve.scalar_tensor_tensor(out=hnt[:, v, :], in0=xs[:, v, :], scalar=rstd[:, v:v + 1],
                                                 in1=mods[:, scale:scale + D], op0=ALU.mult, op1=ALU.mult)\
                           .then_inc(sem("hn_scaled"), 1)
                    if t >= TAKE_LAG:
                        norm_take(n, t - TAKE_LAG)

            def norm_take(n, t):
                dve.wait_ge(sem("hT_tr"), 2 * (NT * n + t) + 2)
                dve.tensor_copy(hTk[:, 4:8, t * P:(t + 1) * P], ps[:, (t % 2) * 2 + 1, :].rearrange("p (k s) -> p k s", k=4))\
                   .then_inc(sem("hT_d"), 1)

            def rope(heads, cos, sin, tmp):
                x1, x2 = heads[:, :, 0:HALF], heads[:, :, HALF:ROT]
                rows, n = heads.shape[0], heads.shape[1]
                shape = [rows, n, HALF]
                cos = cos.rearrange("p (o e) -> p o e", o=1).to_broadcast(shape)
                sin = sin.rearrange("p (o e) -> p o e", o=1).to_broadcast(shape)
                a, b, d = tmp
                dve.tensor_tensor(a, x1, cos, ALU.mult)
                dve.tensor_tensor(b, x2, sin, ALU.mult)
                link(dve.tensor_tensor(d, x1, sin, ALU.mult))
                link(dve.tensor_tensor(x1, a, b, ALU.subtract))
                link(dve.tensor_tensor(a, x2, cos, ALU.mult))
                return dve.tensor_tensor(x2, a, d, ALU.add)

            def nsa_norm(t):
                u = t % 2
                heads = nrm[u].rearrange("p (h e) -> p h e", e=DH)
                dve.wait_ge(sem("proj0_taken"), 4 * t + 4)
                if t:
                    dve.wait_ge(sem("nrm_ready"), t)
                for lo in range(0, 20, 8):
                    n = min(8, 20 - lo)
                    sq = area[:, A_SMALL:A_SMALL + n * DH]
                    link(dve.tensor_tensor(sq, nrm[u][:, lo * DH:(lo + n) * DH], nrm[u][:, lo * DH:(lo + n) * DH], ALU.mult))
                    link(dve.tensor_reduce(head_rstd(u)[:, lo:lo + n], sq.rearrange("p (h e) -> p h e", e=DH), AX, ALU.add))
                dve.tensor_scalar(head_rstd(u), head_rstd(u), 1.0 / DH, EPS, ALU.mult, ALU.add).then_inc(sem("head_var"), 1)
                dve.wait_ge(sem("head_std"), t + 1)
                link(dve.reciprocal(head_rstd(u), head_rstd(u)))
                link(dve.tensor_tensor(heads, heads, head_rstd(u).rearrange("p (h o) -> p h o", o=1).to_broadcast([P, 20, DH]),
                                       ALU.mult))
                for g, (lo, hi) in enumerate(((0, 16), (16, 18), (18, 20))):
                    gain = hgain[:, g * DH:(g + 1) * DH].rearrange("p (o e) -> p o e", o=1).to_broadcast([P, hi - lo, DH])
                    ins = dve.tensor_tensor(heads[:, lo:hi, :], heads[:, lo:hi, :], gain, ALU.mult)
                link(ins)
                at = C_ROPE + t * ROT
                rope(heads, cs[:, at:at + HALF], cs[:, at + HALF:at + ROT],
                     [r.rearrange("p (h e) -> p h e", e=HALF) for r in rope_tmp]).then_inc(sem("nrm_ready"), 1)

            def nsa_take_T(t):
                cols = slice(t * P, (t + 1) * P)
                dve.wait_ge(sem("nsa_tr"), t + 1)
                dve.tensor_copy(qT[:, 4:8, cols], ps[:, 5, :].rearrange("p (r s) -> p r s", r=4))
                src = ps[:, 6, 0:256].rearrange("p (b s) -> p b s", b=2)
                for g in range(2):
                    for r in range(2):
                        ins = dve.tensor_copy(ktz[64 * r:64 * r + 64, :, g, r, cols], src[64 * g:64 * g + 64, :, :])
                ins.then_inc(sem("qT_d"), 1)

            def compress():
                dve.wait_ge(sem("qT_a"), NT)
                for a in range(2):
                    for g in range(2):
                        for hi in range(2):
                            lo = 1 + 16 * hi
                            src = kcvT[:, a, g, lo:lo + SEQ].rearrange("p (c m two) -> p m c two", m=8, two=2)[:, :, :, 0]
                            ins = dve.tensor_tensor(blk[:, a, 8 * hi:8 * hi + 8, g * NC:(g + 1) * NC], src,
                                                    pe_t[:, a, 8 * hi:8 * hi + 8].rearrange("p (m o) -> p m o", o=1)
                                                    .to_broadcast([P, 8, NC]), ALU.add)
                    ins.then_inc(sem("cmp_dve"), 1)
                k0 = kcn[:, 0:DH]
                dve.wait_ge(sem("cmp_pe"), CMP_OUT)
                link(dve.tensor_copy(k0, ps[0:64, 3, 0:DH]))
                link(dve.tensor_tensor(ksq, k0, k0, ALU.mult))
                link(dve.tensor_reduce(head_ss[0:64, 0:1], ksq, AX, ALU.add))
                dve.tensor_scalar(head_ss[0:64, 1:2], head_ss[0:64, 0:1], 1.0 / DH, EPS, ALU.mult, ALU.add).then_inc(sem("cmp_dve"), 1)
                dve.wait_ge(sem("cmp_act"), KEY_STD)
                link(dve.reciprocal(head_ss[0:64, 2:3], head_ss[0:64, 1:2]))
                link(dve.scalar_tensor_tensor(out=k0, in0=k0, scalar=head_ss[0:64, 2:3], in1=hgain[0:64, 3 * DH:4 * DH],
                                              op0=ALU.mult, op1=ALU.mult))
                link(rope(k0.rearrange("p (h e) -> p h e", h=1), cs[0:64, C_CROPE:C_CROPE + HALF],
                          cs[0:64, C_CROPE + HALF:C_CROPE + ROT],
                          [r[0:64, 0:HALF].rearrange("p (h e) -> p h e", e=HALF) for r in rope_tmp]))
                dve.tensor_copy(kcn[:, DH:2 * DH], k0).then_inc(sem("cmp_dve"), 1)
                dve.wait_ge(sem("cmp_pe"), KEY_T)
                dve.tensor_copy(kctz[0:64, 0, :], ps[0:64, 0, 0:64])
                dve.tensor_copy(kctz[64:128, 1, :], ps[64:128, 0, 0:64]).then_inc(sem("cmp_dve"), 1)

            def cmp_softmax(t):
                s = pc[:, t, :]
                heads = s.rearrange("p (h c) -> p h c", c=NC)

                def over_slots(v):
                    return v.rearrange("p (h o) -> p h o", o=1).to_broadcast([P, HEADS, NC])
                mask = cs[:, C_CMASK + t * NC:C_CMASK + (t + 1) * NC].rearrange("p (o c) -> p o c", o=1)\
                    .to_broadcast([P, HEADS, NC])
                r = cmp_r
                dve.wait_ge(sem("cmp_s"), t + 1)
                dve.scalar_tensor_tensor(out=heads, in0=ps[:, 1 + t % 2, :].rearrange("p (h c) -> p h c", c=NC), scalar=SCALE,
                                         in1=mask, op0=ALU.mult, op1=ALU.add).then_inc(sem("cmp_s_read"), 1)
                dve.wait_ge(sem("cmp_s_read"), t + 1)
                link(dve.tensor_reduce(r, heads, AX, ALU.max))
                dve.tensor_tensor(heads, heads, over_slots(r), ALU.subtract).then_inc(sem("pc_shifted"), 1)
                dve.wait_ge(sem("pc_exp"), t + 1)
                link(dve.tensor_reduce(r, heads, AX, ALU.add))
                link(dve.reciprocal(r, r))
                link(dve.scalar_tensor_tensor(out=r, in0=r, scalar=cs[:, C_ROWOK + t:C_ROWOK + t + 1],
                                              in1=gates[:, t * 48:t * 48 + HEADS], op0=ALU.mult, op1=ALU.mult))
                dve.tensor_tensor(heads, heads, over_slots(r), ALU.mult).then_inc(sem("pc_ready"), 1)

            units = [(t, h) for t in range(NT) for h in range(HEADS)]

            def attend():
                causal = cs[:, C_CAUSAL:C_CAUSAL + P].rearrange("p (o s) -> p o s", o=1).to_broadcast([P, 2, P])
                for n in range(len(units) + 3):
                    if n < len(units):
                        t, h = units[n]
                        u = n % 2
                        s = ps[:, 2 * u:2 * u + 2, :]
                        dve.wait_ge(sem("scores"), n + 1)
                        link(dve.tensor_tensor(s[:, :, t * P:(t + 1) * P], s[:, :, t * P:(t + 1) * P], causal, ALU.add))
                        link(dve.tensor_reduce(raw_max(u), s[:, :, 0:(t + 1) * P], AX, ALU.max))
                        dve.tensor_scalar(neg_max(u), raw_max(u), -SCALE, None, ALU.mult).then_inc(sem("neg_max"), 1)
                    if 1 <= n <= len(units):
                        m = n - 1
                        t, h = units[m]
                        u = m % 2
                        gate = gates[:, t * 48 + 16:t * 48 + 48].rearrange("p (b h) -> p b h", b=2)[:, :, h]
                        dve.wait_ge(sem("exp_done"), m + 1)
                        if m >= 2:
                            dve.wait_ge(sem("prob_ready_p"), m - 1)
                        link(dve.reciprocal(inv_l(u), sum_l(u)))
                        dve.tensor_tensor(inv_l(u), inv_l(u), gate, ALU.mult).then_inc(sem("prob_scale"), 1)
                        dve.wait_ge(sem("prob_scale"), m + 1)
                        p1 = prob[m % 3][:, 1, 0:(t + 1) * P]
                        dve.tensor_scalar(p1, p1, inv_l(u)[:, 1:2], None, ALU.mult).then_inc(sem("prob_ready_d"), 1)
                    if 2 <= n < len(units) + 2:
                        m = n - 2
                        t, h = units[m]
                        dve.wait_ge(sem("prob_tr"), m + 1)
                        if m >= 2:
                            dve.wait_ge(sem("pv"), m - 1)
                        dve.tensor_copy(probT[:, m % 2, 1, 0:(t + 1) * P], ps[:, 5, 0:(t + 1) * P]).then_inc(sem("probT_d"), 1)

            def residual(l, t):
                for half in range(2):
                    y = ps[:, 2 * (t % 2) + half, :]
                    cols = slice(half * 512, (half + 1) * 512)
                    dve.wait_ge(sem("y_ready"), 2 * (NT * l + t) + half + 1)
                    link(dve.tensor_tensor(y, y, mods[:, G_M + half * 512:G_M + (half + 1) * 512], ALU.mult))
                    dve.tensor_tensor(xs[:, t, cols], xs[:, t, cols], y, ALU.add).then_inc(sem("y_taken"), 1)
                    dve.wait_ge(sem("y_taken"), 2 * (NT * l + t) + half + 1)
                dve.sem_inc(sem(f"x_ready_{2 * l + 1}"), 1)
                dve.sem_inc(sem("w_out_used"), 1)

            def combine(l, t):
                z0, z1 = z_in[t]
                dve.wait_ge(sem("ffn_gate"), l + 1)
                dve.wait_ge(sem(f"z_in_{t}"), 32 * (l + 1))
                dve.wait_ge(sem("z_scaled"), NT * l + t + 1)
                link(dve.scalar_tensor_tensor(out=z0, in0=z1, scalar=moe_w(1)[:, t:t + 1], in1=z0, op0=ALU.mult, op1=ALU.add))
                link(dve.tensor_tensor(z0, z0, ffn_gate, ALU.mult))
                dve.tensor_tensor(xs[:, t, :], xs[:, t, :], z0, ALU.add).then_inc(sem(f"x_ready_{2 * l + 2}"), 1)

            def routing(l):
                def a(lo, n=P):
                    return arena[:, lo:lo + n]

                def t_e(v):
                    return v.rearrange("p (t e) -> p t e", t=NT)

                def tg_e(v):
                    return v.rearrange("p (q e) -> p q e", e=EPG)
                AFF, CH, EQ, MSK, E1, E2, SUM, BLK, SLT, F, TMP = (a(r) for r in (R_AFF, R_CH, R_EQ, R_MSK, R_E1, R_E2, R_SUM,
                                                                                 R_BLK, R_SLOT, R_F, R_TMP))
                M1, M2, FI, GS, GO = (a(R_S + 16 * i, 16) for i in range(5))
                OV, CUM, EXC = (a(R_S + 96 + 32 * i, 32) for i in range(3))
                QUAD = [a(R_S + 192 + 4 * i, 4) for i in range(4)]
                AT_BLOCK, AT_SLOT = (a(R_S + 208 + 8 * i, 8) for i in range(2))
                OVX = a(R_S + 256, 8)
                CNT = a(R_S + 264, 32)
                OVC = a(R_S + 296, 8 * EXPERTS)

                def bc(v, shape):
                    return v.rearrange("p (q o) -> p q o", o=1).to_broadcast(shape)

                def row(lo, n, times):
                    return cs[:, lo:lo + n].rearrange("p (o e) -> p o e", o=1).to_broadcast([P, times, n])

                def first_of(values, best, hot, groups, per, iota):
                    v, h3 = (w.rearrange("p (q e) -> p q e", e=per) for w in (values, hot))
                    fi = FI[:, 0:groups]
                    link(dve.tensor_tensor(h3, v, bc(best, [P, groups, per]), ALU.is_equal))
                    link(dve.tensor_tensor(h3, h3, row(iota, per, groups), ALU.mult))
                    link(dve.tensor_reduce(fi, h3, AX, ALU.min))
                    link(dve.tensor_tensor(h3, row(iota, per, groups), bc(fi, [P, groups, per]), ALU.is_equal))

                dve.wait_ge(sem("affinity"), l + 1)
                dve.wait_ge(sem("router_w"), 48 * (l + 1))
                link(dve.tensor_tensor(t_e(CH), t_e(AFF), a(R_B, EXPERTS).rearrange("p (o e) -> p o e", o=1)
                                       .to_broadcast([P, NT, EXPERTS]), ALU.add))
                link(dve.tensor_reduce(M1, tg_e(CH), AX, ALU.max))
                first_of(CH, M1, E1, NT * EGROUPS, EPG, C_IOTA_8)
                link(dve.scalar_tensor_tensor(out=MSK, in0=E1, scalar=NEG, in1=CH, op0=ALU.mult, op1=ALU.add))
                link(dve.tensor_reduce(M2, tg_e(MSK), AX, ALU.max))
                first_of(MSK, M2, E2, NT * EGROUPS, EPG, C_IOTA_8)
                link(dve.tensor_tensor(GS, M1, M2, ALU.add))
                link(dve.tensor_reduce(QUAD[0], GS.rearrange("p (t g) -> p t g", t=NT), AX, ALU.max))
                first_of(GS, QUAD[0], GO, NT, EGROUPS, C_IOTA_4)
                for e in (E1, E2):
                    link(dve.tensor_tensor(tg_e(e), tg_e(e), bc(GO, [P, NT * EGROUPS, EPG]), ALU.mult))
                link(dve.memset(BLK[:, 0:EXPERTS], 0.0))
                dve.tensor_tensor(SUM, E1, E2, ALU.add).then_inc(sem("chosen"), 1)
                for k, e in enumerate((E1, E2)):
                    link(dve.tensor_tensor(TMP, AFF, e, ALU.mult))
                    link(dve.tensor_reduce(QUAD[1 + k], t_e(TMP), AX, ALU.add))
                link(dve.tensor_tensor(QUAD[3], QUAD[1], QUAD[2], ALU.add))
                link(dve.reciprocal(QUAD[3], QUAD[3]))
                dve.tensor_tensor(moe_w(0), QUAD[1], QUAD[3], ALU.mult)
                link(dve.tensor_tensor(moe_w(1), QUAD[2], QUAD[3], ALU.mult))
                dve.wait_ge(sem("ranks"), l + 1)
                dve.tensor_copy(CNT, ps[:, 6, 2 * P:2 * P + EXPERTS])
                link(dve.tensor_copy(TMP, ps[:, 6, P:2 * P]))
                for dst, src in ((F, TMP), (OV, CNT)):
                    bound = SLOTS if dst is F else SLOTS + 1
                    link(dve.tensor_scalar(dst, src, float(bound), None, ALU.is_ge))
                    for m in range(1, SEQ // SLOTS - 1):
                        link(dve.scalar_tensor_tensor(out=dst, in0=src, scalar=float(bound + m * SLOTS), in1=dst,
                                                      op0=ALU.is_ge, op1=ALU.add))
                link(dve.scalar_tensor_tensor(out=SLT, in0=F, scalar=-float(SLOTS), in1=TMP, op0=ALU.mult, op1=ALU.add))
                link(dve.tensor_tensor_scan(CUM, OV, cs[:, C_ZERO:C_ZERO + EXPERTS], 0.0, ALU.add, ALU.add))
                link(dve.tensor_tensor(EXC, CUM, OV, ALU.subtract))
                iota_e = cs[:, C_IOTA_E:C_IOTA_E + EXPERTS]
                link(dve.tensor_tensor(EXC, EXC, iota_e, ALU.subtract))
                link(dve.scalar_tensor_tensor(out=t_e(TMP), in0=t_e(F), scalar=float(EXPERTS - 1),
                                              in1=EXC.rearrange("p (o e) -> p o e", o=1).to_broadcast([P, NT, EXPERTS]),
                                              op0=ALU.add, op1=ALU.add))
                link(dve.scalar_tensor_tensor(out=BLK, in0=F, scalar=0.0, in1=TMP, op0=ALU.is_gt, op1=ALU.mult))
                link(dve.tensor_tensor(t_e(BLK), t_e(BLK), row(C_IOTA_E, EXPERTS, NT), ALU.add))
                for k, e in enumerate((E1, E2)):
                    for dst, src in ((AT_BLOCK, BLK), (AT_SLOT, SLT)):
                        link(dve.tensor_tensor(TMP, src, e, ALU.mult))
                        link(dve.tensor_reduce(dst[:, k * NT:(k + 1) * NT], t_e(TMP), AX, ALU.add))
                hot, at_block, vals2 = (v.rearrange("p (i s) -> p i s", i=n_hot) for v in (slot_hot, block_hot, block_val))
                index = a(R_SLOTS, SLOTS).rearrange("p (o s) -> p o s", o=1)
                dve.tensor_tensor(hot, index.to_broadcast([P, n_hot, SLOTS]), bc(AT_SLOT, [P, n_hot, SLOTS]), ALU.is_equal)
                link(dve.tensor_tensor(at_block, index[:, :, 0:NB].to_broadcast([P, n_hot, NB]), bc(AT_BLOCK, [P, n_hot, NB]),
                                       ALU.is_equal))
                token = bc(cs[:, C_TOKEN:C_TOKEN + NT], [P, NT, NB])
                first, second = slice(0, NT), slice(NT, 2 * NT)
                dve.tensor_tensor(vals2[:, second, 0:NB], at_block[:, second, :], token, ALU.mult)
                dve.tensor_tensor(vals2[:, second, NB:2 * NB], at_block[:, second, :], token, ALU.mult)
                link(dve.tensor_tensor(vals2[:, first, 0:NB], at_block[:, first, :], token, ALU.mult))
                dve.scalar_tensor_tensor(out=vals2[:, first, NB:2 * NB], in0=at_block[:, first, :], scalar=-float(SEQ),
                                         in1=vals2[:, first, 0:NB], op0=ALU.mult, op1=ALU.add).then_inc(sem("hots_ready"), 1)
                dve.wait_ge(sem("slots_summed"), l + 1)
                dve.tensor_scalar(EQ[:, 0:NB], ps[:, 6, 384:384 + NB], float(NOBODY), None, ALU.add)
                link(dve.tensor_scalar(EQ[:, NB:2 * NB], ps[:, 6, 384 + NB:384 + 2 * NB], float(2 * SEQ), None, ALU.add))
                dve.tensor_copy(slot_row[:, :], EQ[:, NB:2 * NB])
                dve.tensor_copy(slot_tok[:, :], EQ[:, 0:NB]).then_inc(sem("slots_ready"), 1)
                ovc = OVC.rearrange("p (j e) -> p j e", e=EXPERTS)
                link(dve.tensor_tensor(ovc, CUM.rearrange("p (o e) -> p o e", o=1).to_broadcast([P, 8, EXPERTS]),
                                       bc(cs[:, C_IOTA_OV:C_IOTA_OV + 8], [P, 8, EXPERTS]), ALU.is_le))
                link(dve.tensor_reduce(OVX, ovc, AX, ALU.add))
                link(dve.tensor_scalar(OVX, OVX, float(EXPERTS - 1), None, ALU.min))
                dve.tensor_copy(route[:, 1:8], OVX[:, 0:7])
                dve.tensor_copy(route[:, 0:1], CUM[:, EXPERTS - 1:EXPERTS]).then_inc(sem("route_ready"), 1)

            def moe(l):
                def take_x(b):
                    dve.wait_ge(sem(f"xb_used_{l}"), b + 1)
                    dve.wait_ge(sem(f"gu_{l}"), b * 2)
                    dve.tensor_copy(xbT[:, 4:8, :], ps[:, 3, :].rearrange("p (k s) -> p k s", k=4)).then_inc(sem(f"xbT_d_{l}"), 1)

                def hidden(b):
                    dve.wait_ge(sem(f"sig_{l}"), b + 1)
                    dve.wait_ge(sem(f"hid_tr_{l}"), b)
                    dve.tensor_tensor(hid, sig, ps[:, 0, :], ALU.mult).then_inc(sem(f"silu_{l}"), 1)
                    dve.wait_ge(sem(f"silu_{l}"), b + 1)
                    dve.wait_ge(sem(f"gu_{l}"), b * 2 + 2)
                    dve.tensor_tensor(hid, hid, ps[:, 1, :], ALU.mult).then_inc(sem(f"hid_{l}"), 1)

                take_x(0)
                hidden(0)
                take_x(1)
                with dve.Fori(0, EXPERTS // 2 - 1) as i:
                    for u in range(2):
                        hidden(i * 2 + 1 + u)
                        take_x(i * 2 + 2 + u)
                        if l == 0 and u == 0:
                            ada_block("next", ada_buf, 0, i, i + ADA_BLOCKS, i + ADA_BLOCKS)
                hidden(EXPERTS - 1)
                if l == 0:
                    ada_block("next", ada_buf, 0, ADA_BLOCKS - 1, 2 * ADA_BLOCKS - 1, 2 * ADA_BLOCKS - 1)
                dve.wait_ge(sem("route_ready"), l + 1)
                n_ov = dve.value_load(route[0:1, 0:1], min_val=0, max_val=OVERFLOW)
                with dve.If(n_ov > 0), dve.Fori(0, n_ov) as j:
                    take_x(j + EXPERTS)
                    hidden(j + EXPERTS)

            def mlstm_gates():
                dve.wait_ge(sem("ml_gate_pe"), 1)
                dve.tensor_tensor(ml_li, ps[:, 4, 0:8 * NT].rearrange("p (t g) -> p t g", t=NT),
                                  gates[:, 96:104].rearrange("p (o g) -> p o g", o=1).to_broadcast([P, NT, 8]), ALU.add)\
                   .then_inc(sem("ml_gate_dve"), 1)
                dve.wait_ge(sem("ml_gate_act"), 1)
                dve.tensor_scalar(ml_li[:, :, 0:MH], ml_li[:, :, 0:MH], SOFTCAP, None, ALU.mult)
                dve.tensor_scalar(ml_li[:, :, MH:2 * MH], ml_li[:, :, MH:2 * MH], -1.0, None, ALU.mult).then_inc(sem("ml_gate_dve"), 1)

            def mlstm_rows():
                dve.wait_ge(sem("proj1_ready"), 16)
                dve.wait_ge(sem("ml_gate_pe"), 2)

                def r(i):
                    return ml_row(i)[0:MH, :]
                link(dve.memset(r(ZERO), 0.0))
                link(dve.tensor_copy(r(LF), ps[0:MH, 5, :]))
                link(dve.tensor_tensor_scan(r(CUM_B), r(LF), r(ZERO), 0.0, ALU.add, ALU.add))
                link(dve.tensor_tensor(r(U_IN), ps[0:MH, 6, :], r(CUM_B), ALU.subtract))
                link(dve.tensor_tensor_scan(r(U_MAX), r(U_IN), r(U_IN), 0.0, ALU.max, ALU.max))
                dve.tensor_copy(ml_sel, ident[0:MH, 0:MH].rearrange("p (h o) -> p h o", o=1).to_broadcast([MH, MH, P]))
                dve.tensor_tensor(r(EXP_M), r(CUM_B), r(U_MAX), ALU.add).then_inc(sem("ml_gate_dve"), 1)

            def mlstm():
                later = cs[:, C_CAUSAL_T:C_CAUSAL_T + P].rearrange("p (o s) -> p o s", o=1).to_broadcast([P, NT, P])

                def diagonal(h):
                    dve.wait_ge(sem("ml_u"), h + 1)
                    if h:
                        dve.wait_ge(sem("ml_w"), NT * h)
                    dve.tensor_tensor(ml_diag.rearrange("p (t s) -> p t s", t=NT),
                                      ps[:, 6 + h % 2, :].rearrange("p (t s) -> p t s", t=NT), later, ALU.add)\
                       .then_inc(sem("ml_diag"), 1)

                def weights(h, j):
                    n = NT * h + j
                    dve.wait_ge(sem("ml_s"), n + 1)
                    dve.wait_ge(sem("ml_w"), n + 1)
                    if n >= 2:
                        dve.wait_ge(sem("ml_num"), n - 1)
                    cols = slice(0, (NT - j) * P)
                    dve.scalar_tensor_tensor(out=ml_at(n % 2)[:, cols], in0=ps[:, 4 + n % 2, cols], scalar=DQK ** -0.5,
                                             in1=ml_w(n % 2)[:, cols], op0=ALU.mult, op1=ALU.mult).then_inc(sem("ml_at"), 1)

                def gate_numerators(h, t):
                    dve.wait_ge(sem("ml_sums"), NT * h + t + 1)
                    o = hnt[:, t, h * DV:(h + 1) * DV]
                    dve.tensor_tensor(o, o, ps[:, t, 0:DV], ALU.mult).then_inc(sem("ml_out"), 1)

                dve.wait_ge(sem("ml_o_gained"), NT)
                diagonal(0)
                for h in range(MH):
                    for j in range(NT):
                        weights(h, j)
                        if j >= 2:
                            gate_numerators(h, j - 2)
                    if h + 1 < MH:
                        diagonal(h + 1)
                    gate_numerators(h, NT - 2)
                    gate_numerators(h, NT - 1)
                dve.wait_ge(sem("ml_out"), NT * MH)
                link(dve.scalar_tensor_tensor(out=ml_den, in0=ml_den, scalar=-1.0, in1=ml_den, op0=ALU.mult, op1=ALU.max))
                link(dve.tensor_tensor(ml_den, ml_den, ml_cols[:, 1, :], ALU.max))
                link(dve.reciprocal(ml_den, ml_den))
                link(dve.tensor_tensor(ml_scale, ml_ssq, ml_den, ALU.mult))
                link(dve.tensor_tensor(ml_scale, ml_scale, ml_den, ALU.mult))
                dve.tensor_scalar(ml_scale, ml_scale, 1.0 / DV, EPS, ALU.mult, ALU.add).then_inc(sem("ml_hvar"), 1)
                dve.wait_ge(sem("ml_hstd"), 1)
                link(dve.reciprocal(ml_scale, ml_scale))
                link(dve.tensor_tensor(ml_scale, ml_scale, ml_den, ALU.mult))
                for t in range(NT):
                    o = hnt[:, t, :].rearrange("p (h d) -> p h d", h=MH)
                    factor = ml_scale[:, t * MH:(t + 1) * MH].rearrange("p (h o) -> p h o", o=1).to_broadcast([P, MH, DV])
                    dve.tensor_tensor(o, o, factor, ALU.mult).then_inc(sem("ml_tile"), 1)
                for t in range(NT):
                    dve.wait_ge(sem("mo_tr"), 2 * t + 2)
                    dve.tensor_copy(hTk[:, 4:8, t * P:(t + 1) * P], ps[:, 5 + 2 * (t % 2), :].rearrange("p (k s) -> p k s", k=4))\
                       .then_inc(sem("mo_d"), 1)

            arena_buf = arena[:, 0:KD * ADA_W].rearrange("p (k n) -> p k n", k=KD)

            def ada_pairs(first, n):
                with dve.Fori(first // 2, (first + n) // 2) as i:
                    ada_block("a", ada_buf, 0, i, i * 2, i * 2)
                    ada_block("b", arena_buf, 1, i, i * 2 + 1, i * 2)
            for which in ("a", "b", "next"):
                dve.sem_inc(sem(f"ada_read_{which}"), GRANT)
            dve.wait_ge(sem("cond_sig"), 1)
            link(dve.tensor_tensor(cond[:, KD:2 * KD], cond[:, KD:2 * KD], cond[:, 0:KD], ALU.mult))
            dve.wait_ge(sem("bias_zeroed"), 1)
            ada_pairs(0, 8)
            dve.wait_ge(sem("consts"), 16)
            norm(0)
            ada_pairs(8, 8)
            dve.wait_ge(sem("nsa_small"), 16 * 10)
            dve.wait_ge(sem("nsa_zeroed"), 1)
            nsa_norm(0)
            nsa_norm(1)
            for t in range(2, NT):
                nsa_take_T(t - 2)
                nsa_norm(t)
            for t in range(2, NT):
                nsa_take_T(t)
            compress()
            for t in range(NT):
                cmp_softmax(t)
            attend()
            norm(1, lambda t: residual(0, t))
            routing(0)
            moe(0)

            norm(2, lambda t: combine(0, t))
            mlstm_gates()
            mlstm_rows()
            mlstm()
            norm(3, lambda t: residual(1, t))
            routing(1)
            moe(1)
            for t in range(NT):
                combine(1, t)


def constants():
    import numpy as np
    cs = np.zeros((P, C_COLS), np.float32)
    p = np.arange(P)
    cs[:, C_ID:C_ID + P] = np.eye(P)
    cs[:, C_TRI:C_TRI + P] = p[:, None] < p[None, :]
    cs[:, C_CAUSAL:C_CAUSAL + P] = np.where(p[None, :] <= p[:, None], 0.0, NEG)
    cs[:, C_CAUSAL_T:C_CAUSAL_T + P] = np.where(p[None, :] < p[:, None], -NEG, 0.0)
    slot = np.arange(NC)
    slot_end = slot * CMP_STRIDE + CMP_BLOCK - 1
    inv_freq = np.float32(500000.0) ** (-np.arange(HALF, dtype=np.float32) / np.float32(HALF))

    def angles(pos):
        a = (pos.astype(np.float32)[:, None] * inv_freq[None, :]).astype(np.float32)
        return np.concatenate([np.cos(a), np.sin(a)], 1)
    for t in range(NT):
        token = t * P + p
        cs[:, C_CMASK + t * NC:C_CMASK + (t + 1) * NC] = np.where((slot_end[None, :] <= token[:, None]) & (slot < NCMP), 0.0, NEG)
        cs[:, C_ROPE + t * ROT:C_ROPE + (t + 1) * ROT] = angles(token)
        cs[:, C_ROWOK + t] = token >= CMP_BLOCK - 1
        cs[:, C_TOKEN + t] = token - NOBODY
    cs[0:2 * NC, C_CROPE:C_CROPE + ROT] = angles(np.tile(slot_end, 2))
    cs[:, C_IOTA_E:C_IOTA_E + EXPERTS] = np.arange(EXPERTS)
    cs[:, C_IOTA_8:C_IOTA_8 + EXPERTS] = np.arange(EXPERTS) % EPG - EPG
    cs[:, C_IOTA_4:C_IOTA_4 + EGROUPS] = np.arange(EGROUPS) - EGROUPS
    cs[:, C_IOTA_OV:C_IOTA_OV + 8] = np.arange(8)
    return cs, np.arange(SLOTS, dtype=np.float32)[None, :]


_INS = ["x", "c", "ada_w", "ada_b", "norm_mix_gain", "norm_ffn_gain",
        "nsa_w_in", "nsa_w_out", "nsa_q_gain", "nsa_k_gain", "nsa_cmp_pe", "nsa_cmp_w1", "nsa_cmp_b1", "nsa_cmp_w2",
        "nsa_cmp_b2", "mlstm_w_in", "mlstm_b_igate", "mlstm_b_fgate", "mlstm_norm_gain", "mlstm_w_out",
        "router_w", "router_b", "moe_w_gate", "moe_w_up", "moe_w_down"]


def kernel(**inputs):
    import numpy as np
    import concourse.bacc as bacc
    from concourse.bass_utils import run_bass_kernel_spmd

    nc = bacc.Bacc("TRN2", target_bir_lowering=False, num_devices=1)
    host = {f"in_{name}": np.ascontiguousarray(inputs[name]) for name in _INS}
    host["in_consts"], host["in_slot_index"] = constants()
    args = [nc.dram_tensor(name, a.shape, mybir.dt.from_np(a.dtype), kind="ExternalInput").ap() for name, a in host.items()]
    result = nc.dram_tensor("out_0", (1, SEQ, D), F32, kind="ExternalOutput").ap()
    build_trunk(nc, *args, result)
    run = run_bass_kernel_spmd(nc, [host], core_ids=[0])
    return run.results[0]["out_0"]
```

```python
from contextlib import ExitStack

import concourse.bass as bass
from concourse import mybir

F32 = mybir.dt.float32
I32 = mybir.dt.int32
ALU = mybir.AluOpType
ACT = mybir.ActivationFunctionType
AX = mybir.AxisListType.X

P = 128
SEQ, D = 512, 1024
NT, KD = SEQ // P, D // P
LAYERS = 2
EPS = 1e-6
NEG = -1e30

HEADS, GROUPS, DH = 16, 2, 64
PAIRS = HEADS // 2
ROT = DH // 4
HALF = ROT // 2
CMP_BLOCK, CMP_STRIDE, CMP_HIDDEN = 32, 16, 256
NCMP = (SEQ - CMP_BLOCK) // CMP_STRIDE + 1
NC = 32
CMP_CHUNKS = CMP_BLOCK * DH // P
SEL_BLOCK, SEL_TOPN, WINDOW = 64, 8, 512
assert SEQ // SEL_BLOCK <= SEL_TOPN and WINDOW >= SEQ and NCMP < NC
NSA_COLS = HEADS * DH + 6 * GROUPS * DH + 3 * HEADS
SCALE = DH ** -0.5

MH, DQK, DV = 4, 128, 256
SOFTCAP = 15.0

EXPERTS, EGROUPS, EPG, DE = 32, 4, 8, 512
SLOTS = 128
OVERFLOW = 7
NB = EXPERTS + OVERFLOW + 1
NOBODY = SEQ

ADA_COLS = 6 * D
ADA_BLOCKS, ADA_W = 16, 384
ADA_FIRST = 6
assert ADA_BLOCKS * ADA_W == ADA_COLS
SH_M, SC_M, G_M, SH_F, SC_F, G_F = (D * i for i in range(6))
assert ADA_FIRST * ADA_W >= SC_M + D and ADA_FIRST % 2 == 0

GRANT = 1
TAKE_LAG = 3

C_ID, C_TRI, C_CAUSAL, C_CAUSAL_T, C_CMASK = 0, 128, 256, 384, 512
C_ROPE = 640
C_CROPE = C_ROPE + NT * ROT
C_ROWOK = C_CROPE + ROT
C_IOTA_E = C_ROWOK + NT
C_IOTA_8 = C_IOTA_E + EXPERTS
C_IOTA_4 = C_IOTA_8 + EXPERTS
C_TOKEN = C_IOTA_4 + EGROUPS
C_IOTA_OV = C_TOKEN + NT
C_ZERO = C_IOTA_OV + 8
C_COLS = C_ZERO + EXPERTS

AREA = 24576
SLOT = AREA // 2
UP, DOWN = KD * DE, 2 * KD * DE
A_PROB, A_PROBT = 8192, 8192 + 2048
A_KTZ = KD * NSA_COLS
A_KC = A_KTZ + 8 * SEQ
KC_ROW = 530
A_V = A_KC + 4 * KC_ROW
A_VCBD = A_V + NT * 2 * P
A_KCTZ = A_VCBD + 2 * 256
A_HGAIN = A_KCTZ + P
A_PE = A_HGAIN + 4 * DH
A_B1 = A_PE + 2 * CMP_CHUNKS
A_B2 = A_B1 + 2 * CMP_HIDDEN
A_W2 = A_B2 + 2 * DH
A_SMALL = A_W2 + 4 * DH
A_CBLK = A_SMALL + 500
assert A_KC >= SLOT and A_CBLK <= AREA

LOGITS, RANKS, SLOTS_SUMMED = 1, 2, 3
CHOSEN, HOTS, SLOTS_PLACED, ROUTED = 1, 2, 3, 4

BIAS_ZEROED, ONES_SET, NSA_ZEROED = 1, 2, 3

HIDDEN, HIDDEN_T, CMP_OUT, KEY_T = 2, 3, 4, 5
CMP_VALUES, KEY_STD = 4, 5
KEY_VAR, KEY_ROW, KEY_COLUMNS = 3, 4, 5

M_QK, M_V, M_O = 0, 8192, 16384
VROW = DV + 1
M_VALS = 0
M_ROWS = M_V
M_GAIN = M_ROWS + 7 * SEQ
M_DIAG = M_GAIN + D
M_W = M_DIAG + SEQ
M_AT = M_W + 2 * SEQ
M_SQ = M_AT + 2 * SEQ
assert M_V <= DOWN and M_VALS + NT * MH * VROW <= M_V and M_SQ + DV <= M_O

LF, CUM_B, U_IN, U_MAX, EXP_M, ZERO = range(6)

R_W, R_B = 0, KD * EXPERTS
R_AFF, R_CH, R_EQ, R_MSK, R_E1, R_E2, R_SUM, R_BLK, R_SLOT, R_F, R_TMP = (288 + 128 * i for i in range(11))
R_S = 288 + 128 * 11
R_GATE = 2304
R_SLOTS = R_GATE + D


def build_trunk(nc, x, c, ada_w, ada_b, norm_mix_gain, norm_ffn_gain,
                nsa_w_in, nsa_w_out, nsa_q_gain, nsa_k_gain, nsa_cmp_pe, nsa_cmp_w1, nsa_cmp_b1, nsa_cmp_w2, nsa_cmp_b2,
                mlstm_w_in, mlstm_b_igate, mlstm_b_fgate, mlstm_norm_gain, mlstm_w_out,
                router_w, router_b, moe_w_gate, moe_w_up, moe_w_down, consts, slot_index, out):
    x_d = x.rearrange("b (t p) d -> p (b t) d", p=P)
    out_d = out.rearrange("b (t p) d -> p (b t) d", p=P)
    gate_rows = moe_w_gate.rearrange("l e (k p) f -> p (l e) k f", p=P)
    up_rows = moe_w_up.rearrange("l e (k p) f -> p (l e) k f", p=P)
    down_rows = moe_w_down.rearrange("l e (k p) n -> p (l e) k n", p=P)
    ada_rows = ada_w.rearrange("l (p k) n -> l p k n", k=KD)
    mlstm_rows = mlstm_w_in[0].rearrange("(k p) n -> p k n", p=P)

    with ExitStack() as ctx:
        def sb(name, shape, dt=F32):
            return ctx.enter_context(nc.sbuf_tensor(name, shape, dt))

        hf_dram = [nc.dram_tensor(f"hf_{l}", (SEQ, D), F32).ap() for l in range(LAYERS)]
        z_dram = [nc.dram_tensor(f"z_{l}", (2 * SEQ, D), F32).ap() for l in range(LAYERS)]

        xs = sb("xs", [P, NT, D])
        hn = sb("hn", [P, NT * D])
        hT = sb("hT", [P, KD * SEQ])
        area = sb("area", [P, AREA])
        mods = sb("mods", [P, ADA_COLS])
        ada_buf = sb("ada_buf", [P, KD, ADA_W])
        ada_acc = sb("ada_acc", [P, 2, ADA_W])
        ada_bias = sb("ada_bias", [P, 2, ADA_W])
        arena = sb("arena", [P, 4096])
        cs = sb("cs", [P, C_COLS])
        ones = sb("ones", [P, P])
        cond = sb("cond", [P, 2 * KD])
        small = sb("small", [P, 105])
        gates = sb("gates", [P, NT * 3 * HEADS])
        slot_tok = sb("slot_tok", [P, NB], I32)
        slot_row = sb("slot_row", [P, NB], I32)
        slot_cur = sb("slot_cur", [P, 2], I32)
        row_cur = sb("row_cur", [P, 2], I32)
        route = sb("route", [P, 8], I32)

        ps = ctx.enter_context(nc.psum_tensor("ps", [P, 8, 512], F32))

        sems = {}

        def sem(name):
            if name not in sems:
                sems[name] = ctx.enter_context(nc.semaphore(name))
            return sems[name]

        ident = cs[:, C_ID:C_ID + P]
        hnt = hn[:, :].rearrange("p (t d) -> p t d", t=NT)
        hTk = hT[:, :].rearrange("p (k s) -> p k s", k=KD)
        gain_tile = [hT[:, 0:D]] + 3 * [ada_buf[:, :, :].rearrange("p k n -> p (k n)")[:, 0:D]]
        ssq, rstd, eps = small[:, 0:4], small[:, 4:8], small[:, 104:105]

        w_in0 = area[:, 0:A_KTZ].rearrange("p (k n) -> p k n", k=KD)
        w1 = area[:, 0:2 * CMP_CHUNKS * CMP_HIDDEN].rearrange("p (a m n) -> p a m n", a=2, m=CMP_CHUNKS)
        w_out = [area[:, lo:lo + KD * D].rearrange("p (k n) -> p k n", k=KD) for lo in (0, M_O)]
        prob = [area[:, lo:lo + 1024] for lo in (A_PROB, A_PROB + 1024)] + [hn[:, 0:1024], hn[:, 1024:2048]]
        prob = [v.rearrange("p (b s) -> p b s", b=2) for v in prob]
        probT = area[:, A_PROBT:A_PROBT + 2048].rearrange("p (u b s) -> p u b s", u=2, b=2)
        ktz = area[:, A_KTZ:A_KC].rearrange("p (b g r s) -> p b g r s", b=2, g=2, r=2)
        kcvT = area[:, A_KC:A_V].rearrange("p (a g s) -> p a g s", a=2, g=2)
        vals = area[:, A_V:A_VCBD].rearrange("p (t b n) -> p t b n", t=NT, b=2)
        vcbd = area[:, A_VCBD:A_KCTZ].rearrange("p (g n) -> p g n", g=2)
        kctz = area[:, A_KCTZ:A_HGAIN].rearrange("p (r n) -> p r n", r=2)
        hgain = area[:, A_HGAIN:A_PE]
        pe_t = area[:, A_PE:A_B1].rearrange("p (a m) -> p a m", a=2)
        b1_row, b2_row = area[0:1, A_B1:A_B2], area[0:1, A_B2:A_W2]
        w2 = area[:, A_W2:A_SMALL].rearrange("p (a m n) -> p a m n", a=2, m=2)
        qT = arena[:, :].rearrange("p (r s) -> p r s", r=PAIRS)
        nrm = [hn[:, 2048 * u:2048 * u + 20 * DH] for u in range(2)]
        kcv = [hn[:, 2048 * u + 1280:2048 * u + 1536] for u in range(2)]
        rope_tmp = [area[:, A_SMALL + 160 * i:A_SMALL + 160 * i + 160] for i in range(3)]
        head_ss = small[:, 12:24]
        blk = hn[:, 0:2048].rearrange("p (a m c) -> p a m c", a=2, m=CMP_CHUNKS)
        hid_c = hn[0:64, 3584:4096].rearrange("p (a n) -> p a n", a=2)
        hidT_c = hn[:, 2560:2816].rearrange("p (q c) -> p q c", q=4)
        kcn, ksq = hn[0:64, 2816:2944], hn[0:64, 2944:3008]
        pc = hn[:, 0:2048].rearrange("p (t n) -> p t n", t=NT)
        pcT = hn[:, 2048:4096].rearrange("p (t q n) -> p t q n", t=NT, q=4)

        def head_rstd(u):
            return small[:, 24 + 20 * u:44 + 20 * u]

        def neg_max(u):
            return small[:, 64 + 2 * u:66 + 2 * u]

        def raw_max(u):
            return small[:, 68 + 2 * u:70 + 2 * u]

        def sum_l(u):
            return small[:, 72 + 2 * u:74 + 2 * u]

        def inv_l(u):
            return small[:, 76 + 2 * u:78 + 2 * u]

        def cmp_r(t):
            return small[:, 80:96] if t % 2 else small[:, 24:40]

        def moe_w(k):
            return small[:, 96 + 4 * k:100 + 4 * k]

        ml_vals = area[:, M_VALS:M_VALS + NT * MH * VROW].rearrange("p (t h d) -> p t h d", t=NT, h=MH)
        ml_sel = area[0:MH, M_ROWS + 6 * SEQ:M_ROWS + 7 * SEQ].rearrange("p (h s) -> p h s", h=MH)
        ml_diag = area[:, M_DIAG:M_DIAG + SEQ]
        ml_sq = area[:, M_SQ:M_SQ + DV]
        ml_li = gates[:, 104:136].rearrange("p (t g) -> p t g", t=NT)
        ml_cols = gates[:, 136:168].rearrange("p (a n) -> p a n", a=2)

        ml_den, ml_scale, ml_ssq = small[:, 24:40], small[:, 44:60], small[:, 80:96]

        def ml_row(i):
            return area[:, M_ROWS + i * SEQ:M_ROWS + (i + 1) * SEQ]

        def ml_w(u):
            return area[:, M_W + u * SEQ:M_W + (u + 1) * SEQ]

        def ml_at(u):
            return area[:, M_AT + u * SEQ:M_AT + (u + 1) * SEQ]

        xb = [hn[:, D * u:D * u + D] for u in range(2)]
        zb = [hn[:, 2 * D + D * u:2 * D + D * u + D] for u in range(2)]
        z_in = [[v[:, D * (2 * u + k):D * (2 * u + k) + D] for k in range(2)] for v in (hn, area[:, DOWN:SLOT]) for u in range(2)]
        xbT = hT[:, 0:D].rearrange("p (k s) -> p k s", k=KD)
        hid, sig, hidT = hT[:, 1024:1536], hT[:, 1536:2048], hT[:, 2048:2560].rearrange("p (k s) -> p k s", k=4)
        ffn_gate = arena[:, R_GATE:R_GATE + D]
        n_hot = 2 * NT
        slot_hot, block_hot, block_val = (hT[:, n_hot * lo:n_hot * hi] for lo, hi in (
            (0, SLOTS), (SLOTS, SLOTS + NB), (SLOTS + NB, SLOTS + 3 * NB)))

        def w_gu(u, m):
            return area[:, u * SLOT + m * UP:u * SLOT + m * UP + UP].rearrange("p (k n) -> p k n", k=KD)

        def w_dn(u):
            return area[:, u * SLOT + DOWN:u * SLOT + DOWN + UP].rearrange("p (k n) -> p k n", k=DE // P)

        block = ctx.enter_context(nc.Block())

        @block.sync
        def _(sp):
            def ada_load(layer, buf, b_expr, which, used):
                cols = bass.ds(b_expr * ADA_W, ADA_W)
                sp.wait_ge(sem(f"ada_read_{which}"), used + GRANT)
                u = 1 if which == "b" else 0
                sp.dma_start(buf, ada_rows[layer, :, :, cols]).then_inc(sem(f"ada_loaded_{which}"), 16)
                sp.dma_start(ada_bias[0:1, u, :], ada_b[layer:layer + 1, cols]).then_inc(sem(f"ada_loaded_{which}"), 16)

            def ada_pairs(first, n):
                with sp.Fori(first // 2, (first + n) // 2) as i:
                    ada_load(0, ada_buf[:, :, :], i * 2, "a", i)
                    ada_load(0, arena[:, 0:KD * ADA_W].rearrange("p (k n) -> p k n", k=KD), i * 2 + 1, "b", i)

            def expert_load(l, e_expr, u, before):
                row = bass.ds(e_expr + l * EXPERTS, 1)
                parts = [area[:, u * SLOT + lo:u * SLOT + lo + UP].rearrange("p (e k n) -> p e k n", e=1, k=k)
                         for lo, k in ((0, KD), (UP, KD), (DOWN, DE // P))]
                if before is not None:
                    sp.wait_ge(sem(f"gu_{l}"), before * 2 - 1)
                sp.dma_start(parts[0], gate_rows[:, row, :, :]).then_inc(sem(f"wg_{l}_{u}"), 16)
                if before is not None:
                    sp.wait_ge(sem(f"gu_{l}"), before * 2)
                elif u == 1:
                    sp.wait_ge(sem(f"xb_{l}_1"), 16)
                sp.dma_start(parts[1], up_rows[:, row, :, :]).then_inc(sem(f"wu_{l}_{u}"), 16)
                if before is not None:
                    sp.wait_ge(sem(f"y_{l}"), before)
                sp.dma_start(parts[2], down_rows[:, row, :, :]).then_inc(sem(f"wd_{l}_{u}"), 16)

            def moe_loads(l):
                sp.wait_ge(sem("w_out_used"), NT * (l + 1))
                sp.dma_start(arena[:, R_W:R_B].rearrange("p (k e) -> p k e", k=KD),
                             router_w.rearrange("(k p) e -> p k e", p=P)).then_inc(sem("router_w"), 16)
                sp.dma_start(arena[:, R_B:R_B + EXPERTS],
                             router_b.rearrange("(o e) -> o e", o=1).to_broadcast([P, EXPERTS])).then_inc(sem("router_w"), 16)
                sp.dma_start(arena[:, R_SLOTS:R_SLOTS + SLOTS], slot_index.to_broadcast([P, SLOTS])).then_inc(sem("router_w"), 16)
                for t in range(NT):
                    sp.wait_ge(sem("hn_ready"), NT * (2 * l + 1) + t + 1)
                    sp.dma_start(hf_dram[l][t * P:(t + 1) * P, :], hnt[:, t, :]).then_inc(sem("hf_stored"), 16)
                expert_load(l, 0, 0, None)
                expert_load(l, 1, 1, None)
                if l == 0:
                    sp.wait_ge(sem("ffn_gate"), 1)
                with sp.Fori(1, EXPERTS // 2) as i:
                    if l == 0:
                        ada_load(1, ada_buf[:, :, :], i - 1, "next", i - 1)
                    for u in range(2):
                        expert_load(l, i * 2 + u, u, i * 2 + (u - 1))
                if l == 0:
                    ada_load(1, ada_buf[:, :, :], ADA_BLOCKS - 1, "next", ADA_BLOCKS - 1)
                    sp.wait_ge(sem("gu_0"), 2 * (EXPERTS - 1))
                    sp.dma_start(area[:, M_QK:M_V].rearrange("p (k n) -> p k n", k=KD), mlstm_rows[:, :, 0:qk]).then_inc(sem("w_qk"), 16)
                    sp.wait_ge(sem("ada_read_next"), ADA_BLOCKS + GRANT)
                    sp.dma_start(gain_tile[2], norm_mix_gain[1:2, :].to_broadcast([P, D])).then_inc(sem("norm_gain"), 16)
                sp.wait_ge(sem("route_dve"), 4 * l + ROUTED)
                n_ov = sp.value_load(route[0:1, 0:1], min_val=0, max_val=OVERFLOW)
                with sp.If(n_ov > 0), sp.Fori(0, n_ov) as j:
                    e = sp.value_load(route[0:1, bass.ds(j + 1, 1)], min_val=0, max_val=EXPERTS - 1)
                    expert_load(l, e, 1, j + EXPERTS)
                sp.wait_ge(sem(f"y_{l}"), n_ov + EXPERTS)
                sp.wait_ge(sem("z_whole"), l + 1)
                rows = z_dram[l].rearrange("(k t p) d -> p k t d", k=2, p=P)
                for t in range(NT):
                    for k in range(2):
                        sp.dma_start(z_in[t][k], rows[:, k, t, :]).then_inc(sem(f"z_in_{t}"), 16)

            qk, vo = 2 * MH * DQK, MH * DV

            sp.dma_start(cond[:, 0:KD], c.rearrange("b (p k) -> p (b k)", k=KD)).then_inc(sem("c_loaded"), 16)
            w_rows = nsa_w_in[0].rearrange("(k p) n -> p k n", p=P)

            def w_in_load(first, n):
                for k in range(first, first + n):
                    sp.dma_start(w_in0[:, k, :], w_rows[:, k, :]).then_inc(sem("w_in_0"), 16)
            sp.wait_ge(sem("filled"), BIAS_ZEROED)
            ada_pairs(0, 2)
            sp.dma_start(cs[:, :], consts).then_inc(sem("consts"), 16)
            w_in_load(0, 1)
            ada_pairs(2, 2)
            sp.dma_start(xs[:, :, :], x_d).then_inc(sem("x_ready_0"), 16)
            ada_pairs(4, ADA_FIRST - 4)
            sp.dma_start(gain_tile[0], norm_mix_gain[0:1, :].to_broadcast([P, D])).then_inc(sem("norm_gain"), 16)
            w_in_load(1, KD - 1)
            for g, src in enumerate((nsa_q_gain[0:1, :], nsa_k_gain[0, 1:2, :], nsa_k_gain[0, 2:3, :], nsa_k_gain[0, 0:1, :])):
                sp.dma_start(hgain[:, g * DH:g * DH + DH], src.to_broadcast([P, DH])).then_inc(sem("nsa_small"), 16)
            with nc.allow_non_contiguous_dma(reason="4096 position embeddings, once"):
                for a in range(2):
                    sp.dma_start(pe_t[:, a, :], nsa_cmp_pe[0, a].rearrange("(m r) d -> (r d) m", r=2))\
                      .then_inc(sem("nsa_small"), 16)
            sp.dma_start(b1_row, nsa_cmp_b1.rearrange("o a n -> o (a n)")).then_inc(sem("nsa_small"), 16)
            sp.dma_start(b2_row, nsa_cmp_b2.rearrange("o a n -> o (a n)")).then_inc(sem("nsa_small"), 16)
            for a in range(2):
                sp.dma_start(w2[:, a, :, :], nsa_cmp_w2[0, a].rearrange("(m p) n -> p m n", p=P)).then_inc(sem("nsa_small"), 16)
            ada_pairs(ADA_FIRST, ADA_BLOCKS - ADA_FIRST)
            sp.wait_ge(sem("ada_read_a"), ADA_BLOCKS // 2 + GRANT)
            sp.dma_start(gain_tile[1], norm_ffn_gain[0:1, :].to_broadcast([P, D])).then_inc(sem("norm_gain"), 16)
            sp.wait_ge(sem("proj0_ready"), 4 * NT)
            for a in range(2):
                sp.dma_start(w1[:, a, :, :], nsa_cmp_w1[0, a].rearrange("(m p) n -> p m n", p=P)).then_inc(sem("w1"), 16)
            sp.wait_ge(sem("cmp_pe"), HIDDEN)
            sp.dma_start(w_out[0], nsa_w_out[0].rearrange("(k p) n -> p k n", p=P)).then_inc(sem("w_out_loaded"), 16)
            moe_loads(0)

            sp.dma_start(gates[:, 0:64].rearrange("p (k n) -> p k n", k=KD), mlstm_rows[:, :, qk + 2 * vo:]).then_inc(sem("w_gates"), 16)
            sp.dma_start(gates[:, 96:100], mlstm_b_igate.to_broadcast([P, MH])).then_inc(sem("w_gates"), 16)
            sp.dma_start(gates[:, 100:104], mlstm_b_fgate.to_broadcast([P, MH])).then_inc(sem("w_gates"), 16)
            for t in range(NT):
                sp.wait_ge(sem(f"z_in_{t}"), 32)
            sp.dma_start(area[:, M_O:AREA].rearrange("p (k n) -> p k n", k=KD), mlstm_rows[:, :, qk + vo:qk + 2 * vo])\
              .then_inc(sem("w_o"), 16)
            sp.wait_ge(sem("x_ready_2"), NT)
            sp.dma_start(area[:, M_V:M_O].rearrange("p (k n) -> p k n", k=KD), mlstm_rows[:, :, qk:qk + vo]).then_inc(sem("w_v"), 16)
            sp.wait_ge(sem("hn_ready"), 3 * NT)
            sp.dma_start(gain_tile[3], norm_ffn_gain[1:2, :].to_broadcast([P, D])).then_inc(sem("norm_gain"), 16)
            sp.wait_ge(sem("proj1_ready"), 16)
            sp.dma_start(area[:, M_GAIN:M_GAIN + D],
                         mlstm_norm_gain.rearrange("o h d -> o (h d)").to_broadcast([P, D])).then_inc(sem("ml_gain"), 16)
            sp.wait_ge(sem("proj1_ready"), 24)
            sp.dma_start(w_out[1], mlstm_w_out[0].rearrange("(k p) n -> p k n", p=P)).then_inc(sem("w_out_loaded"), 16)
            moe_loads(1)

            for t in range(NT):
                sp.wait_ge(sem("x_ready_4"), t + 1)
                sp.dma_start(out_d[:, t, :], xs[:, t, :]).then_inc(sem("out_stored"), 16)
            sp.wait_ge(sem("out_stored"), 16 * NT)

        @block.gpsimd
        def _(pool):
            last_row = pool.to_reg(SEQ - 1)
            last_z = pool.to_reg(2 * SEQ - 1)
            pool.memset(ada_bias[:, :, :], 0.0).then_inc(sem("filled"), 1)
            pool.memset(eps, EPS)
            pool.memset(ones[:, :], 1.0).then_inc(sem("filled"), 1)
            pool.memset(area[:, A_KTZ:A_HGAIN], 0.0).then_inc(sem("filled"), 1)

            def settled():
                pool.sem_inc(sem("pool_settled"), 1)

            def norm_shift(n):
                shift = SH_F if n % 2 else SH_M
                for t in range(NT):
                    pool.wait_ge(sem("hn_scaled"), NT * n + t + 1)
                    pool.tensor_tensor(hnt[:, t, :], hnt[:, t, :], mods[:, shift:shift + D], ALU.add)\
                        .then_inc(sem("hn_ready"), 1)

            def gather(l, b_expr, u, transposed):
                src = slot_tok[:, bass.ds(b_expr, 1)]
                if transposed is not None:
                    pool.wait_ge(sem(f"xb_used_{l}"), transposed)
                pool.tensor_copy(slot_cur[:, u:u + 1], src).then_inc(sem(f"slot_cur_{l}_{u}"), 1)

            def gather_go(l, u, nth):
                pool.wait_ge(sem(f"slot_cur_{l}_{u}"), nth)
                settled()
                pool.indirect_dma_start(xb[u], None, hf_dram[l], bass.IndirectOffsetOnAxis(ap=slot_cur[:, u:u + 1], axis=0),
                                        bounds_check=last_row, oob_is_err=False).then_inc(sem(f"xb_{l}_{u}"), 16)

            def store(l, b_expr, u, stored=None):
                pool.wait_ge(sem(f"zb_{l}"), b_expr + 1 + GRANT)
                pool.tensor_copy(row_cur[:, u:u + 1], slot_row[:, bass.ds(b_expr, 1)]).then_inc(sem(f"row_cur_{l}"), 1)
                pool.wait_ge(sem(f"row_cur_{l}"), b_expr + 1)
                settled()
                pool.indirect_dma_start(z_dram[l], bass.IndirectOffsetOnAxis(ap=row_cur[:, u:u + 1], axis=0), zb[u], None,
                                        bounds_check=last_z, oob_is_err=False).then_inc(sem(stored or f"z_stored_{l}_{u}"), 16)

            def moe_pool(l):
                pool.wait_ge(sem("route_dve"), 4 * l + SLOTS_PLACED)
                pool.wait_ge(sem("hf_stored"), 16 * NT * (l + 1))
                for b in range(4):
                    gather(l, b, b % 2, b - 1 if b > 1 else None)
                    gather_go(l, b % 2, b // 2 + 1)
                with pool.Fori(2, EXPERTS // 2) as i:
                    for u in range(2):
                        gather(l, i * 2 + u, u, i * 2 + u - 1)
                        gather_go(l, u, i + 1)
                        store(l, i * 2 + u - 4, u)
                for b in range(EXPERTS - 4, EXPERTS):
                    store(l, b, b % 2)
                pool.wait_ge(sem("route_dve"), 4 * l + ROUTED)
                n_ov = pool.value_load(route[0:1, 0:1], min_val=0, max_val=OVERFLOW)
                with pool.If(n_ov > 0), pool.Fori(0, n_ov) as j:
                    gather(l, j + EXPERTS, 0, j + EXPERTS)
                    gather_go(l, 0, j + EXPERTS // 2 + 1)
                    store(l, j + EXPERTS, 0, stored=f"z_stored_{l}_ov")
                    pool.wait_ge(sem(f"z_stored_{l}_ov"), j * 16 + 16)
                    settled()
                for u in range(2):
                    pool.wait_ge(sem(f"z_stored_{l}_{u}"), 16 * (EXPERTS // 2))
                pool.sem_inc(sem("z_whole"), 1)

            norm_shift(0)
            for t in range(NT):
                pool.wait_ge(sem("pc_factor"), t + 1)
                heads = pc[:, t, :].rearrange("p (h c) -> p h c", c=NC)
                pool.tensor_tensor(heads, heads, cmp_r(t).rearrange("p (h o) -> p h o", o=1).to_broadcast([P, HEADS, NC]), ALU.mult)\
                    .then_inc(sem("pc_ready"), 1)
            norm_shift(1)
            moe_pool(0)
            norm_shift(2)
            pool.wait_ge(sem("proj1_ready"), 8)
            pool.memset(ml_vals[:, :, :, DV:VROW], 1.0).then_inc(sem("ml_ones"), 1)
            pool.wait_ge(sem("ml_gain"), 16)
            for t in range(NT):
                pool.wait_ge(sem("proj1_taken"), 16 + 2 * t + 2)
                pool.tensor_tensor(hnt[:, t, :], hnt[:, t, :], area[:, M_GAIN:M_GAIN + D], ALU.mult).then_inc(sem("ml_o_gained"), 1)
            norm_shift(3)
            moe_pool(1)

        @block.tensor
        def _(pe):
            def ada_sum(u, b):
                pe.wait_ge(sem("ada_acc"), b + 1)
                pe.wait_ge(sem("ada_mods"), b + GRANT)
                pe.matmul(ps[:, 7, 0:ADA_W], ones[:, :], ada_acc[:, u, :], start=True, stop=True).then_inc(sem("ada_summed"), 1)

            def norm_transposes(n):
                l = n // 2
                if n % 2:
                    pe.wait_ge(sem("router_w"), 48 * (l + 1))
                for t in range(NT + 1):
                    if t < NT:
                        pe.wait_ge(sem("hn_ready"), NT * n + t + 1)
                        if n % 2 and t < 2:
                            pe.wait_ge(sem("y_taken"), 2 * (NT * l + t + 3))
                        for half in range(2):
                            if t >= 2:
                                pe.wait_ge(sem(f"hT_{'ad'[half]}"), NT * n + t - 1)
                            for k in range(4):
                                ins = pe.transpose(ps[:, (t % 2) * 2 + half, k * P:(k + 1) * P],
                                                   hnt[:, t, (4 * half + k) * P:(4 * half + k + 1) * P], ident)
                            ins.then_inc(sem("hT_tr"), 1)
                    if t:
                        pe.wait_ge(sem("hT_a"), NT * n + t)
                        pe.wait_ge(sem("hT_d"), NT * n + t)
                        if n % 2:
                            router(t - 1)

            def router(t):
                for k in range(KD):
                    ins = pe.matmul(ps[:, 6, t * EXPERTS:(t + 1) * EXPERTS], hTk[:, k, t * P:(t + 1) * P],
                                    arena[:, R_W + k * EXPERTS:R_W + (k + 1) * EXPERTS], start=(k == 0), stop=(k == KD - 1))
                if t == NT - 1:
                    ins.then_inc(sem("route_pe"), 1)

            def nsa_project(t, g):
                cols = slice(512 * g, min(512 * g + 512, NSA_COLS))
                if t:
                    pe.wait_ge(sem("proj0_taken"), 4 * (t - 1) + g + 1)
                for k in range(KD):
                    ins = pe.matmul(ps[:, g, 0:cols.stop - cols.start], hTk[:, k, t * P:(t + 1) * P], w_in0[:, k, cols],
                                    start=(k == 0), stop=(k == KD - 1))
                ins.then_inc(sem("proj0_ready"), 1)

            def kcv_transposes(t):
                pe.wait_ge(sem("proj0_taken"), 4 * t + 3)
                pe.wait_ge(sem("ada_mods"), ADA_BLOCKS + GRANT)
                if t:
                    pe.wait_ge(sem("kcv_taken"), t)
                for a in range(2):
                    ins = pe.transpose(ps[:, 7, a * P:(a + 1) * P], kcv[t % 2][:, a * P:(a + 1) * P], ident)
                ins.then_inc(sem("kcv_tr"), 1)

            def nsa_transposes(t):
                pe.wait_ge(sem("nrm_ready"), t + 1)
                if t:
                    pe.wait_ge(sem("qT_a"), t)
                    pe.wait_ge(sem("qT_d"), t)
                for pr in range(PAIRS):
                    pe.transpose(ps[:, 4 + pr // 4, (pr % 4) * P:(pr % 4 + 1) * P], nrm[t % 2][:, pr * P:(pr + 1) * P], ident)
                for b in range(2):
                    ins = pe.transpose(ps[:, 6, b * P:(b + 1) * P], nrm[t % 2][:, 1024 + b * P:1024 + (b + 1) * P], ident)
                ins.then_inc(sem("nsa_tr"), 1)

            def compress():
                pe.wait_ge(sem("w1"), 32)
                pe.wait_ge(sem("nsa_small"), 16 * 10)
                for a in range(2):
                    pe.wait_ge(sem("cmp_dve"), a + 1)
                    for m in range(CMP_CHUNKS):
                        pe.matmul(ps[0:64, a, 0:CMP_HIDDEN], blk[:, a, m, :], w1[:, a, m, :], start=(m == 0), stop=False)
                    pe.matmul(ps[0:64, a, 0:CMP_HIDDEN], ones[0:1, 0:64], b1_row[:, a * CMP_HIDDEN:(a + 1) * CMP_HIDDEN],
                              start=False, stop=True).then_inc(sem("cmp_pe"), 1)
                nsa_transposes(NT - 1)
                for a in range(2):
                    pe.wait_ge(sem("cmp_act"), a + 1)
                    for m in range(2):
                        ins = pe.transpose(ps[:, 2, (2 * a + m) * 64:(2 * a + m + 1) * 64], hid_c[:, a, m * P:(m + 1) * P],
                                           ident[0:64, 0:64])
                ins.then_inc(sem("cmp_pe"), 1)
                pe.wait_ge(sem("cmp_act"), HIDDEN_T)
                for a in range(2):
                    for m in range(2):
                        pe.matmul(ps[0:64, 3 + a, 0:DH], hidT_c[:, 2 * a + m, :], w2[:, a, m, :],
                                  start=(m == 0), stop=False)
                    ins = pe.matmul(ps[0:64, 3 + a, 0:DH], ones[0:1, 0:64], b2_row[:, a * DH:(a + 1) * DH],
                                    start=False, stop=True)
                ins.then_inc(sem("cmp_pe"), 1)
                pe.wait_ge(sem("cmp_dve"), KEY_ROW)
                pe.transpose(ps[:, 0, 0:64], kcn, ident[0:64, 0:64]).then_inc(sem("cmp_pe"), 1)
                pe.wait_ge(sem("cmp_dve"), KEY_COLUMNS)

            def cmp_scores(t):
                if t >= 2:
                    pe.wait_ge(sem("cmp_s_read"), t - 1)
                for pr in range(PAIRS):
                    g = pr // (PAIRS // 2)
                    ins = pe.matmul(ps[:, 1 + t % 2, pr * 64:(pr + 1) * 64].rearrange("p (r c) -> p r c", r=2),
                                    qT[:, pr, t * P:(t + 1) * P],
                                    kctz[:, :, g * NC:(g + 1) * NC], start=True, stop=True)
                ins.then_inc(sem("cmp_s"), 1)

            def cmp_transposes(t):
                pe.wait_ge(sem("pc_ready"), t + 1)
                if t >= 2:
                    pe.wait_ge(sem("pcT_ready"), t - 1)
                for q in range(4):
                    ins = pe.transpose(ps[:, 4 + t % 2, q * P:(q + 1) * P], pc[:, t, q * P:(q + 1) * P], ident)
                ins.then_inc(sem("pc_tr"), 1)

            units = [(t, h) for t in range(NT) for h in range(HEADS)]

            def scores(n):
                t, h = units[n]
                if n >= 2:
                    pe.wait_ge(sem("exp_done"), n - 1)
                for b in range(2):
                    ins = pe.matmul(ps[:, 2 * (n % 2) + b, 0:(t + 1) * P], qT[:, h // 2, t * P:(t + 1) * P],
                                    ktz[:, b, h // 8, h % 2, 0:(t + 1) * P], start=True, stop=True)
                ins.then_inc(sem("scores"), 1)

            def prob_transposes(n):
                t, h = units[n]
                pe.wait_ge(sem("prob_ready"), n + 1)
                if n:
                    pe.wait_ge(sem("probT"), n)
                for b in range(2):
                    for j in range(t + 1):
                        ins = pe.transpose(ps[:, 4 + b, j * P:(j + 1) * P], prob[n % 4][:, b, j * P:(j + 1) * P], ident)
                ins.then_inc(sem("prob_tr"), 1)

            def weighted_values(n):
                t, h = units[n]
                pr, r = n // 2, h % 2
                bank = 6 + pr % 2
                pe.wait_ge(sem("probT"), n + 1)
                if r == 0:
                    if pr >= 2:
                        pe.wait_ge(sem("oT_ready"), pr - 1)
                    quad, half = h // 4, (h // 2) % 2
                    pe.matmul(ps[:, bank, 0:P], vcbd[:, h // 8, half * P:(half + 1) * P], pcT[:, t, quad, :],
                              start=True, stop=False, skip_group_check=True)
                for b in range(2):
                    for j in range(t + 1):
                        ins = pe.matmul(ps[r * 64:(r + 1) * 64, bank, 0:P], vals[:, j, b, (h // 8) * DH:(h // 8 + 1) * DH],
                                        probT[:, n % 2, b, j * P:(j + 1) * P], start=False,
                                        stop=(b == 1 and j == t), skip_group_check=True)
                ins.then_inc(sem("pv"), 1)

            def out_project(l):
                pe.wait_ge(sem("w_out_loaded"), 16 * (l + 1))
                for t in range(NT):
                    for half in range(2):
                        if t >= 2:
                            pe.wait_ge(sem("y_taken"), 2 * (NT * l + t - 2) + half + 1)
                        for k in range(KD):
                            ins = pe.matmul(ps[:, 2 * (t % 2) + half, :], hTk[:, k, t * P:(t + 1) * P],
                                            w_out[l][:, k, half * 512:(half + 1) * 512], start=(k == 0), stop=(k == KD - 1))
                        ins.then_inc(sem("y_ready"), 1)

            def place(l):
                pe.wait_ge(sem("route_dve"), 4 * l + CHOSEN)
                total = arena[:, R_SUM:R_SUM + P + EXPERTS]
                pe.matmul(ps[:, 6, P:2 * P + EXPERTS], cs[:, C_TRI:C_TRI + P], total, start=True, stop=False, skip_group_check=True)
                for back in range(NT, 0, -1):
                    n = (NT + 1 - back) * EXPERTS
                    ins = pe.matmul(ps[:, 6, P + back * EXPERTS:P + (NT + 1) * EXPERTS], ones[:, :], total[:, 0:n],
                                    start=False, stop=(back == 1), skip_group_check=True)
                ins.then_inc(sem("route_pe"), 1)
                pe.wait_ge(sem("route_dve"), 4 * l + HOTS)
                for i in range(2 * NT):
                    ins = pe.matmul(ps[:, 6, 384:384 + 2 * NB], slot_hot[:, i * SLOTS:(i + 1) * SLOTS],
                                    block_val[:, i * 2 * NB:(i + 1) * 2 * NB],
                                    start=(i == 0), stop=(i == 2 * NT - 1), skip_group_check=True)
                ins.then_inc(sem("route_pe"), 1)

            def x_transposes(l, u, nth, b):
                pe.wait_ge(sem(f"xb_{l}_{u}"), nth * 16 + 16)
                pe.wait_ge(sem(f"xbT_a_{l}"), b)
                pe.wait_ge(sem(f"xbT_d_{l}"), b)
                for k in range(KD):
                    ins = pe.transpose(ps[:, 2 + k // 4, (k % 4) * P:(k % 4 + 1) * P], xb[u][:, k * P:(k + 1) * P], ident)
                ins.then_inc(sem(f"xb_used_{l}"), 1)

            def gate_up(l, u, nth, b):
                pe.wait_ge(sem(f"xbT_a_{l}"), b + 1)
                pe.wait_ge(sem(f"xbT_d_{l}"), b + 1)
                pe.wait_ge(sem(f"hid_{l}"), b)
                for m in range(2):
                    pe.wait_ge(sem(f"w{'gu'[m]}_{l}_{u}"), nth * 16 + 16)
                    for k in range(KD):
                        ins = pe.matmul(ps[:, m, :], xbT[:, k, :], w_gu(u, m)[:, k, :], start=(k == 0), stop=(k == KD - 1))
                    ins.then_inc(sem(f"gu_{l}"), 1)

            def hid_transposes(l, b):
                pe.wait_ge(sem(f"hid_{l}"), b + 1)
                pe.wait_ge(sem(f"hidT_{l}"), b)
                for k in range(4):
                    ins = pe.transpose(ps[:, 6, k * P:(k + 1) * P], hid[:, k * P:(k + 1) * P], ident)
                ins.then_inc(sem(f"hid_tr_{l}"), 1)

            def down(l, u, nth, b):
                pe.wait_ge(sem(f"wd_{l}_{u}"), nth * 16 + 16)
                pe.wait_ge(sem(f"hidT_{l}"), b + 1)
                pe.wait_ge(sem(f"zb_{l}"), b + GRANT)
                for half in range(2):
                    for k in range(4):
                        ins = pe.matmul(ps[:, 4 + half, :], hidT[:, k, :], w_dn(u)[:, k, half * 512:(half + 1) * 512],
                                        start=(k == 0), stop=(k == 3))
                ins.then_inc(sem(f"y_{l}"), 1)

            def moe(l):
                place(l)
                x_transposes(l, 0, 0, 0)
                gate_up(l, 0, 0, 0)
                x_transposes(l, 1, 0, 1)
                hid_transposes(l, 0)

                def step(u, nth, b, prev_nth, next_nth):
                    gate_up(l, u, nth, b)
                    if next_nth is not None:
                        x_transposes(l, 1 - u, next_nth, b + 1)
                    down(l, 1 - u, prev_nth, b - 1)
                    hid_transposes(l, b)
                with pe.Fori(0, EXPERTS // 2 - 1) as i:
                    step(1, i, i * 2 + 1, i, i + 1)
                    if l == 0:
                        ada_sum(0, i + ADA_BLOCKS)
                    step(0, i + 1, i * 2 + 2, i, i + 1)
                last = EXPERTS - 1
                step(1, last // 2, last, last // 2, None)
                if l == 0:
                    ada_sum(0, 2 * ADA_BLOCKS - 1)
                down(l, 1, last // 2, last)
                pe.wait_ge(sem("route_dve"), 4 * l + ROUTED)
                n_ov = pe.value_load(route[0:1, 0:1], min_val=0, max_val=OVERFLOW)
                with pe.If(n_ov > 0), pe.Fori(0, n_ov) as j:
                    x_transposes(l, 0, j + EXPERTS // 2, j + EXPERTS)
                    gate_up(l, 1, j + EXPERTS // 2, j + EXPERTS)
                    hid_transposes(l, j + EXPERTS)
                    down(l, 1, j + EXPERTS // 2, j + EXPERTS)

            def mlstm_project():
                def begin(job):
                    if job >= 4:
                        pe.wait_ge(sem("proj1_taken"), job - 3)
                    return ps[:, job % 4, :]
                pe.wait_ge(sem("w_qk"), 16)
                w = area[:, M_QK:M_V].rearrange("p (k n) -> p k n", k=KD)
                for r in range(2 * MH):
                    o = begin(r)
                    for k in range(KD):
                        ins = pe.matmul(o, w[:, k, r * P:(r + 1) * P], hTk[:, k, :], start=(k == 0), stop=(k == KD - 1))
                    ins.then_inc(sem("proj1_ready"), 1)
                pe.wait_ge(sem("w_gates"), 48)
                wg = gates[:, 0:64].rearrange("p (k n) -> p k n", k=KD)
                for t in range(NT):
                    for k in range(KD):
                        ins = pe.matmul(ps[:, 4, t * 8:(t + 1) * 8], hTk[:, k, t * P:(t + 1) * P], wg[:, k, :],
                                        start=(k == 0), stop=(k == KD - 1))
                ins.then_inc(sem("ml_gate_pe"), 1)
                for part, (name, lo) in enumerate((("w_v", M_V), ("w_o", M_O))):
                    pe.wait_ge(sem(name), 16)
                    w = area[:, lo:lo + KD * D].rearrange("p (k n) -> p k n", k=KD)
                    for t in range(NT):
                        for half in range(2):
                            o = begin(8 + 8 * part + 2 * t + half)
                            for k in range(KD):
                                ins = pe.matmul(o, hTk[:, k, t * P:(t + 1) * P], w[:, k, half * 512:(half + 1) * 512],
                                                start=(k == 0), stop=(k == KD - 1))
                            ins.then_inc(sem("proj1_ready"), 1)
                    if part == 0:
                        pe.wait_ge(sem("ml_gate_dve"), 2)
                        for t in range(NT):
                            pe.transpose(ps[0:MH, 5, t * P:(t + 1) * P], ml_li[:, t, MH:2 * MH], ident)
                            ins = pe.transpose(ps[0:MH, 6, t * P:(t + 1) * P], ml_li[:, t, 0:MH], ident)
                        ins.then_inc(sem("ml_gate_pe"), 1)

            def mlstm():
                pe.wait_ge(sem("ml_gate_act"), 2)
                for t in range(NT):
                    pe.transpose(ps[:, 7, t * MH:(t + 1) * MH], ml_row(U_IN)[0:MH, t * P:(t + 1) * P], ident[0:MH, 0:MH])
                    ins = pe.transpose(ps[:, 7, 64 + t * MH:64 + (t + 1) * MH], ml_row(EXP_M)[0:MH, t * P:(t + 1) * P],
                                       ident[0:MH, 0:MH])
                ins.then_inc(sem("ml_gate_pe"), 1)
                pe.wait_ge(sem("ml_ones"), 1)
                def ml_u(h):
                    if h < 2:
                        pe.wait_ge(sem("ml_gate_act"), 3)
                    else:
                        pe.wait_ge(sem("ml_w"), NT * (h - 1))
                        pe.wait_ge(sem("ml_diag"), h - 1)
                    pe.matmul(ps[:, 6 + h % 2, :], ml_sel[:, h, :], ml_row(U_MAX)[0:MH, :], start=True, stop=True)\
                      .then_inc(sem("ml_u"), 1)

                ml_u(0)
                pe.wait_ge(sem("proj1_taken"), 24)
                for h in range(MH):
                    def ml_scores(j):
                        n = NT * h + j
                        if n >= 2:
                            pe.wait_ge(sem("ml_at"), n - 1)
                        pe.matmul(ps[:, 4 + n % 2, 0:(NT - j) * P], qT[:, MH + h, j * P:(j + 1) * P], qT[:, h, j * P:SEQ],
                                  start=True, stop=True).then_inc(sem("ml_s"), 1)

                    def ml_values(j):
                        n = NT * h + j
                        pe.wait_ge(sem("ml_at"), n + 1)
                        for t in reversed(range(j, NT)):
                            if j == 0 and h:
                                pe.wait_ge(sem("ml_out"), NT * (h - 1) + t + 1)
                            ins = pe.matmul(ps[:, t, 0:VROW], ml_at(n % 2)[:, (t - j) * P:(t - j + 1) * P], ml_vals[:, j, h, :],
                                            start=(j == 0), stop=(j == t))
                        ins.then_inc(sem("ml_num"), 1)
                    ml_scores(0)
                    for j in range(NT):
                        if j + 1 < NT:
                            ml_scores(j + 1)
                        ml_values(j)
                        if j == 1 and h + 1 < MH:
                            ml_u(h + 1)
                for t in range(NT):
                    pe.wait_ge(sem("ml_tile"), t + 1)
                    if t == 0:
                        pe.wait_ge(sem("ml_at"), NT * MH)
                        pe.wait_ge(sem("ml_diag"), MH)
                    for half in range(2):
                        if t >= 2:
                            pe.wait_ge(sem(f"mo_{'ad'[half]}"), t - 1)
                        for k in range(4):
                            ins = pe.transpose(ps[:, 4 + 2 * (t % 2) + half, k * P:(k + 1) * P],
                                               hnt[:, t, (4 * half + k) * P:(4 * half + k + 1) * P], ident)
                        ins.then_inc(sem("mo_tr"), 1)
                pe.wait_ge(sem("mo_a"), NT)
                pe.wait_ge(sem("mo_d"), NT)

            pe.sem_inc(sem("ada_summed"), GRANT)
            pe.wait_ge(sem("filled"), ONES_SET)
            with pe.Fori(0, ADA_FIRST // 2) as i:
                for u in range(2):
                    ada_sum(u, i * 2 + u)
            pe.wait_ge(sem("consts"), 16)
            norm_transposes(0)
            pe.wait_ge(sem("w_in_0"), 16 * KD)
            for i in range(8):
                nsa_project(i // 4, i % 4)
                ada_sum(i % 2, ADA_FIRST + i)
            for g in range(4):
                nsa_project(2, g)
                if ADA_FIRST + 8 + g < ADA_BLOCKS:
                    ada_sum(g % 2, ADA_FIRST + 8 + g)
            kcv_transposes(0)
            nsa_transposes(0)
            for g in range(4):
                nsa_project(3, g)
            kcv_transposes(1)
            nsa_transposes(1)
            kcv_transposes(2)
            nsa_transposes(2)
            kcv_transposes(3)
            compress()
            pe.wait_ge(sem("qT_a"), NT)
            pe.wait_ge(sem("qT_d"), NT)
            for t in range(NT + 2):
                if t < NT:
                    cmp_scores(t)
                if t >= 2:
                    cmp_transposes(t - 2)
            pe.wait_ge(sem("pcT_ready"), NT)
            pe.wait_ge(sem("cmp_act"), CMP_VALUES)
            pe.wait_ge(sem("ada_mods"), ADA_BLOCKS + GRANT)
            for n in range(len(units) + 4):
                if n < len(units):
                    scores(n)
                if 3 <= n < len(units) + 3:
                    prob_transposes(n - 3)
                if n >= 4:
                    weighted_values(n - 4)
            pe.wait_ge(sem("oT_ready"), NT * PAIRS)
            out_project(0)
            norm_transposes(1)
            moe(0)

            norm_transposes(2)
            mlstm_project()
            mlstm()
            out_project(1)
            norm_transposes(3)
            moe(1)

        @block.scalar
        def _(act):
            count = [0]

            def link(ins):
                count[0] += 1
                ins.then_inc(sem("act_chain"), 1)
                act.wait_ge(sem("act_chain"), count[0])

            def ada_take(b):
                act.wait_ge(sem("ada_summed"), b + 1 + GRANT)
                act.activation(mods[:, bass.ds(b * ADA_W, ADA_W)], ps[:, 7, 0:ADA_W], ACT.Copy).then_inc(sem("ada_mods"), 1)

            def norm(n):
                act.wait_ge(sem("filled"), ONES_SET)
                for t in range(NT + TAKE_LAG):
                    if t < NT:
                        act.wait_ge(sem(f"x_ready_{n}"), 16 if n == 0 else t + 1)
                        link(act.activation(ps[:, 4:6, :], xs[:, t, :].rearrange("p (a n) -> p a n", a=2), ACT.Square,
                                            accum_out=ssq[:, t:t + 1]))
                        act.activation(rstd[:, t:t + 1], ssq[:, t:t + 1], ACT.Sqrt, bias=eps, scale=1.0 / D)\
                           .then_inc(sem("norm_std"), 1)
                    if t >= TAKE_LAG:
                        norm_take(n, t - TAKE_LAG)

            def norm_take(n, t):
                act.wait_ge(sem("hT_tr"), 2 * (NT * n + t) + 1)
                act.activation(hTk[:, 0:4, t * P:(t + 1) * P], ps[:, (t % 2) * 2, :].rearrange("p (k s) -> p k s", k=4),
                               ACT.Copy).then_inc(sem("hT_a"), 1)

            def nsa_take(t, g):
                u = t % 2
                if t >= 2:
                    act.wait_ge(sem("nsa_tr"), t - 1)
                    act.wait_ge(sem("kcv_tr"), t - 1)
                act.wait_ge(sem("filled"), NSA_ZEROED)
                act.wait_ge(sem("proj0_ready"), 4 * t + g + 1)
                if g < 2:
                    ins = act.activation(nrm[u][:, 512 * g:512 * g + 512], ps[:, g, :], ACT.Copy)
                elif g == 2:
                    act.activation(kcv[u], ps[:, 2, 0:256], ACT.Copy)
                    act.activation(nrm[u][:, 1024:1152], ps[:, 2, 256:384], ACT.Copy)
                    ins = act.activation(vals[:, t, 0, :], ps[:, 2, 384:512], ACT.Copy)
                else:
                    act.activation(nrm[u][:, 1152:1280], ps[:, 3, 0:128], ACT.Copy)
                    act.activation(vals[:, t, 1, :], ps[:, 3, 128:256], ACT.Copy)
                    ins = act.activation(gates[:, t * 48:(t + 1) * 48], ps[:, 3, 256:304], ACT.Sigmoid)
                ins.then_inc(sem("proj0_taken"), 1)

            def nsa_std(t):
                act.wait_ge(sem("head_var"), t + 1)
                act.activation(head_rstd(t % 2), head_rstd(t % 2), ACT.Sqrt).then_inc(sem("head_std"), 1)

            def nsa_take_T(t):
                act.wait_ge(sem("nsa_tr"), t + 1)
                act.activation(qT[:, 0:4, t * P:(t + 1) * P], ps[:, 4, :].rearrange("p (r s) -> p r s", r=4), ACT.Copy)\
                   .then_inc(sem("qT_a"), 1)

            def kcv_take(t):
                act.wait_ge(sem("kcv_tr"), t + 1)
                src = ps[:, 7, 0:256].rearrange("p (a s) -> p a s", a=2)
                for g in range(2):
                    rows = slice(64 * g, 64 * g + 64)
                    act.activation(kcvT[0:64, :, g, t * P + 1:t * P + 1 + P], src[rows, :, :], ACT.Copy)
                    ins = act.activation(kcvT[64:128, :, g, t * P:t * P + P], src[rows, :, :], ACT.Copy)
                ins.then_inc(sem("kcv_taken"), 1)

            def compress():
                for a in range(2):
                    act.wait_ge(sem("cmp_pe"), a + 1)
                    act.activation(hid_c[:, a, :], ps[0:64, a, 0:CMP_HIDDEN], ACT.Gelu_apprx_tanh).then_inc(sem("cmp_act"), 1)
                nsa_take_T(NT - 1)
                act.wait_ge(sem("cmp_pe"), HIDDEN_T)
                act.activation(hidT_c, ps[:, 2, 0:256].rearrange("p (q c) -> p q c", q=4), ACT.Copy).then_inc(sem("cmp_act"), 1)
                act.wait_ge(sem("cmp_pe"), CMP_OUT)
                for g in range(2):
                    for j in range(4):
                        ins = act.activation(vcbd[32 * j:32 * j + 32, g, 64 * j:64 * j + 64], ps[32 * g:32 * g + 32, 4, 0:DH],
                                             ACT.Copy)
                ins.then_inc(sem("cmp_act"), 1)
                act.wait_ge(sem("cmp_dve"), KEY_VAR)
                act.activation(head_ss[0:64, 1:2], head_ss[0:64, 1:2], ACT.Sqrt).then_inc(sem("cmp_act"), 1)

            def cmp_exp(t):
                act.wait_ge(sem("pc_shifted"), t + 1)
                act.activation(pc[:, t, :], pc[:, t, :], ACT.Exp).then_inc(sem("pc_exp"), 1)

            def cmp_take(t):
                act.wait_ge(sem("pc_tr"), t + 1)
                act.activation(pcT[:, t, :, :], ps[:, 4 + t % 2, :].rearrange("p (q n) -> p q n", q=4), ACT.Copy)\
                   .then_inc(sem("pcT_ready"), 1)

            units = [(t, h) for t in range(NT) for h in range(HEADS)]

            def attend():
                for n in range(len(units) + 4):
                    if 3 <= n < len(units) + 3:
                        m = n - 3
                        t, h = units[m]
                        act.wait_ge(sem("prob_tr"), m + 1)
                        if m >= 2:
                            act.wait_ge(sem("pv"), m - 1)
                        act.activation(probT[:, m % 2, :, 0:(t + 1) * P], ps[:, 4:6, 0:(t + 1) * P], ACT.Copy)\
                           .then_inc(sem("probT"), 1)
                    if n < len(units):
                        t, h = units[n]
                        act.wait_ge(sem("neg_max"), n + 1)
                        if n >= 4:
                            act.wait_ge(sem("prob_tr"), n - 3)
                        for b in range(2):
                            ins = act.activation(prob[n % 4][:, b, 0:(t + 1) * P], ps[:, 2 * (n % 2) + b, 0:(t + 1) * P],
                                                 ACT.Exp, bias=neg_max(n % 2)[:, b:b + 1], scale=SCALE,
                                                 accum_out=sum_l(n % 2)[:, b:b + 1])
                        ins.then_inc(sem("exp_done"), 1)
                    if n >= 4 and (n - 4) % 2:
                        m = n - 4
                        t, h = units[m]
                        act.wait_ge(sem("pv"), m + 1)
                        act.activation(hTk[:, h // 2, t * P:(t + 1) * P], ps[:, 6 + (m // 2) % 2, 0:P], ACT.Copy)\
                           .then_inc(sem("oT_ready"), 1)

            def moe(l):
                act.wait_ge(sem("route_pe"), 3 * l + LOGITS)
                act.activation(arena[:, R_AFF:R_AFF + P], ps[:, 6, 0:P], ACT.Sigmoid).then_inc(sem("affinity"), 1)
                act.activation(ffn_gate, mods[:, G_F:G_F + D], ACT.Copy).then_inc(sem("ffn_gate"), 1)

                def take_x(b):
                    act.wait_ge(sem(f"xb_used_{l}"), b + 1)
                    act.activation(xbT[:, 0:4, :], ps[:, 2, :].rearrange("p (k s) -> p k s", k=4), ACT.Copy)\
                       .then_inc(sem(f"xbT_a_{l}"), 1)

                def sigmoid(b):
                    act.wait_ge(sem(f"gu_{l}"), b * 2 + 1)
                    act.activation(sig, ps[:, 0, :], ACT.Sigmoid).then_inc(sem(f"sig_{l}"), 1)
                    act.wait_ge(sem(f"gu_{l}"), b * 2 + 2)

                def take_hid(b):
                    act.wait_ge(sem(f"hid_tr_{l}"), b + 1)
                    act.activation(hidT, ps[:, 6, :].rearrange("p (k s) -> p k s", k=4), ACT.Copy).then_inc(sem(f"hidT_{l}"), 1)

                take_x(0)
                sigmoid(0)
                take_x(1)
                take_hid(0)

                def step(b, last=False):
                    sigmoid(b)
                    if not last:
                        take_x(b + 1)
                    take_hid(b)
                with act.Fori(0, EXPERTS // 2 - 1) as i:
                    step(i * 2 + 1)
                    if l == 0:
                        act.wait_ge(sem("ada_summed"), i + ADA_BLOCKS + 1 + GRANT)
                        act.activation(mods[:, bass.ds(i * ADA_W, ADA_W)], ps[:, 7, 0:ADA_W], ACT.Copy).then_inc(sem("ada_mods"), 1)
                    step(i * 2 + 2)
                step(EXPERTS - 1, last=True)
                if l == 0:
                    act.wait_ge(sem("ada_summed"), 2 * ADA_BLOCKS + GRANT)
                    act.activation(mods[:, (ADA_BLOCKS - 1) * ADA_W:ADA_COLS], ps[:, 7, 0:ADA_W], ACT.Copy)\
                       .then_inc(sem("ada_mods"), 1)
                act.wait_ge(sem("route_dve"), 4 * l + ROUTED)
                n_ov = act.value_load(route[0:1, 0:1], min_val=0, max_val=OVERFLOW)
                with act.If(n_ov > 0), act.Fori(0, n_ov) as j:
                    take_x(j + EXPERTS)
                    sigmoid(j + EXPERTS)
                    take_hid(j + EXPERTS)

            def mlstm_take(job):
                act.wait_ge(sem("proj1_ready"), job + 1)
                src = ps[:, job % 4, :]
                if job < 8:
                    ins = act.activation(qT[:, job, :], src, ACT.Copy)
                elif job < 16:
                    t, half = divmod(job - 8, 2)
                    ins = act.activation(ml_vals[:, t, 2 * half:2 * half + 2, 0:DV], src.rearrange("p (h d) -> p h d", h=2), ACT.Copy)
                else:
                    t, half = divmod(job - 16, 2)
                    ins = act.activation(hnt[:, t, half * 512:(half + 1) * 512], src, ACT.Sigmoid)
                ins.then_inc(sem("proj1_taken"), 1)

            def mlstm_gates():
                act.wait_ge(sem("ml_gate_dve"), 1)
                link(act.activation(ml_li, ml_li, ACT.Tanh, scale=1.0 / SOFTCAP))
                link(act.activation(ml_li[:, :, MH:2 * MH], ml_li[:, :, MH:2 * MH], ACT.Exp, scale=-SOFTCAP))
                act.activation(ml_li[:, :, MH:2 * MH], ml_li[:, :, MH:2 * MH], ACT.Ln, bias=1.0).then_inc(sem("ml_gate_act"), 1)

            def mlstm():
                act.wait_ge(sem("ml_gate_dve"), 3)
                act.activation(ml_row(EXP_M)[0:MH, :], ml_row(EXP_M)[0:MH, :], ACT.Exp, scale=-1.0).then_inc(sem("ml_gate_act"), 1)
                act.wait_ge(sem("ml_gate_pe"), 3)
                act.activation(ml_cols, ps[:, 7, 0:128].rearrange("p (a n) -> p a n", a=2)[:, :, 0:16], ACT.Copy)\
                   .then_inc(sem("ml_gate_act"), 1)
                act.wait_ge(sem("ml_gate_act"), 3)
                for h in range(MH):
                    act.wait_ge(sem("ml_u"), h + 1)
                    act.wait_ge(sem("ml_diag"), h + 1)
                    for j in range(NT):
                        n = NT * h + j
                        if n >= 2:
                            act.wait_ge(sem("ml_at"), n - 1)
                        u_col = ml_cols[:, 0, j * MH + h:j * MH + h + 1]
                        ins = act.activation(ml_w(n % 2)[:, 0:P], ml_diag[:, j * P:(j + 1) * P], ACT.Exp, bias=u_col, scale=-1.0)
                        if j < NT - 1:
                            ins = act.activation(ml_w(n % 2)[:, P:(NT - j) * P], ps[:, 6 + h % 2, (j + 1) * P:SEQ], ACT.Exp,
                                                 bias=u_col, scale=-1.0)
                        ins.then_inc(sem("ml_w"), 1)
                    for t in range(NT):
                        at = t * MH + h
                        act.wait_ge(sem("ml_num"), NT * h + t + 1)
                        act.activation(ml_den[:, at:at + 1], ps[:, t, DV:VROW], ACT.Copy)
                        if h + t:
                            act.wait_ge(sem("ml_sums"), NT * h + t)
                        act.activation(ml_sq, ps[:, t, 0:DV], ACT.Square, accum_out=ml_ssq[:, at:at + 1]).then_inc(sem("ml_sums"), 1)
                act.wait_ge(sem("ml_hvar"), 1)
                act.activation(ml_scale, ml_scale, ACT.Sqrt).then_inc(sem("ml_hstd"), 1)
                for t in range(NT):
                    act.wait_ge(sem("mo_tr"), 2 * t + 1)
                    act.activation(hTk[:, 0:4, t * P:(t + 1) * P], ps[:, 4 + 2 * (t % 2), :].rearrange("p (k s) -> p k s", k=4),
                                   ACT.Copy).then_inc(sem("mo_a"), 1)

            act.sem_inc(sem("ada_mods"), GRANT)
            act.wait_ge(sem("c_loaded"), 16)
            act.activation(cond[:, KD:2 * KD], cond[:, 0:KD], ACT.Sigmoid).then_inc(sem("cond_sig"), 1)
            with act.Fori(0, ADA_FIRST) as b:
                ada_take(b)
            norm(0)
            for i in range(8):
                nsa_take(i // 4, i % 4)
                ada_take(ADA_FIRST + i)
            for b in range(ADA_FIRST + 8, ADA_BLOCKS):
                ada_take(b)
            nsa_std(0)
            nsa_std(1)
            for t in range(2, NT):
                kcv_take(t - 2)
                nsa_take_T(t - 2)
                for g in range(4):
                    nsa_take(t, g)
                if t < NT - 1:
                    nsa_std(t)
            kcv_take(2)
            kcv_take(3)
            nsa_take_T(2)
            nsa_std(NT - 1)
            compress()
            for t in range(NT + 2):
                if t < NT:
                    cmp_exp(t)
                if t >= 2:
                    cmp_take(t - 2)
            attend()
            norm(1)
            moe(0)

            norm(2)
            for job in range(8):
                mlstm_take(job)
            mlstm_gates()
            for job in range(8, 24):
                mlstm_take(job)
            mlstm()
            norm(3)
            moe(1)

        @block.vector
        def _(dve):
            count = [0]

            def link(ins):
                count[0] += 1
                ins.then_inc(sem("dve_chain"), 1)
                dve.wait_ge(sem("dve_chain"), count[0])

            def ada_products(buf, u, done, steps):
                dve.wait_ge(sem("ada_summed"), done + GRANT)
                src = ada_bias[:, u, :]
                for k in range(KD):
                    ins = dve.scalar_tensor_tensor(out=ada_acc[:, u, :], in0=buf[:, k, :], scalar=cond[:, KD + k:KD + k + 1],
                                                   in1=src, op0=ALU.mult, op1=ALU.add)
                    src = ada_acc[:, u, :]
                    if k < KD - 1:
                        ins.then_inc(sem("ada_chain"), 1)
                        dve.wait_ge(sem("ada_chain"), steps * (KD - 1) + (k + 1))
                return ins

            def ada_block(which, buf, u, nth, b, summed):
                dve.wait_ge(sem(f"ada_loaded_{which}"), nth * 32 + 32)
                ada_products(buf, u, summed, b).then_inc(sem("ada_acc"), 1)
                dve.wait_ge(sem("ada_acc"), b + 1)
                dve.sem_inc(sem(f"ada_read_{which}"), 1)

            def norm(n, produce=None):
                scale = SC_F if n % 2 else SC_M
                dve.wait_ge(sem("norm_gain"), 16 * (n + 1))
                if n != 3:
                    dve.wait_ge(sem("ada_mods"), (ADA_FIRST, ADA_BLOCKS, 2 * ADA_BLOCKS)[n] + GRANT)
                link(dve.scalar_tensor_tensor(out=mods[:, scale:scale + D], in0=mods[:, scale:scale + D], scalar=1.0,
                                              in1=gain_tile[n], op0=ALU.add, op1=ALU.mult))
                for t in range(NT + TAKE_LAG):
                    if produce and t < NT:
                        produce(t)
                    if 1 <= t <= NT:
                        v = t - 1
                        dve.wait_ge(sem("norm_std"), NT * n + v + 1)
                        link(dve.reciprocal(rstd[:, v:v + 1], rstd[:, v:v + 1]))
                        dve.scalar_tensor_tensor(out=hnt[:, v, :], in0=xs[:, v, :], scalar=rstd[:, v:v + 1],
                                                 in1=mods[:, scale:scale + D], op0=ALU.mult, op1=ALU.mult)\
                           .then_inc(sem("hn_scaled"), 1)
                    if t >= TAKE_LAG:
                        norm_take(n, t - TAKE_LAG)

            def norm_take(n, t):
                dve.wait_ge(sem("hT_tr"), 2 * (NT * n + t) + 2)
                dve.tensor_copy(hTk[:, 4:8, t * P:(t + 1) * P], ps[:, (t % 2) * 2 + 1, :].rearrange("p (k s) -> p k s", k=4))\
                   .then_inc(sem("hT_d"), 1)

            def rope(heads, cos, sin, tmp):
                x1, x2 = heads[:, :, 0:HALF], heads[:, :, HALF:ROT]
                rows, n = heads.shape[0], heads.shape[1]
                shape = [rows, n, HALF]
                cos = cos.rearrange("p (o e) -> p o e", o=1).to_broadcast(shape)
                sin = sin.rearrange("p (o e) -> p o e", o=1).to_broadcast(shape)
                a, b, d = tmp
                dve.tensor_tensor(a, x1, cos, ALU.mult)
                dve.tensor_tensor(b, x2, sin, ALU.mult)
                link(dve.tensor_tensor(d, x1, sin, ALU.mult))
                link(dve.tensor_tensor(x1, a, b, ALU.subtract))
                link(dve.tensor_tensor(a, x2, cos, ALU.mult))
                return dve.tensor_tensor(x2, a, d, ALU.add)

            def nsa_norm(t):
                u = t % 2
                heads = nrm[u].rearrange("p (h e) -> p h e", e=DH)
                dve.wait_ge(sem("proj0_taken"), 4 * t + 4)
                if t:
                    dve.wait_ge(sem("nrm_ready"), t)
                for lo in range(0, 20, 8):
                    n = min(8, 20 - lo)
                    sq = area[:, A_SMALL:A_SMALL + n * DH]
                    link(dve.tensor_tensor(sq, nrm[u][:, lo * DH:(lo + n) * DH], nrm[u][:, lo * DH:(lo + n) * DH], ALU.mult))
                    link(dve.tensor_reduce(head_rstd(u)[:, lo:lo + n], sq.rearrange("p (h e) -> p h e", e=DH), AX, ALU.add))
                dve.tensor_scalar(head_rstd(u), head_rstd(u), 1.0 / DH, EPS, ALU.mult, ALU.add).then_inc(sem("head_var"), 1)
                dve.wait_ge(sem("head_std"), t + 1)
                link(dve.reciprocal(head_rstd(u), head_rstd(u)))
                link(dve.tensor_tensor(heads, heads, head_rstd(u).rearrange("p (h o) -> p h o", o=1).to_broadcast([P, 20, DH]),
                                       ALU.mult))
                for g, (lo, hi) in enumerate(((0, 16), (16, 18), (18, 20))):
                    gain = hgain[:, g * DH:(g + 1) * DH].rearrange("p (o e) -> p o e", o=1).to_broadcast([P, hi - lo, DH])
                    ins = dve.tensor_tensor(heads[:, lo:hi, :], heads[:, lo:hi, :], gain, ALU.mult)
                link(ins)
                at = C_ROPE + t * ROT
                rope(heads, cs[:, at:at + HALF], cs[:, at + HALF:at + ROT],
                     [r.rearrange("p (h e) -> p h e", e=HALF) for r in rope_tmp]).then_inc(sem("nrm_ready"), 1)

            def nsa_take_T(t):
                cols = slice(t * P, (t + 1) * P)
                dve.wait_ge(sem("nsa_tr"), t + 1)
                dve.tensor_copy(qT[:, 4:8, cols], ps[:, 5, :].rearrange("p (r s) -> p r s", r=4))
                src = ps[:, 6, 0:256].rearrange("p (b s) -> p b s", b=2)
                for g in range(2):
                    for r in range(2):
                        ins = dve.tensor_copy(ktz[64 * r:64 * r + 64, :, g, r, cols], src[64 * g:64 * g + 64, :, :])
                ins.then_inc(sem("qT_d"), 1)

            def cmp_blocks():
                dve.wait_ge(sem("kcv_taken"), NT)
                dve.wait_ge(sem("nsa_tr"), 3)
                for a in range(2):
                    for g in range(2):
                        for hi in range(2):
                            lo = 1 + 16 * hi
                            src = kcvT[:, a, g, lo:lo + SEQ].rearrange("p (c m two) -> p m c two", m=8, two=2)[:, :, :, 0]
                            ins = dve.tensor_tensor(blk[:, a, 8 * hi:8 * hi + 8, g * NC:(g + 1) * NC], src,
                                                    pe_t[:, a, 8 * hi:8 * hi + 8].rearrange("p (m o) -> p m o", o=1)
                                                    .to_broadcast([P, 8, NC]), ALU.add)
                    ins.then_inc(sem("cmp_dve"), 1)

            def compress():
                k0 = kcn[:, 0:DH]
                dve.wait_ge(sem("cmp_pe"), CMP_OUT)
                link(dve.tensor_copy(k0, ps[0:64, 3, 0:DH]))
                link(dve.tensor_tensor(ksq, k0, k0, ALU.mult))
                link(dve.tensor_reduce(head_ss[0:64, 0:1], ksq, AX, ALU.add))
                dve.tensor_scalar(head_ss[0:64, 1:2], head_ss[0:64, 0:1], 1.0 / DH, EPS, ALU.mult, ALU.add).then_inc(sem("cmp_dve"), 1)
                dve.wait_ge(sem("cmp_act"), KEY_STD)
                link(dve.reciprocal(head_ss[0:64, 2:3], head_ss[0:64, 1:2]))
                link(dve.scalar_tensor_tensor(out=k0, in0=k0, scalar=head_ss[0:64, 2:3], in1=hgain[0:64, 3 * DH:4 * DH],
                                              op0=ALU.mult, op1=ALU.mult))
                link(rope(k0.rearrange("p (h e) -> p h e", h=1), cs[0:64, C_CROPE:C_CROPE + HALF],
                          cs[0:64, C_CROPE + HALF:C_CROPE + ROT],
                          [r[0:64, 0:HALF].rearrange("p (h e) -> p h e", e=HALF) for r in rope_tmp]))
                dve.tensor_copy(kcn[:, DH:2 * DH], k0).then_inc(sem("cmp_dve"), 1)
                dve.wait_ge(sem("cmp_pe"), KEY_T)
                dve.tensor_copy(kctz[0:64, 0, :], ps[0:64, 0, 0:64])
                dve.tensor_copy(kctz[64:128, 1, :], ps[64:128, 0, 0:64]).then_inc(sem("cmp_dve"), 1)

            def over_slots(v):
                return v.rearrange("p (h o) -> p h o", o=1).to_broadcast([P, HEADS, NC])

            def cmp_shift(t):
                heads = pc[:, t, :].rearrange("p (h c) -> p h c", c=NC)
                mask = cs[:, C_CMASK + t * NC:C_CMASK + (t + 1) * NC].rearrange("p (o c) -> p o c", o=1)\
                    .to_broadcast([P, HEADS, NC])
                dve.wait_ge(sem("cmp_s"), t + 1)
                if t >= 2:
                    dve.wait_ge(sem("pc_ready"), t - 1)
                dve.scalar_tensor_tensor(out=heads, in0=ps[:, 1 + t % 2, :].rearrange("p (h c) -> p h c", c=NC), scalar=SCALE,
                                         in1=mask, op0=ALU.mult, op1=ALU.add).then_inc(sem("cmp_s_read"), 1)
                dve.wait_ge(sem("cmp_s_read"), t + 1)
                link(dve.tensor_reduce(cmp_r(t), heads, AX, ALU.max))
                dve.tensor_tensor(heads, heads, over_slots(cmp_r(t)), ALU.subtract).then_inc(sem("pc_shifted"), 1)

            def cmp_factor(t):
                heads, r = pc[:, t, :].rearrange("p (h c) -> p h c", c=NC), cmp_r(t)
                dve.wait_ge(sem("pc_exp"), t + 1)
                link(dve.tensor_reduce(r, heads, AX, ALU.add))
                link(dve.reciprocal(r, r))
                dve.scalar_tensor_tensor(out=r, in0=r, scalar=cs[:, C_ROWOK + t:C_ROWOK + t + 1],
                                         in1=gates[:, t * 48:t * 48 + HEADS], op0=ALU.mult, op1=ALU.mult).then_inc(sem("pc_factor"), 1)

            units = [(t, h) for t in range(NT) for h in range(HEADS)]

            def attend():
                causal = cs[:, C_CAUSAL:C_CAUSAL + P].rearrange("p (o s) -> p o s", o=1).to_broadcast([P, 2, P])
                for n in range(len(units) + 1):
                    if n < len(units):
                        t, h = units[n]
                        u = n % 2
                        s = ps[:, 2 * u:2 * u + 2, :]
                        dve.wait_ge(sem("scores"), n + 1)
                        link(dve.tensor_tensor(s[:, :, t * P:(t + 1) * P], s[:, :, t * P:(t + 1) * P], causal, ALU.add))
                        link(dve.tensor_reduce(raw_max(u), s[:, :, 0:(t + 1) * P], AX, ALU.max))
                        dve.tensor_scalar(neg_max(u), raw_max(u), -SCALE, None, ALU.mult).then_inc(sem("neg_max"), 1)
                    if n:
                        m = n - 1
                        t, h = units[m]
                        gate = gates[:, t * 48 + 16:t * 48 + 48].rearrange("p (b h) -> p b h", b=2)[:, :, h]
                        dve.wait_ge(sem("exp_done"), m + 1)
                        link(dve.reciprocal(inv_l(m % 2), sum_l(m % 2)))
                        for b in range(2):
                            p_b = prob[m % 4][:, b, 0:(t + 1) * P]
                            ins = dve.tensor_scalar(p_b, p_b, inv_l(m % 2)[:, b:b + 1], gate[:, b:b + 1], ALU.mult, ALU.mult)
                        ins.then_inc(sem("prob_ready"), 1)

            def residual(l, t):
                for half in range(2):
                    y = ps[:, 2 * (t % 2) + half, :]
                    cols = slice(half * 512, (half + 1) * 512)
                    dve.wait_ge(sem("y_ready"), 2 * (NT * l + t) + half + 1)
                    link(dve.tensor_tensor(y, y, mods[:, G_M + half * 512:G_M + (half + 1) * 512], ALU.mult))
                    dve.tensor_tensor(xs[:, t, cols], xs[:, t, cols], y, ALU.add).then_inc(sem("y_taken"), 1)
                    dve.wait_ge(sem("y_taken"), 2 * (NT * l + t) + half + 1)
                dve.sem_inc(sem(f"x_ready_{2 * l + 1}"), 1)
                dve.sem_inc(sem("w_out_used"), 1)

            def combine(l, t):
                x = xs[:, t, :]
                dve.wait_ge(sem(f"z_in_{t}"), 32 * (l + 1))
                link(dve.scalar_tensor_tensor(out=x, in0=z_in[t][0], scalar=moe_w(0)[:, t:t + 1], in1=x, op0=ALU.mult, op1=ALU.add))
                dve.scalar_tensor_tensor(out=x, in0=z_in[t][1], scalar=moe_w(1)[:, t:t + 1], in1=x, op0=ALU.mult, op1=ALU.add)\
                   .then_inc(sem(f"x_ready_{2 * l + 2}"), 1)

            def routing(l):
                def a(lo, n=P):
                    return arena[:, lo:lo + n]

                def t_e(v):
                    return v.rearrange("p (t e) -> p t e", t=NT)

                def tg_e(v):
                    return v.rearrange("p (q e) -> p q e", e=EPG)
                AFF, CH, EQ, MSK, E1, E2, SUM, BLK, SLT, F, TMP = (a(r) for r in (R_AFF, R_CH, R_EQ, R_MSK, R_E1, R_E2, R_SUM,
                                                                                 R_BLK, R_SLOT, R_F, R_TMP))
                M1, M2, FI, GS, GO = (a(R_S + 16 * i, 16) for i in range(5))
                OV, CUM, EXC = (a(R_S + 96 + 32 * i, 32) for i in range(3))
                QUAD = [a(R_S + 192 + 4 * i, 4) for i in range(4)]
                AT_BLOCK, AT_SLOT = (a(R_S + 208 + 8 * i, 8) for i in range(2))
                OVX = a(R_S + 256, 8)
                CNT = a(R_S + 264, 32)
                OVC = a(R_S + 296, 8 * EXPERTS)

                def bc(v, shape):
                    return v.rearrange("p (q o) -> p q o", o=1).to_broadcast(shape)

                def row(lo, n, times):
                    return cs[:, lo:lo + n].rearrange("p (o e) -> p o e", o=1).to_broadcast([P, times, n])

                def first_of(values, best, hot, groups, per, iota):
                    v, h3 = (w.rearrange("p (q e) -> p q e", e=per) for w in (values, hot))
                    fi = FI[:, 0:groups]
                    link(dve.tensor_tensor(h3, v, bc(best, [P, groups, per]), ALU.is_equal))
                    link(dve.tensor_tensor(h3, h3, row(iota, per, groups), ALU.mult))
                    link(dve.tensor_reduce(fi, h3, AX, ALU.min))
                    link(dve.tensor_tensor(h3, row(iota, per, groups), bc(fi, [P, groups, per]), ALU.is_equal))

                dve.wait_ge(sem("affinity"), l + 1)
                dve.wait_ge(sem("router_w"), 48 * (l + 1))
                link(dve.tensor_tensor(t_e(CH), t_e(AFF), a(R_B, EXPERTS).rearrange("p (o e) -> p o e", o=1)
                                       .to_broadcast([P, NT, EXPERTS]), ALU.add))
                link(dve.tensor_reduce(M1, tg_e(CH), AX, ALU.max))
                first_of(CH, M1, E1, NT * EGROUPS, EPG, C_IOTA_8)
                link(dve.scalar_tensor_tensor(out=MSK, in0=E1, scalar=NEG, in1=CH, op0=ALU.mult, op1=ALU.add))
                link(dve.tensor_reduce(M2, tg_e(MSK), AX, ALU.max))
                first_of(MSK, M2, E2, NT * EGROUPS, EPG, C_IOTA_8)
                link(dve.tensor_tensor(GS, M1, M2, ALU.add))
                link(dve.tensor_reduce(QUAD[0], GS.rearrange("p (t g) -> p t g", t=NT), AX, ALU.max))
                first_of(GS, QUAD[0], GO, NT, EGROUPS, C_IOTA_4)
                for e in (E1, E2):
                    link(dve.tensor_tensor(tg_e(e), tg_e(e), bc(GO, [P, NT * EGROUPS, EPG]), ALU.mult))
                link(dve.memset(BLK[:, 0:EXPERTS], 0.0))
                dve.tensor_tensor(SUM, E1, E2, ALU.add).then_inc(sem("route_dve"), 1)
                for k, e in enumerate((E1, E2)):
                    link(dve.tensor_tensor(TMP, AFF, e, ALU.mult))
                    link(dve.tensor_reduce(QUAD[1 + k], t_e(TMP), AX, ALU.add))
                link(dve.tensor_tensor(QUAD[3], QUAD[1], QUAD[2], ALU.add))
                link(dve.reciprocal(QUAD[3], QUAD[3]))
                dve.tensor_tensor(moe_w(0), QUAD[1], QUAD[3], ALU.mult)
                link(dve.tensor_tensor(moe_w(1), QUAD[2], QUAD[3], ALU.mult))
                dve.wait_ge(sem("route_pe"), 3 * l + RANKS)
                dve.tensor_copy(CNT, ps[:, 6, 2 * P:2 * P + EXPERTS])
                link(dve.tensor_copy(TMP, ps[:, 6, P:2 * P]))
                for dst, src in ((F, TMP), (OV, CNT)):
                    bound = SLOTS if dst is F else SLOTS + 1
                    link(dve.tensor_scalar(dst, src, float(bound), None, ALU.is_ge))
                    for m in range(1, SEQ // SLOTS - 1):
                        link(dve.scalar_tensor_tensor(out=dst, in0=src, scalar=float(bound + m * SLOTS), in1=dst,
                                                      op0=ALU.is_ge, op1=ALU.add))
                link(dve.scalar_tensor_tensor(out=SLT, in0=F, scalar=-float(SLOTS), in1=TMP, op0=ALU.mult, op1=ALU.add))
                link(dve.tensor_tensor_scan(CUM, OV, cs[:, C_ZERO:C_ZERO + EXPERTS], 0.0, ALU.add, ALU.add))
                link(dve.tensor_tensor(EXC, CUM, OV, ALU.subtract))
                iota_e = cs[:, C_IOTA_E:C_IOTA_E + EXPERTS]
                link(dve.tensor_tensor(EXC, EXC, iota_e, ALU.subtract))
                link(dve.scalar_tensor_tensor(out=t_e(TMP), in0=t_e(F), scalar=float(EXPERTS - 1),
                                              in1=EXC.rearrange("p (o e) -> p o e", o=1).to_broadcast([P, NT, EXPERTS]),
                                              op0=ALU.add, op1=ALU.add))
                link(dve.scalar_tensor_tensor(out=BLK, in0=F, scalar=0.0, in1=TMP, op0=ALU.is_gt, op1=ALU.mult))
                link(dve.tensor_tensor(t_e(BLK), t_e(BLK), row(C_IOTA_E, EXPERTS, NT), ALU.add))
                for k, e in enumerate((E1, E2)):
                    for dst, src in ((AT_BLOCK, BLK), (AT_SLOT, SLT)):
                        link(dve.tensor_tensor(TMP, src, e, ALU.mult))
                        link(dve.tensor_reduce(dst[:, k * NT:(k + 1) * NT], t_e(TMP), AX, ALU.add))
                hot, at_block, vals2 = (v.rearrange("p (i s) -> p i s", i=n_hot) for v in (slot_hot, block_hot, block_val))
                index = a(R_SLOTS, SLOTS).rearrange("p (o s) -> p o s", o=1)
                dve.tensor_tensor(hot, index.to_broadcast([P, n_hot, SLOTS]), bc(AT_SLOT, [P, n_hot, SLOTS]), ALU.is_equal)
                link(dve.tensor_tensor(at_block, index[:, :, 0:NB].to_broadcast([P, n_hot, NB]), bc(AT_BLOCK, [P, n_hot, NB]),
                                       ALU.is_equal))
                token = bc(cs[:, C_TOKEN:C_TOKEN + NT], [P, NT, NB])
                first, second = slice(0, NT), slice(NT, 2 * NT)
                dve.tensor_tensor(vals2[:, second, 0:NB], at_block[:, second, :], token, ALU.mult)
                dve.tensor_tensor(vals2[:, second, NB:2 * NB], at_block[:, second, :], token, ALU.mult)
                link(dve.tensor_tensor(vals2[:, first, 0:NB], at_block[:, first, :], token, ALU.mult))
                dve.scalar_tensor_tensor(out=vals2[:, first, NB:2 * NB], in0=at_block[:, first, :], scalar=-float(SEQ),
                                         in1=vals2[:, first, 0:NB], op0=ALU.mult, op1=ALU.add).then_inc(sem("route_dve"), 1)
                dve.wait_ge(sem("route_pe"), 3 * l + SLOTS_SUMMED)
                dve.tensor_scalar(EQ[:, 0:NB], ps[:, 6, 384:384 + NB], float(NOBODY), None, ALU.add)
                link(dve.tensor_scalar(EQ[:, NB:2 * NB], ps[:, 6, 384 + NB:384 + 2 * NB], float(2 * SEQ), None, ALU.add))
                dve.tensor_copy(slot_row[:, :], EQ[:, NB:2 * NB])
                dve.tensor_copy(slot_tok[:, :], EQ[:, 0:NB]).then_inc(sem("route_dve"), 1)
                ovc = OVC.rearrange("p (j e) -> p j e", e=EXPERTS)
                link(dve.tensor_tensor(ovc, CUM.rearrange("p (o e) -> p o e", o=1).to_broadcast([P, 8, EXPERTS]),
                                       bc(cs[:, C_IOTA_OV:C_IOTA_OV + 8], [P, 8, EXPERTS]), ALU.is_le))
                link(dve.tensor_reduce(OVX, ovc, AX, ALU.add))
                link(dve.tensor_scalar(OVX, OVX, float(EXPERTS - 1), None, ALU.min))
                dve.tensor_copy(route[:, 1:8], OVX[:, 0:7])
                dve.tensor_copy(route[:, 0:1], CUM[:, EXPERTS - 1:EXPERTS]).then_inc(sem("route_dve"), 1)

            def moe(l):
                def take_x(b):
                    dve.wait_ge(sem(f"xb_used_{l}"), b + 1)
                    dve.wait_ge(sem(f"gu_{l}"), b * 2)
                    dve.tensor_copy(xbT[:, 4:8, :], ps[:, 3, :].rearrange("p (k s) -> p k s", k=4)).then_inc(sem(f"xbT_d_{l}"), 1)

                def hidden(b):
                    dve.wait_ge(sem(f"sig_{l}"), b + 1)
                    dve.wait_ge(sem(f"hid_tr_{l}"), b)
                    dve.tensor_tensor(hid, sig, ps[:, 0, :], ALU.mult).then_inc(sem(f"silu_{l}"), 1)
                    dve.wait_ge(sem(f"silu_{l}"), b + 1)
                    dve.wait_ge(sem(f"gu_{l}"), b * 2 + 2)
                    dve.tensor_tensor(hid, hid, ps[:, 1, :], ALU.mult).then_inc(sem(f"hid_{l}"), 1)

                def take_y(b, u, nth):
                    dve.wait_ge(sem(f"y_{l}"), b + 1)
                    if nth is not None:
                        dve.wait_ge(sem(f"z_stored_{l}_{u}"), nth * 16)
                    dve.tensor_tensor(zb[u].rearrange("p (a n) -> p a n", a=2), ps[:, 4:6, :],
                                      ffn_gate.rearrange("p (a n) -> p a n", a=2), ALU.mult).then_inc(sem(f"zb_{l}"), 1)

                def pair(i, nth):
                    for u in range(2):
                        hidden(i * 2 + 1 + u)
                        take_x(i * 2 + 2 + u)
                        if l == 0 and u == 0:
                            ada_block("next", ada_buf, 0, i, i + ADA_BLOCKS, i + ADA_BLOCKS)
                        take_y(i * 2 + u, u, nth)
                dve.sem_inc(sem(f"zb_{l}"), GRANT)
                dve.wait_ge(sem("ffn_gate"), l + 1)
                take_x(0)
                hidden(0)
                take_x(1)
                pair(0, None)
                with dve.Fori(1, EXPERTS // 2 - 1) as i:
                    pair(i, i)
                hidden(EXPERTS - 1)
                if l == 0:
                    ada_block("next", ada_buf, 0, ADA_BLOCKS - 1, 2 * ADA_BLOCKS - 1, 2 * ADA_BLOCKS - 1)
                take_y(EXPERTS - 2, 0, EXPERTS // 2 - 1)
                take_y(EXPERTS - 1, 1, EXPERTS // 2 - 1)
                dve.wait_ge(sem("route_dve"), 4 * l + ROUTED)
                n_ov = dve.value_load(route[0:1, 0:1], min_val=0, max_val=OVERFLOW)
                with dve.If(n_ov > 0), dve.Fori(0, n_ov) as j:
                    dve.wait_ge(sem(f"z_stored_{l}_0"), 16 * (EXPERTS // 2))
                    take_x(j + EXPERTS)
                    hidden(j + EXPERTS)
                    take_y(j + EXPERTS, 0, None)

            def mlstm_gates():
                dve.wait_ge(sem("ml_gate_pe"), 1)
                dve.tensor_tensor(ml_li, ps[:, 4, 0:8 * NT].rearrange("p (t g) -> p t g", t=NT),
                                  gates[:, 96:104].rearrange("p (o g) -> p o g", o=1).to_broadcast([P, NT, 8]), ALU.add)\
                   .then_inc(sem("ml_gate_dve"), 1)
                dve.wait_ge(sem("ml_gate_act"), 1)
                dve.tensor_scalar(ml_li[:, :, 0:MH], ml_li[:, :, 0:MH], SOFTCAP, None, ALU.mult)
                dve.tensor_scalar(ml_li[:, :, MH:2 * MH], ml_li[:, :, MH:2 * MH], -1.0, None, ALU.mult).then_inc(sem("ml_gate_dve"), 1)

            def mlstm_rows():
                dve.wait_ge(sem("proj1_ready"), 16)
                dve.wait_ge(sem("ml_gate_pe"), 2)

                def r(i):
                    return ml_row(i)[0:MH, :]
                link(dve.memset(r(ZERO), 0.0))
                link(dve.tensor_copy(r(LF), ps[0:MH, 5, :]))
                link(dve.tensor_tensor_scan(r(CUM_B), r(LF), r(ZERO), 0.0, ALU.add, ALU.add))
                link(dve.tensor_tensor(r(U_IN), ps[0:MH, 6, :], r(CUM_B), ALU.subtract))
                link(dve.tensor_tensor_scan(r(U_MAX), r(U_IN), r(U_IN), 0.0, ALU.max, ALU.max))
                dve.tensor_copy(ml_sel, ident[0:MH, 0:MH].rearrange("p (h o) -> p h o", o=1).to_broadcast([MH, MH, P]))
                dve.tensor_tensor(r(EXP_M), r(CUM_B), r(U_MAX), ALU.add).then_inc(sem("ml_gate_dve"), 1)

            def mlstm():
                later = cs[:, C_CAUSAL_T:C_CAUSAL_T + P].rearrange("p (o s) -> p o s", o=1).to_broadcast([P, NT, P])

                def diagonal(h):
                    dve.wait_ge(sem("ml_u"), h + 1)
                    if h:
                        dve.wait_ge(sem("ml_w"), NT * h)
                    dve.tensor_tensor(ml_diag.rearrange("p (t s) -> p t s", t=NT),
                                      ps[:, 6 + h % 2, :].rearrange("p (t s) -> p t s", t=NT), later, ALU.add)\
                       .then_inc(sem("ml_diag"), 1)

                def weights(h, j):
                    n = NT * h + j
                    dve.wait_ge(sem("ml_s"), n + 1)
                    dve.wait_ge(sem("ml_w"), n + 1)
                    if n >= 2:
                        dve.wait_ge(sem("ml_num"), n - 1)
                    cols = slice(0, (NT - j) * P)
                    dve.scalar_tensor_tensor(out=ml_at(n % 2)[:, cols], in0=ps[:, 4 + n % 2, cols], scalar=DQK ** -0.5,
                                             in1=ml_w(n % 2)[:, cols], op0=ALU.mult, op1=ALU.mult).then_inc(sem("ml_at"), 1)

                def gate_numerators(h, t):
                    dve.wait_ge(sem("ml_sums"), NT * h + t + 1)
                    o = hnt[:, t, h * DV:(h + 1) * DV]
                    dve.tensor_tensor(o, o, ps[:, t, 0:DV], ALU.mult).then_inc(sem("ml_out"), 1)

                dve.wait_ge(sem("ml_o_gained"), NT)
                diagonal(0)
                for h in range(MH):
                    for j in range(NT):
                        weights(h, j)
                        if j >= 2:
                            gate_numerators(h, j - 2)
                    if h + 1 < MH:
                        diagonal(h + 1)
                    gate_numerators(h, NT - 2)
                    gate_numerators(h, NT - 1)
                dve.wait_ge(sem("ml_out"), NT * MH)
                link(dve.scalar_tensor_tensor(out=ml_den, in0=ml_den, scalar=-1.0, in1=ml_den, op0=ALU.mult, op1=ALU.max))
                link(dve.tensor_tensor(ml_den, ml_den, ml_cols[:, 1, :], ALU.max))
                link(dve.reciprocal(ml_den, ml_den))
                link(dve.tensor_tensor(ml_scale, ml_ssq, ml_den, ALU.mult))
                link(dve.tensor_tensor(ml_scale, ml_scale, ml_den, ALU.mult))
                dve.tensor_scalar(ml_scale, ml_scale, 1.0 / DV, EPS, ALU.mult, ALU.add).then_inc(sem("ml_hvar"), 1)
                dve.wait_ge(sem("ml_hstd"), 1)
                link(dve.reciprocal(ml_scale, ml_scale))
                link(dve.tensor_tensor(ml_scale, ml_scale, ml_den, ALU.mult))
                for t in range(NT):
                    o = hnt[:, t, :].rearrange("p (h d) -> p h d", h=MH)
                    factor = ml_scale[:, t * MH:(t + 1) * MH].rearrange("p (h o) -> p h o", o=1).to_broadcast([P, MH, DV])
                    dve.tensor_tensor(o, o, factor, ALU.mult).then_inc(sem("ml_tile"), 1)
                for t in range(NT):
                    dve.wait_ge(sem("mo_tr"), 2 * t + 2)
                    dve.tensor_copy(hTk[:, 4:8, t * P:(t + 1) * P], ps[:, 5 + 2 * (t % 2), :].rearrange("p (k s) -> p k s", k=4))\
                       .then_inc(sem("mo_d"), 1)

            arena_buf = arena[:, 0:KD * ADA_W].rearrange("p (k n) -> p k n", k=KD)

            def ada_pairs(first, n):
                with dve.Fori(first // 2, (first + n) // 2) as i:
                    ada_block("a", ada_buf, 0, i, i * 2, i * 2)
                    ada_block("b", arena_buf, 1, i, i * 2 + 1, i * 2)
            for which in ("a", "b", "next"):
                dve.sem_inc(sem(f"ada_read_{which}"), GRANT)
            dve.wait_ge(sem("cond_sig"), 1)
            link(dve.tensor_tensor(cond[:, KD:2 * KD], cond[:, KD:2 * KD], cond[:, 0:KD], ALU.mult))
            dve.wait_ge(sem("filled"), BIAS_ZEROED)
            ada_pairs(0, ADA_FIRST)
            dve.wait_ge(sem("consts"), 16)
            norm(0)
            ada_pairs(ADA_FIRST, ADA_BLOCKS - ADA_FIRST)
            dve.wait_ge(sem("nsa_small"), 16 * 10)
            dve.wait_ge(sem("filled"), NSA_ZEROED)
            nsa_norm(0)
            nsa_norm(1)
            nsa_take_T(0)
            nsa_norm(2)
            nsa_take_T(1)
            cmp_blocks()
            nsa_take_T(2)
            nsa_norm(3)
            nsa_take_T(3)
            compress()
            for t in range(NT + 1):
                if t < NT:
                    cmp_shift(t)
                if t:
                    cmp_factor(t - 1)
            attend()
            norm(1, lambda t: residual(0, t))
            routing(0)
            moe(0)

            norm(2, lambda t: combine(0, t))
            mlstm_gates()
            mlstm_rows()
            mlstm()
            norm(3, lambda t: residual(1, t))
            routing(1)
            moe(1)
            for t in range(NT):
                combine(1, t)


def constants():
    import numpy as np
    cs = np.zeros((P, C_COLS), np.float32)
    p = np.arange(P)
    cs[:, C_ID:C_ID + P] = np.eye(P)
    cs[:, C_TRI:C_TRI + P] = p[:, None] < p[None, :]
    cs[:, C_CAUSAL:C_CAUSAL + P] = np.where(p[None, :] <= p[:, None], 0.0, NEG)
    cs[:, C_CAUSAL_T:C_CAUSAL_T + P] = np.where(p[None, :] < p[:, None], -NEG, 0.0)
    slot = np.arange(NC)
    slot_end = slot * CMP_STRIDE + CMP_BLOCK - 1
    inv_freq = np.float32(500000.0) ** (-np.arange(HALF, dtype=np.float32) / np.float32(HALF))

    def angles(pos):
        a = (pos.astype(np.float32)[:, None] * inv_freq[None, :]).astype(np.float32)
        return np.concatenate([np.cos(a), np.sin(a)], 1)
    for t in range(NT):
        token = t * P + p
        cs[:, C_CMASK + t * NC:C_CMASK + (t + 1) * NC] = np.where((slot_end[None, :] <= token[:, None]) & (slot < NCMP), 0.0, NEG)
        cs[:, C_ROPE + t * ROT:C_ROPE + (t + 1) * ROT] = angles(token)
        cs[:, C_ROWOK + t] = token >= CMP_BLOCK - 1
        cs[:, C_TOKEN + t] = token - NOBODY
    cs[0:2 * NC, C_CROPE:C_CROPE + ROT] = angles(np.tile(slot_end, 2))
    cs[:, C_IOTA_E:C_IOTA_E + EXPERTS] = np.arange(EXPERTS)
    cs[:, C_IOTA_8:C_IOTA_8 + EXPERTS] = np.arange(EXPERTS) % EPG - EPG
    cs[:, C_IOTA_4:C_IOTA_4 + EGROUPS] = np.arange(EGROUPS) - EGROUPS
    cs[:, C_IOTA_OV:C_IOTA_OV + 8] = np.arange(8)
    return cs, np.arange(SLOTS, dtype=np.float32)[None, :]


_INS = ["x", "c", "ada_w", "ada_b", "norm_mix_gain", "norm_ffn_gain",
        "nsa_w_in", "nsa_w_out", "nsa_q_gain", "nsa_k_gain", "nsa_cmp_pe", "nsa_cmp_w1", "nsa_cmp_b1", "nsa_cmp_w2",
        "nsa_cmp_b2", "mlstm_w_in", "mlstm_b_igate", "mlstm_b_fgate", "mlstm_norm_gain", "mlstm_w_out",
        "router_w", "router_b", "moe_w_gate", "moe_w_up", "moe_w_down"]


def kernel(**inputs):
    import numpy as np
    import concourse.bacc as bacc
    from concourse.bass_utils import run_bass_kernel_spmd

    nc = bacc.Bacc("TRN2", target_bir_lowering=False, num_devices=1)
    host = {f"in_{name}": np.ascontiguousarray(inputs[name]) for name in _INS}
    host["in_consts"], host["in_slot_index"] = constants()
    args = [nc.dram_tensor(name, a.shape, mybir.dt.from_np(a.dtype), kind="ExternalInput").ap() for name, a in host.items()]
    result = nc.dram_tensor("out_0", (1, SEQ, D), F32, kind="ExternalOutput").ap()
    build_trunk(nc, *args, result)
    run = run_bass_kernel_spmd(nc, [host], core_ids=[0])
    return run.results[0]["out_0"]
```
